# Optimizing a Trainium2 kernel written in Bass

```python
import jax, jax.numpy as jnp
from jax import lax
import numpy as np

D_MODEL = 2048
BATCH = 1
SEQ = 256
DEPTH = 1
DEC_BATCH = 8
DEC_SEQ = 8
PAST_LEN = 2048
PAGE_SIZE = 128

E_A = D_MODEL // 2
HA = 4
DA = E_A // HA
CHUNK = 128
HB = 4
E_B = D_MODEL // 2
DV = E_B // HB
DK = DV // 2
K_B = HB * DK
GATE_RANK = 16
GATE_TAU = 16.0
GLA_CHUNK = 16
PLE_DIM = 256
EPS = 1e-6
SPLIT_SIZES = (E_A, E_A, E_A, K_B, K_B, E_B, E_B, GATE_RANK, D_MODEL, D_MODEL)
N_IN = sum(SPLIT_SIZES)

kernel_name = "hybrid_gmlp_gla_gated_merge_step"

def rms_norm(x, g):
    xf = x.astype(jnp.float32)
    y = xf * lax.rsqrt(jnp.mean(xf * xf, axis=-1, keepdims=True) + EPS)
    return (y * g.astype(jnp.float32)).astype(x.dtype)

def split_cols(t):
    outs, off = [], 0
    for s in SPLIT_SIZES:
        outs.append(t[..., off:off + s])
        off += s
    return outs

def chunk_spatial_gate(u, v, w_s, b_s):
    B, L, _ = v.shape
    n_c = -(-L // CHUNK)
    pad = n_c * CHUNK - L
    vp = jnp.pad(v, ((0, 0), (0, pad), (0, 0))).reshape(B, n_c, CHUNK, HA, DA)
    mask = jnp.tril(jnp.ones((CHUNK, CHUNK), dtype=bool))
    w = jnp.where(mask[None], w_s, jnp.zeros((), w_s.dtype))
    s = jnp.einsum('gts,bcsgd->bctgd', w, vp) + b_s.T[None, None, :, :, None]
    s = s.reshape(B, n_c * CHUNK, E_A)[:, :L]
    return u * s

def gla(q, k, v, log_a, s0):
    B, L = q.shape[:2]
    n_c = -(-L // GLA_CHUNK)
    pad = n_c * GLA_CHUNK - L

    def blocks(t):
        t = jnp.pad(t, ((0, 0), (0, pad), (0, 0), (0, 0)))
        return t.reshape(B, n_c, GLA_CHUNK, HB, t.shape[-1]).transpose(1, 0, 3, 2, 4)

    qc, kc, vc, ac = blocks(q), blocks(k), blocks(v), blocks(log_a)
    mask = jnp.tril(jnp.ones((GLA_CHUNK, GLA_CHUNK), dtype=bool))

    def step(S, inp):
        qb, kb, vb, ab = inp
        qb = qb.astype(jnp.float32)
        kb = kb.astype(jnp.float32)
        vb = vb.astype(jnp.float32)
        b = jnp.cumsum(ab.astype(jnp.float32), axis=-2)
        q_t = qb * jnp.exp(b)
        k_t = kb * jnp.exp(-b)
        att = jnp.where(mask, jnp.einsum('bhtd,bhsd->bhts', q_t, k_t), 0.0)
        o = jnp.einsum('bhts,bhsv->bhtv', att, vb) + jnp.einsum('bhtd,bhdv->bhtv', q_t, S)
        b_last = b[..., -1:, :]
        k_d = kb * jnp.exp(b_last - b)
        S = jnp.exp(b_last[..., 0, :])[..., None] * S + jnp.einsum('bhsd,bhsv->bhdv', k_d, vb)
        return S, o

    S, o = lax.scan(step, s0.astype(jnp.float32), (qc, kc, vc, ac))
    o = o.transpose(1, 0, 3, 2, 4).reshape(B, n_c * GLA_CHUNK, HB, DV)[:, :L]
    return o.astype(v.dtype), S.astype(s0.dtype)

def layer(x, p, s0, g_pre, w_in, g_v, w_s, b_s, w_a2, b_a, g_o, w_pa, w_pb, w_o, g_post, w_pg, w_pe):
    B, L, _ = x.shape
    xn = rms_norm(x, g_pre)
    u_a, v_a, z_a, q_b, k_b, v_b, z_b, a_lr, m_a, m_b = split_cols(xn @ w_in)
    v_a = rms_norm(v_a, g_v)
    y_a = chunk_spatial_gate(u_a, v_a, w_s, b_s) * jax.nn.silu(z_a)
    log_a = jax.nn.log_sigmoid((a_lr @ w_a2 + b_a).astype(jnp.float32)) / GATE_TAU
    q = q_b.reshape(B, L, HB, DK) * (DK ** -0.5)
    k = k_b.reshape(B, L, HB, DK)
    v = v_b.reshape(B, L, HB, DV)
    o, s_new = gla(q, k, v, log_a.reshape(B, L, HB, DK), s0)
    y_b = rms_norm(o, g_o).reshape(B, L, E_B) * jax.nn.silu(z_b)
    m = jax.nn.sigmoid(m_a) * (y_a @ w_pa) + jax.nn.sigmoid(m_b) * (y_b @ w_pb)
    h = x + rms_norm(m @ w_o, g_post)
    h = h + jax.nn.sigmoid(h @ w_pg) * (p @ w_pe)
    return h, s_new, v_a

def setup_inputs(seed: int = 0) -> dict:
    key = jax.random.key(seed)
    ks = jax.random.split(key, 20)
    f32 = jnp.float32
    nrm = lambda k, shape, scale: jax.random.normal(k, shape, f32) * scale
    return {
        "x_prompt": nrm(ks[0], (BATCH, SEQ, D_MODEL), 1.0),
        "x_sample": nrm(ks[1], (DEC_BATCH, DEC_SEQ, D_MODEL), 1.0),
        "p_prompt": nrm(ks[2], (DEPTH, BATCH, SEQ, PLE_DIM), 1.0),
        "p_sample": nrm(ks[3], (DEPTH, DEC_BATCH, DEC_SEQ, PLE_DIM), 1.0),
        "state_gla": nrm(ks[4], (DEPTH, DEC_BATCH, HB, DK, DV), 0.5),
        "g_pre": 1.0 + nrm(ks[5], (DEPTH, D_MODEL), 0.05),
        "w_in": nrm(ks[6], (DEPTH, D_MODEL, N_IN), D_MODEL ** -0.5),
        "g_v": 1.0 + nrm(ks[7], (DEPTH, E_A), 0.05),
        "w_s": nrm(ks[8], (DEPTH, HA, CHUNK, CHUNK), CHUNK ** -0.5),
        "b_s": 1.0 + nrm(ks[9], (DEPTH, HA, CHUNK), 0.1),
        "w_a2": nrm(ks[10], (DEPTH, GATE_RANK, K_B), GATE_RANK ** -0.5),
        "b_a": nrm(ks[11], (DEPTH, K_B), 0.1),
        "g_o": 1.0 + nrm(ks[12], (DEPTH, HB, DV), 0.05),
        "w_pa": nrm(ks[13], (DEPTH, E_A, D_MODEL), E_A ** -0.5),
        "w_pb": nrm(ks[14], (DEPTH, E_B, D_MODEL), E_B ** -0.5),
        "w_o": nrm(ks[15], (DEPTH, D_MODEL, D_MODEL), D_MODEL ** -0.5),
        "g_post": 1.0 + nrm(ks[16], (DEPTH, D_MODEL), 0.05),
        "w_pg": nrm(ks[17], (DEPTH, D_MODEL, D_MODEL), D_MODEL ** -0.5),
        "w_pe": nrm(ks[18], (DEPTH, PLE_DIM, D_MODEL), PLE_DIM ** -0.5),
    }

def reference(x_prompt, x_sample, p_prompt, p_sample, state_gla, g_pre, w_in, g_v, w_s, b_s,
              w_a2, b_a, g_o, w_pa, w_pb, w_o, g_post, w_pg, w_pe):
    hp, hs = x_prompt, x_sample
    sp_list, ss_list, cv_list = [], [], []
    for i in range(DEPTH):
        wts = (g_pre[i], w_in[i], g_v[i], w_s[i], b_s[i], w_a2[i], b_a[i], g_o[i],
               w_pa[i], w_pb[i], w_o[i], g_post[i], w_pg[i], w_pe[i])
        s0_prompt = jnp.zeros((hp.shape[0], HB, DK, DV), hp.dtype)
        hp, s_p, _ = layer(hp, p_prompt[i], s0_prompt, *wts)
        hs, s_s, v_s = layer(hs, p_sample[i], state_gla[i], *wts)
        sp_list.append(s_p)
        ss_list.append(s_s)
        cv_list.append(v_s)
    state_gla_prompt = jnp.stack(sp_list)
    state_gla_sample = jnp.stack(ss_list)
    chunk_v_sample = jnp.stack(cv_list)
    return (hp, hs, state_gla_prompt, state_gla_sample, chunk_v_sample)


_drawn_inputs = setup_inputs


def setup_inputs(seed=0):
    import zlib

    import numpy as np

    out = dict(_drawn_inputs(seed))
    spreads = {}
    factors = {}
    for name, (base, spread) in spreads.items():
        noise = np.random.default_rng([zlib.crc32(name.encode()), seed]).standard_normal(out[name].shape)
        drawn = base * np.exp(spread * noise) if base else spread * noise
        out[name] = __import__('jax').numpy.asarray(drawn.astype(out[name].dtype))
    for name, factor in factors.items():
        out[name] = (out[name] * factor).astype(out[name].dtype)
    return out
```

```python
from contextlib import ExitStack, contextmanager

import concourse.bass as bass
import numpy as np
from concourse import mybir

F32, F32R, I32 = mybir.dt.float32, mybir.dt.float32r, mybir.dt.int32
ACT = mybir.ActivationFunctionType
ALU = mybir.AluOpType

P = 128
D = 2048
SEQ, CHUNK = 256, 128
DEC_B, DEC_L = 8, 8
DEC = DEC_B * DEC_L
T = SEQ + DEC
EA = EB = D // 2
HA, HB = 4, 4
DV, DK = EB // HB, EB // HB // 2
RANK, TAU, EPS = 16, 16.0, 1e-6
PLE = 256
KX = D // P
KE = EA // P
UK = 8
BLK = 32
NBLK = SEQ // BLK
MID = BLK // 2 - 1

S_K = 0
S_Q = S_K + HB
S_V = S_Q + HB
S_ZB = S_V + KE
S_VA = S_ZB + KE
S_ZA = S_VA + KE
S_U = S_ZA + KE
S_GATE = S_U + KE
S_WO = S_GATE + 3 * KX
S_PE = S_WO + KX
S_PG = S_PE + 2
STEPS = S_PG + KX
UNITS = 2 * STEPS

C_GPRE, C_GV, C_GO, C_BA, C_GPOST, C_PARAMS = 0, KX, KX + KE, KX + 2 * KE, KX + 2 * KE + HB, 2 * KX + 2 * KE + HB
C_ID, C_ONE, C_ATT, C_ATS, C_SEQ, C_RESET, C_CONSTS = 0, P, 2 * P, 3 * P, 3 * P + DEC, 3 * P + DEC + 4, 3 * P + DEC + 4 + T


class Tally:

    def __init__(self, sem):
        self.sem, self.base, self.k = sem, 0, 0

    @property
    def value(self):
        return self.base + self.k

    def up(self, ins):
        ins.then_inc(self.sem, 1)
        self.k += 1

    def next(self, eng, n=1):
        self.k += n
        eng.wait_ge(self.sem, self.value)


@contextmanager
def repeat(eng, n, per):
    starts = {t: t.value for t in per}
    with eng.Fori(0, n) as i:
        for t, by in per.items():
            t.base, t.k = starts[t] + by * i, 0
        yield i
        for t, by in per.items():
            assert t.k == by, (t.sem, t.k, by)
    for t, by in per.items():
        t.base, t.k = starts[t] + by * n, 0


def build(nc, A, O):
    ctx = ExitStack()
    with ctx:
        def sem(name):
            return ctx.enter_context(nc.semaphore(name))

        KB = 1024
        start = -(-nc.sbuf_base // 64) * 64
        SMALL = 19 * KB + 256
        total = 188 * KB + SMALL
        ctx.enter_context(nc.sbuf_tensor("arena", [P, (total + start - nc.sbuf_base + 3) // 4 + 1], F32))

        def at(name, off, shape, dtype=F32):
            assert off + int(np.prod(shape[1:])) * 4 <= total, name
            return nc.alloc_sbuf_tensor_at(name, shape, dtype, offset=start + off)

        W0, XG0, M0, Y0, X0, C0 = 0, 48 * KB, 88 * KB, 128 * KB, 168 * KB, 188 * KB
        TB = T * 4

        raw = at("w_raw", W0, [P, 4, UK, P])
        whi = at("w_hi", W0 + 16 * KB, [P, 4, UK, P], F32R)
        wlo = at("w_lo", W0 + 32 * KB, [P, 4, UK, P], F32R)
        xhi = at("x_hi", XG0, [P, KX, T], F32R)
        xlo = at("x_lo", XG0 + 20 * KB, [P, KX, T], F32R)
        p_raw = at("p_raw", XG0, [P, PLE // P, T])
        p_hi = at("p_hi", XG0 + 2 * TB, [P, PLE // P, T], F32R)
        p_lo = at("p_lo", XG0 + 4 * TB, [P, PLE // P, T], F32R)
        pe_out = at("pe_out", XG0 + 20 * KB, [P, KX, T])
        slot = HB * TB
        squares = at("squares", M0 + 2 * slot, [P, KX, T])
        dec_in = at("decay_in", M0, [P, HB, T])
        cum = at("decay_cum", M0 + slot, [P, HB, T])
        q_sb = at("q", M0 + 2 * slot, [P, HB, T])
        k_sb = at("k", M0 + 3 * slot, [P, HB, T])
        q_mid = at("q_mid", M0 + 4 * slot, [P, HB, T])
        k_mid = at("k_mid", M0 + 5 * slot, [P, HB, T])
        q_dec = at("q_dec", M0 + 6 * slot, [P, HB, T])
        wa2 = at("w_a2_sb", M0 + 7 * slot, [RANK, HB * DK])
        alr = at("a_lr", M0 + 7 * slot + 2 * KB, [RANK, T])
        o_sb = at("o", M0 + 2 * slot, [P, KE, T])
        za_gate = at("za_gate", M0, [P, KE, T])
        va_t = at("va_tokens", M0 + 4 * slot, [P, 2, EA])
        va_ts = at("va_tokens_dec", M0 + 7 * slot, [DEC, EA])
        v_sq = at("v_sq", M0 + 7 * slot + 2 * TB, [P, T])
        v_sum = at("v_sum", M0 + 7 * slot + 3 * TB, [P, T])
        o_sq = at("o_sq", M0 + 4 * slot, [P, HB, 2, T])
        r_o = at("r_o", M0 + 6 * slot, [P, HB, T])
        o_sum = at("o_sum", M0 + 7 * slot, [P, HB, T])
        mhi = at("m_hi", M0, [P, KX, T], F32R)
        mlo = at("m_lo", M0 + 20 * KB, [P, KX, T], F32R)
        kd_s = at("kd_tokens_dec", Y0, [DEC, 4, HB * DK])
        v_ts = at("v_tokens_dec", Y0 + 8 * KB, [DEC, EB])
        att_s = at("att_dec", Y0 + 12 * KB, [DEC, HB, DEC])
        wr_raw = at("w_alr_raw", Y0 + 13 * KB, [P, KX, RANK])
        wr_hi = at("w_alr_hi", Y0 + 14 * KB, [P, KX, RANK], F32R)
        wr_lo = at("w_alr_lo", Y0 + 15 * KB, [P, KX, RANK], F32R)
        st = at("state", Y0 + 16 * KB, [P, 2, HB, DV])
        v_t = at("v_tokens", Y0 + 24 * KB, [P, 2, EB])
        kd_t = at("kd_tokens", Y0 + 32 * KB, [P, 2, HB * DK])
        att = at("att", Y0 + 36 * KB, [P, 2, HB, P])
        s0 = at("state_dec", Y0 + 24 * KB, [P, 4, HB, DV])
        yhi = [at(n, Y0 + o * KB, [P, KE, T], F32R) for n, o in (("ya_hi", 0), ("yb_hi", 20))]
        ylo = [at(n, Y0 + o * KB, [P, KE, T], F32R) for n, o in (("ya_lo", 10), ("yb_lo", 30))]
        h_sb = at("h", Y0, [P, KX, T])
        x_sb = at("x_sb", X0, [P, KX, T])
        v_sb = at("v_b", X0, [P, KE, T])
        va_sb = at("v_a", X0, [P, KE, T])
        sp_sb = at("spatial", X0, [P, KE, T])
        zb_gate = at("zb_gate", X0 + 10 * KB, [P, KE, T])
        mo_sb = at("mo", X0, [P, KX, T])
        off = C0
        small = {}
        for name, shape in (("params", [P, C_PARAMS]), ("consts", [P, C_CONSTS]), ("w_s_t", [P, HA, CHUNK]),
                            ("w_s_dec", [DEC, HA, DEC]), ("b_s_sb", [P, HA, CHUNK]), ("decays", [P, HB, 2 * NBLK]),
                            ("r_tok", [P, T]), ("tmp", [P, 4, T]), ("sig", [P, 2, T])):
            small[name] = at(name, off, shape)
            off += -(-int(np.prod(shape[1:])) * 4 // 32) * 32
        par, con, wst, wsb, bs = (small[n] for n in ("params", "consts", "w_s_t", "w_s_dec", "b_s_sb"))
        decays, r_tok, tmp, sig = (small[n] for n in ("decays", "r_tok", "tmp", "sig"))
        ident, ones = con[:, C_ID:C_ID + P], con[:, C_ONE:C_ONE + P]

        def col(c, i):
            return par[:, c + i:c + i + 1]

        bank = [ctx.enter_context(nc.psum_tensor(f"bank{b}", [P, 512], F32)) for b in range(8)]

        x_loaded = [sem(f"x_loaded{c}") for c in range(4)]
        par_loaded, consts_loaded, alrw_loaded = sem("par_loaded"), sem("consts_loaded"), sem("alrw_loaded")
        raw_loaded = [sem(f"raw_loaded{q}") for q in range(4)]
        hi_ready = sem("hi_ready")
        lo_ready = sem("lo_ready")
        units_used = sem("units_used")
        acc_read = sem("acc_read")
        alr_hi, alr_lo = sem("alr_hi"), sem("alr_lo")
        x_rounded, x_split = sem("x_rounded"), sem("x_split")
        alr_done, alr_ready = sem("alr_done"), sem("alr_ready")
        sq_ready = sem("sq_ready")
        sum_done = sem("sum_done")
        var_ready = sem("var_ready")
        r_ready = sem("r_ready")
        logits_done = sem("logits_done")
        absneg_ready, softplus_ready = sem("absneg_ready"), sem("softplus_ready")
        spans_ready, exps_ready = sem("spans_ready"), sem("exps_ready")
        decays_kept, gla_in = sem("decays_kept"), sem("gla_in")
        att_zeroed, att_done, att_masked = sem("att_zeroed"), sem("att_done"), sem("att_masked")
        kdt_done, kdt_copied, kds_ready = sem("kdt_done"), sem("kdt_copied"), sem("kds_ready")
        vt_done, vt_copied = sem("vt_done"), sem("vt_copied")
        kv_done, st_ready = sem("kv_done"), sem("st_ready")
        o_done, o_copied = sem("o_done"), sem("o_copied")
        ws_masked = sem("ws_masked")
        va_normed, vat_done, vat_copied = sem("va_normed"), sem("vat_done"), sem("vat_copied")
        sp_done, sp_read = sem("sp_done"), sem("sp_read")
        s0_loaded = [sem(f"s0_loaded{q}") for q in range(4)]
        s0_stored = [sem(f"s0_stored{q}") for q in range(4)]
        st_stored, cv_stored = sem("st_stored"), sem("cv_stored")
        sig_done = sem("sig_done")
        y_full, y_rounded, y_split = sem("y_full"), sem("y_rounded"), sem("y_split")
        m_full, m_rounded, m_split = sem("m_full"), sem("m_rounded"), sem("m_split")
        p_loaded, p_rounded, p_split = sem("p_loaded"), sem("p_rounded"), sem("p_split")
        xr_loaded = [sem(f"xr_loaded{c}") for c in range(4)]
        pe_read = sem("pe_read")
        hn_ready, h_full, h_rounded, h_split = sem("hn_ready"), sem("h_full"), sem("h_rounded"), sem("h_split")
        out_ready, out_stored = sem("out_ready"), sem("out_stored")
        dve_own, act_own, pool_own = sem("dve_own"), sem("act_own"), sem("pool_own")

        block = ctx.enter_context(nc.Block())

        @block.sync
        def _(sp):
            for c in range(4):
                sp.dma_start(x_sb[:, 4 * c:4 * c + 4, :], A["x_t"][:, 4 * c:4 * c + 4, :]).then_inc(x_loaded[c], 16)
                if c == 0:
                    sp.dma_start(wr_raw[:, :, :], A["w_alr"]).then_inc(alrw_loaded, 16)
            for q in range(4):
                sp.dma_start(raw[:, q], A["w_units"][q]).then_inc(raw_loaded[q], 16)
            with sp.Fori(1, UNITS // 4) as i:
                for q in range(4):
                    sp.wait_ge(lo_ready, 4 * i + (q - 3))
                    sp.dma_start(raw[:, q], A["w_units"][4 * i + q]).then_inc(raw_loaded[q], 16)

        @block.scalar
        def _(act):
            sig_t, m_full_t, out_t = Tally(sig_done), Tally(m_full), Tally(out_ready)
            y_full_t, own = Tally(y_full), Tally(act_own)

            def split_hi(s, i=None):
                for half in range(2):
                    q = 2 * (s % 2) + half
                    turn = 16 * ((s + 2) // 2 + 1)
                    used = 2 * (s + 2) + half - 3
                    act.wait_ge(raw_loaded[q], turn if i is None else 16 * i + turn)
                    act.wait_ge(units_used, used if i is None else 4 * i + used)
                    act.activation(whi[:, q], raw[:, q], ACT.Copy).then_inc(hi_ready, 1)

            act.dma_start(par[:, :], A["params"]).then_inc(par_loaded, 16)
            for dst, name in ((con, "consts"), (wst, "w_s_t"), (wsb, "w_s_dec"), (bs, "b_s_rows")):
                act.dma_start(dst[:], A[name]).then_inc(consts_loaded, 16)
            act.dma_start(wa2[:, :], A["w_a2"]).then_inc(consts_loaded, 16)
            act.wait_ge(par_loaded, 16)
            for k in range(KX):
                if k % 4 == 0:
                    act.wait_ge(x_loaded[k // 4], 16)
                act.activation(xhi[:, k, :], x_sb[:, k, :], ACT.Copy, scale=col(C_GPRE, k)).then_inc(x_rounded, 1)
                if k == 3:
                    act.wait_ge(alrw_loaded, 16)
                    act.activation(wr_hi[:], wr_raw[:], ACT.Copy).then_inc(alr_hi, 1)
            for q in range(4):
                act.wait_ge(raw_loaded[q], 16)
                act.activation(whi[:, q], raw[:, q], ACT.Copy).then_inc(hi_ready, 1)

            def root(n, out, x):
                act.wait_ge(var_ready, n)
                act.activation(out, x, ACT.Sqrt).then_inc(r_ready, 1)

            for s in range(S_K, S_Q):
                split_hi(s)
                if s == S_K:
                    root(1, r_tok[:, :], tmp[:, 0, :])
                if s == S_K + 1:
                    act.wait_ge(absneg_ready, 1)
                    act.activation(cum[:], cum[:], ACT.Exp).then_inc(act_own, 1)
                    act.wait_ge(act_own, 1)
                    act.activation(cum[:], cum[:], ACT.Ln, bias=1.0).then_inc(softplus_ready, 1)
            act.wait_ge(spans_ready, 4)
            act.activation(q_dec[:], cum[:], ACT.Exp, scale=1 / TAU).then_inc(exps_ready, 1)
            act.activation(k_mid[:], q_mid[:], ACT.Exp, scale=-1 / TAU).then_inc(exps_ready, 1)
            act.wait_ge(exps_ready, 2)
            act.activation(q_mid[:], q_mid[:], ACT.Exp, scale=1 / TAU).then_inc(exps_ready, 1)
            act.activation(dec_in[:], dec_in[:], ACT.Exp, scale=1 / TAU).then_inc(exps_ready, 1)
            with repeat(act, HB // 2, {}) as i:
                for b in range(2):
                    split_hi(S_Q + b, i)
            with repeat(act, KE // 2, {}) as i:
                for b in range(2):
                    split_hi(S_V + b, i)

            def sigmoid(s):
                act.wait_ge(acc_read, s + 1)
                sig_t.up(act.activation(sig[:, 0, :], tmp[:, 0, :], ACT.Sigmoid))

            for t, s in enumerate(range(S_ZB, S_VA)):
                split_hi(s)
                sigmoid(s)
                if t == 1:
                    act.wait_ge(kdt_done, 1)
                    for c in range(2):
                        act.activation(kd_t[:, c, :], bank[4 + c][:, :], ACT.Copy).then_inc(kdt_copied, 1)
                if 2 <= t <= 4:
                    act.wait_ge(vt_done, t - 1)
                    rows, dst = (P, v_t[:, t - 2, :]) if t < 4 else (DEC, v_ts[:, :])
                    for c in range(2):
                        act.activation(dst[:, 512 * c:512 * c + 512], bank[2 + c][0:rows, :], ACT.Copy)\
                           .then_inc(vt_copied, 1)
            for c, s in enumerate(range(S_VA, S_ZA)):
                split_hi(s)
                act.wait_ge(o_done, c + 1)
                act.activation(o_sb[:, :, BLK * c:BLK * c + BLK],
                               bank[6 + c % 2][:, 0:KE * BLK].rearrange("p (i t) -> p i t", t=BLK),
                               ACT.Copy).then_inc(o_copied, 1)

            def load_s0(b):
                act.dma_start(s0[:, b % 4], A["s0"][b].rearrange("h d v -> d h v")).then_inc(s0_loaded[b % 4], 16)

            for b, s in enumerate(range(S_ZA, S_U)):
                if b == 0:
                    for n in range(4):
                        load_s0(n)
                    act.wait_ge(st_ready, HB * NBLK)
                    act.dma_start(O["st_prompt"].rearrange("h d v -> d h v"), st[:, 0]).then_inc(st_stored, 16)
                split_hi(s)
                if b == 0:
                    root(2, tmp[:, 1, :], tmp[:, 1, :])
                sigmoid(s)
                if b == 1:
                    act.wait_ge(va_normed, KE)
                    act.dma_start(O["cv"].rearrange("i p t -> p i t"), va_sb[:, :, SEQ:T]).then_inc(cv_stored, 16)
                if 1 <= b <= 3:
                    act.wait_ge(vat_done, b)
                    rows, dst = (P, va_t[:, b - 1, :]) if b < 3 else (DEC, va_ts[:, :])
                    for c in range(2):
                        act.activation(dst[:, 512 * c:512 * c + 512], bank[2 + c][0:rows, :], ACT.Copy)\
                           .then_inc(vat_copied, 1)
                if b >= 1:
                    act.wait_ge(st_ready, HB * (NBLK + b))
                    act.dma_start(O["st_dec"][b - 1].rearrange("h d v -> d h v"), s0[:, (b - 1) % 4])\
                       .then_inc(s0_stored[(b - 1) % 4], 16)
                if 2 <= b and b + 2 < DEC_B:
                    act.wait_ge(s0_stored[(b - 2) % 4], 16)
                    load_s0(b + 2)
                if b == DEC_B - 1:
                    act.wait_ge(o_done, NBLK + DEC_B)
                    act.activation(o_sb[:, :, SEQ:T], bank[6][:, :].rearrange("p (i t) -> p i t", t=DEC),
                                   ACT.Copy).then_inc(o_copied, 1)

            for j, s in enumerate(range(S_U, S_GATE)):
                if j == 0:
                    act.wait_ge(st_ready, HB * (NBLK + DEC_B))
                    act.dma_start(O["st_dec"][DEC_B - 1].rearrange("h d v -> d h v"), s0[:, 3])\
                       .then_inc(s0_stored[3], 16)
                    act.wait_ge(st_stored, 16)
                    for q in range(4):
                        act.wait_ge(s0_stored[q], 32)
                split_hi(s)
                if j == 1:
                    root(2 + HB, r_o[:], r_o[:])
                tiles = [(0, j)] + ([(1, j - 1)] if j else [])
                for br, i in tiles:
                    y_full_t.next(act)
                    act.activation(yhi[br][:, i, :], tmp[:, 2 + br, :], ACT.Copy).then_inc(y_rounded, 1)
            y_full_t.next(act)
            act.activation(yhi[1][:, KE - 1, :], tmp[:, 3, :], ACT.Copy).then_inc(y_rounded, 1)

            with repeat(act, KX // 2, {sig_t: 4, m_full_t: 2}) as i:
                for b in range(2):
                    for g in range(3):
                        n = 3 * b + g
                        for half in range(2):
                            q = 2 * (n % 2) + half
                            turn = 16 * ((S_GATE + n + 2) // 2 + 1)
                            used = 2 * (S_GATE + n + 2) + half - 3
                            act.wait_ge(raw_loaded[q], 48 * i + turn)
                            act.wait_ge(units_used, 12 * i + used)
                            act.activation(whi[:, q], raw[:, q], ACT.Copy).then_inc(hi_ready, 1)
                        if g < 2:
                            act.wait_ge(acc_read, 6 * i + (S_GATE + n + 1))
                            sig_t.up(act.activation(sig[:, g, :], tmp[:, g, :], ACT.Sigmoid))
                        else:
                            m_full_t.next(act)
                            act.activation(mhi[:, 2 * i + b, :], tmp[:, 2, :], ACT.Copy).then_inc(m_rounded, 1)

            act.wait_ge(units_used, 2 * S_WO)
            act.dma_start(p_raw[:], A["p_t"]).then_inc(p_loaded, 16)
            for c in range(4):
                act.dma_start(h_sb[:, 4 * c:4 * c + 4, :], A["x_t"][:, 4 * c:4 * c + 4, :]).then_inc(xr_loaded[c], 16)
            with repeat(act, KX // 2, {}) as i:
                for b in range(2):
                    for half in range(2):
                        q = 2 * b + half
                        act.wait_ge(raw_loaded[q], 16 * i + 16 * ((S_WO + b + 2) // 2 + 1))
                        act.wait_ge(units_used, 4 * i + (2 * (S_WO + b + 2) + half - 3))
                        act.activation(whi[:, q], raw[:, q], ACT.Copy).then_inc(hi_ready, 1)
            act.wait_ge(p_loaded, 16)
            act.activation(p_hi[:], p_raw[:], ACT.Copy).then_inc(p_rounded, 1)
            for n, s in enumerate((S_PE, S_PE + 1)):
                for half in range(2):
                    act.wait_ge(units_used, 2 * s + half + 1)
                    for c in range(4):
                        act.activation(pe_out[:, 8 * n + 4 * half + c, :], bank[(4 * half + 4 * n + c) % 8][:, 0:T],
                                       ACT.Copy).then_inc(pe_read, 1)
                split_hi(s)
                if n == 0:
                    root(3 + HB, r_tok[:, :], r_tok[:, :])
            for k in range(KX):
                act.wait_ge(h_full, k + 1)
                act.activation(mhi[:, k, :], h_sb[:, k, :], ACT.Copy).then_inc(h_rounded, 1)

            def last_gate(s, b, i=None):
                act.wait_ge(units_used, 2 * s + 2 if i is None else 4 * i + (2 * s + 2))
                sig_t.up(act.activation(sig[:, b, :], bank[b][:, 0:T], ACT.Sigmoid))

            def store(j):
                out_t.next(act)
                act.dma_start(O["y"][:, j, :], pe_out[:, j, :]).then_inc(out_stored, 16)

            for j in range(2):
                split_hi(S_PG + j)
                last_gate(S_PG + j, j)
            with repeat(act, KX // 2 - 2, {sig_t: 2, out_t: 2}) as i:
                for b in range(2):
                    split_hi(S_PG + 2 + b, i)
                    last_gate(S_PG + 2 + b, b, i)
                    store(2 * i + b)
            for j in range(KX - 2, KX):
                last_gate(S_PG + j, j % 2)
                store(j - 2)
            store(KX - 2)
            store(KX - 1)
            act.wait_ge(out_stored, 16 * KX)
            act.wait_ge(cv_stored, 16)

        @block.vector
        def _(dve):
            own = Tally(dve_own)
            sig_t, acc_t = Tally(sig_done), Tally(acc_read)
            y_full_t, y_round_t = Tally(y_full), Tally(y_rounded)
            m_full_t, m_round_t = Tally(m_full), Tally(m_rounded)
            out_t = Tally(out_ready)
            st_t = Tally(st_ready)

            def then(ins):
                own.up(ins)
                dve.wait_ge(dve_own, own.value)

            def low(q, ready, used):
                dve.wait_ge(hi_ready, ready)
                dve.wait_ge(units_used, used)
                dve.tensor_tensor(wlo[:, q], raw[:, q], whi[:, q].bitcast(F32), ALU.subtract).then_inc(lo_ready, 1)

            def split_lo(s, i=None):
                for half in range(2):
                    u = 2 * (s + 2) + half
                    low(2 * (s % 2) + half, *((u + 1, u - 3) if i is None else (4 * i + (u + 1), 4 * i + (u - 3))))

            def sums(s, i=None, by=4):
                dve.wait_ge(units_used, 2 * s + 2 if i is None else by * i + (2 * s + 2))

            def variance(out, src, n):
                then(dve.tensor_scalar(out, src, 1.0 / n, EPS, ALU.mult, ALU.add))
                dve.reciprocal(out, out).then_inc(var_ready, 1)

            dve.wait_ge(par_loaded, 16)
            for k in range(KX):
                if k == 4:
                    dve.wait_ge(alr_hi, 1)
                    dve.tensor_tensor(wr_lo[:], wr_raw[:], wr_hi[:].bitcast(F32), ALU.subtract).then_inc(alr_lo, 1)
                dve.wait_ge(x_rounded, k + 1)
                dve.scalar_tensor_tensor(xlo[:, k, :], x_sb[:, k, :], col(C_GPRE, k), xhi[:, k, :].bitcast(F32),
                                         ALU.mult, ALU.subtract).then_inc(x_split, 1)
            for q in range(4):
                dve.wait_ge(hi_ready, q + 1)
                dve.tensor_tensor(wlo[:, q], raw[:, q], whi[:, q].bitcast(F32), ALU.subtract).then_inc(lo_ready, 1)
            dve.wait_ge(consts_loaded, 16 * 5)

            r = r_tok[:, :]
            for s in range(S_K, S_Q):
                split_lo(s)
                if s == S_K:
                    dve.wait_ge(sum_done, 1)
                    variance(tmp[:, 0, :], bank[5][:, 0:T], D)
                    dve.wait_ge(r_ready, 1)
                sums(s)
                acc_t.up(dve.tensor_tensor(k_sb[:, s - S_K, :], bank[s % 2][:, 0:T], r, ALU.mult))
                if s == S_K:
                    dve.tensor_tensor(alr[:, :], bank[4][0:RANK, 0:T], r_tok[0:RANK, :], ALU.mult)\
                       .then_inc(alr_ready, 1)
                if s == S_K + 1:
                    dve.wait_ge(logits_done, 1)
                    for h in range(HB):
                        own.up(dve.tensor_scalar(dec_in[:, h, :], bank[4 + h][:, 0:T], col(C_BA, h), None, ALU.add))
                    dve.wait_ge(dve_own, own.value)
                    dve.scalar_tensor_tensor(cum[:], dec_in[:], -1.0, dec_in[:], ALU.mult, ALU.min)\
                       .then_inc(absneg_ready, 1)
                if s == S_K + 2:
                    dve.wait_ge(softplus_ready, 1)
                    then(dve.scalar_tensor_tensor(dec_in[:], dec_in[:], 0.0, cum[:], ALU.min, ALU.subtract))
                    for h in range(HB):
                        own.up(dve.tensor_tensor_scan(cum[:, h, :], con[:, C_RESET:C_RESET + T], dec_in[:, h, :], 0.0,
                                                      ALU.mult, ALU.add))
                    dve.wait_ge(dve_own, own.value)
                if s == S_K + 3:
                    prompt = [x[:, :, 0:SEQ].rearrange("p h (c t) -> p h c t", t=BLK) for x in (cum, q_mid, dec_in)]
                    dec = [x[:, :, SEQ:T].rearrange("p h (c t) -> p h c t", t=DEC_L) for x in (cum, dec_in)]
                    mid = prompt[0][:, :, :, MID:MID + 1].to_broadcast([P, HB, NBLK, BLK])
                    end = prompt[0][:, :, :, BLK - 1:BLK].to_broadcast([P, HB, NBLK, BLK])
                    end_d = dec[0][:, :, :, DEC_L - 1:DEC_L].to_broadcast([P, HB, DEC_B, DEC_L])
                    dve.tensor_tensor(prompt[1], prompt[0], mid, ALU.subtract).then_inc(spans_ready, 1)
                    dve.tensor_copy(q_mid[:, :, SEQ:T], cum[:, :, SEQ:T]).then_inc(spans_ready, 1)
                    dve.tensor_tensor(prompt[2], end, prompt[0], ALU.subtract).then_inc(spans_ready, 1)
                    dve.tensor_tensor(dec[1], end_d, dec[0], ALU.subtract).then_inc(spans_ready, 1)
            with repeat(dve, HB // 2, {acc_t: 2}) as i:
                for b in range(2):
                    split_lo(S_Q + b, i)
                    sums(S_Q + b, i)
                    acc_t.up(dve.scalar_tensor_tensor(q_sb[:, 2 * i + b, :], bank[b][:, 0:T], float(DK) ** -0.5, r,
                                                      ALU.mult, ALU.mult))
            dve.wait_ge(exps_ready, 4)
            ends = q_dec[:, :, 0:SEQ].rearrange("p h (c t) -> p h c t", t=BLK)[:, :, :, BLK - 1]
            ends_d = q_dec[:, :, SEQ:T].rearrange("p h (c t) -> p h c t", t=DEC_L)[:, :, :, DEC_L - 1]
            dve.tensor_copy(decays[:, :, 0:NBLK], ends).then_inc(decays_kept, 1)
            dve.tensor_copy(decays[:, :, NBLK:NBLK + DEC_B], ends_d).then_inc(decays_kept, 1)
            with repeat(dve, KE // 2, {acc_t: 2}) as i:
                for b in range(2):
                    split_lo(S_V + b, i)
                    sums(S_V + b, i)
                    acc_t.up(dve.tensor_tensor(v_sb[:, 2 * i + b, :], bank[b][:, 0:T], r, ALU.mult))

            def silu(s, out):
                sums(s)
                acc_t.up(dve.tensor_tensor(tmp[:, 0, :], bank[s % 2][:, 0:T], r, ALU.mult))
                sig_t.next(dve)
                then(dve.tensor_tensor(out, tmp[:, 0, :], sig[:, 0, :], ALU.mult))

            for t, s in enumerate(range(S_ZB, S_VA)):
                split_lo(s)
                silu(s, zb_gate[:, t, :])
                if t == 0:
                    dve.wait_ge(att_zeroed, 2)
                    dve.wait_ge(att_done, 1)
                    mask = con[:, C_ATT:C_ATT + P].bitcast(I32)
                    for c in range(2):
                        for h in range(HB):
                            last = dve.copy_predicated(att[:, c, h, :], mask, bank[4 + c][:, P * h:P * h + P])
                        last.then_inc(att_masked, 1)
                    mask = con[0:DEC, C_ATS:C_ATS + DEC].bitcast(I32)
                    for h in range(HB):
                        last = dve.copy_predicated(att_s[:, h, :], mask, bank[6][0:DEC, DEC * h:DEC * h + DEC])
                    last.then_inc(att_masked, 1)
                if t == 1:
                    dve.wait_ge(kdt_done, 1)
                    for n in range(4):
                        dve.tensor_scalar(kd_s[:, n, :], bank[6][0:DEC, :], con[0:DEC, C_SEQ + n:C_SEQ + n + 1], None,
                                          ALU.mult).then_inc(kds_ready, 1)

            def new_state(n, c, src, dst):
                dve.wait_ge(kv_done, n + 1)
                if n:
                    dve.wait_ge(o_done, n + 1)
                for h in range(HB):
                    kv = bank[4 + h // 2][:, DV * (h % 2):DV * (h % 2) + DV]
                    if src is None:
                        st_t.up(dve.tensor_copy(dst[:, h, :], kv))
                    else:
                        st_t.up(dve.scalar_tensor_tensor(dst[:, h, :], src[:, h, :], decays[:, h, n:n + 1], kv,
                                                         ALU.mult, ALU.add))
                dve.wait_ge(st_ready, st_t.value)

            for c, s in enumerate(range(S_VA, S_ZA)):
                split_lo(s)
                sums(s)
                acc_t.up(dve.tensor_tensor(va_sb[:, c, :], bank[s % 2][:, 0:T], r, ALU.mult))
                new_state(c, c, st[:, c % 2] if c else None, st[:, (c + 1) % 2])

            for b, s in enumerate(range(S_ZA, S_U)):
                split_lo(s)
                if b == 0:
                    dve.wait_ge(sum_done, 2)
                    variance(tmp[:, 1, :], bank[7][:, 0:T], EA)
                silu(s, za_gate[:, b, :])
                new_state(NBLK + b, b, s0[:, b % 4], s0[:, b % 4])
                if b == 0:
                    dve.wait_ge(r_ready, 2)
                    for i in range(KE):
                        dve.scalar_tensor_tensor(va_sb[:, i, :], va_sb[:, i, :], col(C_GV, i), tmp[:, 1, :],
                                                 ALU.mult, ALU.mult).then_inc(va_normed, 1)
                if b >= 4:
                    dve.wait_ge(sp_done, b - 3)
                    if b == 4:
                        dve.wait_ge(cv_stored, 16)
                    for c in range(2):
                        i = 2 * (b - 4) + c
                        h = i // 2
                        dve.tensor_tensor(sp_sb[:, i, 0:SEQ].rearrange("p (c t) -> p c t", t=CHUNK),
                                          bank[2 + c][:, 0:SEQ].rearrange("p (c t) -> p c t", t=CHUNK),
                                          bs[:, h:h + 1, :].to_broadcast([P, 2, CHUNK]), ALU.add).then_inc(sp_read, 1)
                        dve.tensor_tensor(sp_sb[:, i, SEQ:T].rearrange("p (c t) -> p c t", t=DEC_L),
                                          bank[2 + c][:, SEQ:T].rearrange("p (c t) -> p c t", t=DEC_L),
                                          bs[:, h:h + 1, 0:DEC_L].to_broadcast([P, DEC_B, DEC_L]), ALU.add)\
                           .then_inc(sp_read, 1)
            dve.wait_ge(sp_read, 4 * 4)

            def yb(i):
                then(dve.scalar_tensor_tensor(tmp[:, 1, :], o_sb[:, i, :], col(C_GO, i), r_o[:, i // 2, :],
                                              ALU.mult, ALU.mult))
                y_full_t.up(dve.tensor_tensor(tmp[:, 3, :], tmp[:, 1, :], zb_gate[:, i, :], ALU.mult))

            def y_low(br, i):
                y_round_t.next(dve)
                dve.tensor_tensor(ylo[br][:, i, :], tmp[:, 2 + br, :], yhi[br][:, i, :].bitcast(F32), ALU.subtract)\
                   .then_inc(y_split, 1)

            for j, s in enumerate(range(S_U, S_GATE)):
                split_lo(s)
                sums(s)
                acc_t.up(dve.tensor_tensor(tmp[:, 0, :], bank[s % 2][:, 0:T], r, ALU.mult))
                dve.wait_ge(acc_read, acc_t.value)
                then(dve.tensor_tensor(tmp[:, 1, :], tmp[:, 0, :], za_gate[:, j, :], ALU.mult))
                if j:
                    dve.wait_ge(y_split, 2 * j - 1)
                y_full_t.up(dve.tensor_tensor(tmp[:, 2, :], tmp[:, 1, :], sp_sb[:, j, :], ALU.mult))
                if j:
                    dve.wait_ge(y_full, y_full_t.value)
                    if j == 1:
                        dve.wait_ge(r_ready, 3)
                    yb(j - 1)
                y_low(0, j)
                if j:
                    y_low(1, j - 1)
                if j == 0:
                    dve.wait_ge(sum_done, 3)
                    for h in range(HB):
                        variance(r_o[:, h, :], bank[4 + h][:, 0:T], DV)
            dve.wait_ge(y_split, 2 * KE - 1)
            yb(KE - 1)
            y_low(1, KE - 1)
            dve.wait_ge(y_split, 2 * KE)

            with repeat(dve, KX // 2, {acc_t: 6, sig_t: 4, own: 2, m_full_t: 2, m_round_t: 2}) as i:
                for b in range(2):
                    for g in range(3):
                        n = 3 * b + g
                        for half in range(2):
                            u = 2 * (S_GATE + n + 2) + half
                            low(2 * (n % 2) + half, 12 * i + (u + 1), 12 * i + (u - 3))
                        sums(S_GATE + n, i, 12)
                        if g < 2:
                            acc_t.up(dve.tensor_tensor(tmp[:, g, :], bank[n % 2][:, 0:T], r, ALU.mult))
                    sig_t.next(dve, 2)
                    own.up(dve.tensor_tensor(tmp[:, 2, :], bank[2][:, 0:T], sig[:, 0, :], ALU.mult))
                    acc_t.up(dve.tensor_tensor(tmp[:, 3, :], bank[3][:, 0:T], sig[:, 1, :], ALU.mult))
                    dve.wait_ge(acc_read, acc_t.value)
                    m_full_t.up(dve.tensor_tensor(tmp[:, 2, :], tmp[:, 2, :], tmp[:, 3, :], ALU.add))
                    m_round_t.next(dve)
                    dve.tensor_tensor(mlo[:, 2 * i + b, :], tmp[:, 2, :], mhi[:, 2 * i + b, :].bitcast(F32),
                                      ALU.subtract).then_inc(m_split, 1)
                    dve.wait_ge(m_split, 2 * i + (b + 1))

            with repeat(dve, KX // 2, {acc_t: 2}) as i:
                for b in range(2):
                    split_lo(S_WO + b, i)
                    sums(S_WO + b, i)
                    acc_t.up(dve.tensor_copy(mo_sb[:, 2 * i + b, :], bank[b][:, 0:T]))
            dve.wait_ge(p_rounded, 1)
            dve.tensor_tensor(p_lo[:], p_raw[:], p_hi[:].bitcast(F32), ALU.subtract).then_inc(p_split, 1)
            split_lo(S_PE)
            dve.wait_ge(sum_done, 4)
            variance(r_tok[:, :], bank[0][:, 0:T], D)
            split_lo(S_PE + 1)
            dve.wait_ge(r_ready, 4)
            AHEAD = 3
            for k in range(KX + AHEAD):
                if k < KX:
                    if k >= 4:
                        dve.wait_ge(h_full, k - 3)
                    dve.scalar_tensor_tensor(tmp[:, k % 4, :], mo_sb[:, k, :], col(C_GPOST, k), r, ALU.mult, ALU.mult)\
                       .then_inc(hn_ready, 1)
                if k >= AHEAD:
                    n = k - AHEAD
                    dve.wait_ge(h_rounded, n + 1)
                    dve.tensor_tensor(mlo[:, n, :], h_sb[:, n, :], mhi[:, n, :].bitcast(F32), ALU.subtract)\
                       .then_inc(h_split, 1)

            def output(j, b):
                sig_t.next(dve)
                acc_t.up(dve.tensor_tensor(tmp[:, b, :], sig[:, b, :], pe_out[:, j, :], ALU.mult))
                dve.wait_ge(acc_read, acc_t.value)
                out_t.up(dve.tensor_tensor(pe_out[:, j, :], tmp[:, b, :], h_sb[:, j, :], ALU.add))
                dve.wait_ge(out_ready, out_t.value)

            for j in range(2):
                split_lo(S_PG + j)
                output(j, j)
            with repeat(dve, KX // 2 - 2, {sig_t: 2, acc_t: 2, out_t: 2}) as i:
                for b in range(2):
                    split_lo(S_PG + 2 + b, i)
                    output(2 * i + (b + 2), b)
            for j in range(KX - 2, KX):
                output(j, j % 2)

        @block.gpsimd
        def _(pool):
            own = Tally(pool_own)

            def then(ins):
                own.up(ins)
                pool.wait_ge(pool_own, own.value)

            pool.memset(att[:], 0.0).then_inc(att_zeroed, 1)
            pool.memset(att_s[:], 0.0).then_inc(att_zeroed, 1)
            for c in range(4):
                pool.wait_ge(x_loaded[c], 16)
                own.up(pool.tensor_tensor(squares[:, 4 * c:4 * c + 4, :], x_sb[:, 4 * c:4 * c + 4, :],
                                          x_sb[:, 4 * c:4 * c + 4, :], ALU.mult))
                pool.wait_ge(pool_own, own.value)
                if c:
                    own.up(pool.tensor_tensor(squares[:, 0:4, :], squares[:, 0:4, :],
                                              squares[:, 4 * c:4 * c + 4, :], ALU.add))
            pool.wait_ge(pool_own, own.value)
            then(pool.tensor_tensor(squares[:, 0:2, :], squares[:, 0:2, :], squares[:, 2:4, :], ALU.add))
            pool.tensor_tensor(squares[:, 0, :], squares[:, 0, :], squares[:, 1, :], ALU.add).then_inc(sq_ready, 1)
            pool.wait_ge(consts_loaded, 16 * 5)
            for w, n in ((wst, CHUNK), (wsb, DEC)):
                pool.affine_select(out=w[:], in_=w[:], compare_op=ALU.is_ge, fill=0.0, base=0,
                                   pattern=[[0, HA], [1, n]], channel_multiplier=-1).then_inc(ws_masked, 1)
            pool.wait_ge(acc_read, S_V)
            pool.wait_ge(decays_kept, 2)
            for x, y in ((k_mid, k_sb), (q_mid, q_sb), (dec_in, k_sb), (q_dec, q_sb)):
                pool.tensor_tensor(x[:], x[:], y[:], ALU.mult).then_inc(gla_in, 1)

            def add_squares(x, first, last):
                if first:
                    then(pool.tensor_tensor(v_sum[:, :], x, x, ALU.mult))
                else:
                    then(pool.tensor_tensor(v_sq[:, :], x, x, ALU.mult))
                    add = pool.tensor_tensor(v_sum[:, :], v_sum[:, :], v_sq[:, :], ALU.add)
                    if last:
                        add.then_inc(sq_ready, 1)
                    else:
                        then(add)

            for c in range(KE):
                pool.wait_ge(acc_read, S_VA + c + 1)
                add_squares(va_sb[:, c, :], c == 0, c == KE - 1)
            pool.wait_ge(sp_done, 4)
            pool.wait_ge(o_copied, NBLK + 1)
            then(pool.tensor_tensor(o_sq[:], o_sb[:].rearrange("p (h i) t -> p h i t", i=2),
                                    o_sb[:].rearrange("p (h i) t -> p h i t", i=2), ALU.mult))
            pool.tensor_tensor(o_sum[:], o_sq[:, :, 0, :], o_sq[:, :, 1, :], ALU.add).then_inc(sq_ready, 1)
            pool.wait_ge(acc_read, S_WO + 1)
            then(pool.tensor_tensor(sig[:, 0, :], mo_sb[:, 0, :], mo_sb[:, 0, :], ALU.mult))
            with repeat(pool, KX - 2, {own: 2}) as i:
                pool.wait_ge(acc_read, i + (S_WO + 2))
                then(pool.tensor_tensor(sig[:, 1, :], mo_sb[:, i + 1, :], mo_sb[:, i + 1, :], ALU.mult))
                then(pool.tensor_tensor(sig[:, 0, :], sig[:, 0, :], sig[:, 1, :], ALU.add))
            pool.wait_ge(acc_read, S_WO + KX)
            then(pool.tensor_tensor(sig[:, 1, :], mo_sb[:, KX - 1, :], mo_sb[:, KX - 1, :], ALU.mult))
            pool.tensor_tensor(sig[:, 0, :], sig[:, 0, :], sig[:, 1, :], ALU.add).then_inc(sq_ready, 1)
            for k in range(KX):
                if k % 4 == 0:
                    pool.wait_ge(xr_loaded[k // 4], 16)
                pool.wait_ge(hn_ready, k + 1)
                pool.tensor_tensor(h_sb[:, k, :], h_sb[:, k, :], tmp[:, k % 4, :], ALU.add).then_inc(h_full, 1)

        @block.tensor
        def _(pe):
            def product(acc, q, hi, lo, k0, first, last, used=True, wait_k=None):
                for k in range(UK):
                    if wait_k is not None:
                        pe.wait_ge(wait_k, k0 + k + 1)
                    h, l = whi[:, q, k, :], wlo[:, q, k, :]
                    pe.matmul(acc, h, hi[:, k0 + k, :], start=first and k == 0, stop=False)
                    pe.matmul(acc, h, lo[:, k0 + k, :], start=False, stop=False)
                    m = pe.matmul(acc, l, hi[:, k0 + k, :], start=False, stop=last and k == UK - 1)
                m.then_inc(units_used, 1)

            def ready(u, i=None, by=4):
                pe.wait_ge(lo_ready, u + 1 if i is None else by * i + (u + 1))

            def step(s, hi, lo, i=None, by=2, free=None, wait_k=None):
                if s >= 2:
                    n = s - 1 if free is None else free
                    pe.wait_ge(acc_read, n if i is None else by * i + n)
                for half in range(2):
                    ready(2 * s + half, i, 2 * by)
                    product(bank[s % 2][:, 0:T], 2 * (s % 2) + half, hi, lo, UK * half, half == 0, half == 1,
                            wait_k=wait_k)

            def sum_partitions(acc, x):
                return pe.matmul(acc, ones, x, start=True, stop=True)

            pe.wait_ge(alr_lo, 1)
            for k in range(KX):
                pe.wait_ge(x_split, k + 1)
                acc = bank[4][0:RANK, 0:T]
                pe.matmul(acc, wr_hi[:, k, :], xhi[:, k, :], start=k == 0, stop=False)
                pe.matmul(acc, wr_hi[:, k, :], xlo[:, k, :], start=False, stop=False)
                m = pe.matmul(acc, wr_lo[:, k, :], xhi[:, k, :], start=False, stop=k == KX - 1)
            m.then_inc(alr_done, 1)
            pe.wait_ge(consts_loaded, 16 * 5)
            for s in range(S_K, S_Q):
                step(s, xhi, xlo)
                if s == S_K:
                    pe.wait_ge(sq_ready, 1)
                    sum_partitions(bank[5][:, 0:T], squares[:, 0, :]).then_inc(sum_done, 1)
                if s == S_K + 1:
                    pe.wait_ge(alr_ready, 1)
                    for h in range(HB):
                        m = pe.matmul(bank[4 + h][:, 0:T], wa2[:, DK * h:DK * h + DK], alr[:, :], start=True, stop=True)
                    m.then_inc(logits_done, 1)
            for at_, n in ((S_Q, HB), (S_V, KE)):
                with repeat(pe, n // 2, {}) as i:
                    for b in range(2):
                        step(at_ + b, xhi, xlo, i)

            def to_tokens(x, t, done):
                w = P if t < 2 else DEC
                for i in range(KE):
                    m = pe.transpose(bank[2 + i // 4][0:w, P * (i % 4):P * (i % 4) + P],
                                     x[:, i, P * t:P * t + w], ident)
                m.then_inc(done, 1)

            for t, s in enumerate(range(S_ZB, S_VA)):
                step(s, xhi, xlo)
                if t == 0:
                    pe.wait_ge(gla_in, 4)
                    for c in range(2):
                        for h in range(HB):
                            pe.matmul(bank[4 + c][:, P * h:P * h + P], k_mid[:, h, P * c:P * c + P],
                                      q_mid[:, h, P * c:P * c + P], start=True, stop=True)
                    for h in range(HB):
                        m = pe.matmul(bank[6][0:DEC, DEC * h:DEC * h + DEC], k_mid[:, h, SEQ:T], q_mid[:, h, SEQ:T],
                                      start=True, stop=True)
                    m.then_inc(att_done, 1)
                if t == 1:
                    pe.wait_ge(att_masked, 3)
                    for c in range(3):
                        w = P if c < 2 else DEC
                        for h in range(HB):
                            m = pe.transpose(bank[4 + c][0:w, P * h:P * h + P], dec_in[:, h, P * c:P * c + w], ident)
                    m.then_inc(kdt_done, 1)
                if 2 <= t <= 4:
                    if t > 2:
                        pe.wait_ge(vt_copied, 2 * (t - 2))
                    to_tokens(v_sb, t - 2, vt_done)

            def outer(n, k_rows, v_rows):
                for h in range(HB):
                    m = pe.matmul(bank[4 + h // 2][:, DV * (h % 2):DV * (h % 2) + DV], k_rows[:, DK * h:DK * h + DK],
                                  v_rows[:, DV * h:DV * h + DV], start=True, stop=True)
                m.then_inc(kv_done, 1)

            for c, s in enumerate(range(S_VA, S_ZA)):
                step(s, xhi, xlo)
                if c == 0:
                    pe.wait_ge(kdt_copied, 2)
                    pe.wait_ge(kds_ready, 4)
                    pe.wait_ge(vt_copied, 6)
                else:
                    pe.wait_ge(st_ready, HB * c)
                r0, t = BLK * (c % 4), c // 4
                rows = slice(r0, r0 + BLK)
                outer(c, kd_t[rows, t, :], v_t[rows, t, :])
                if c >= 2:
                    pe.wait_ge(o_copied, c - 1)
                acc = bank[6 + c % 2]
                for i in range(KE):
                    m = pe.matmul(acc[:, BLK * i:BLK * i + BLK], v_t[rows, t, P * i:P * i + P],
                                  att[rows, t, i // 2, rows], start=i == 0, stop=False, skip_group_check=True)
                if c:
                    for i in range(KE):
                        h, half = i // 2, i % 2
                        m = pe.matmul(acc[:, BLK * i:BLK * i + BLK], st[:, c % 2, h, P * half:P * half + P],
                                      q_dec[:, h, BLK * c:BLK * c + BLK], start=False, stop=i == KE - 1,
                                      skip_group_check=True)
                m.then_inc(o_done, 1)

            for b, s in enumerate(range(S_ZA, S_U)):
                step(s, xhi, xlo)
                if b == 0:
                    pe.wait_ge(sq_ready, 2)
                    pe.wait_ge(o_copied, NBLK)
                    sum_partitions(bank[7][:, 0:T], v_sum[:, :]).then_inc(sum_done, 1)
                pe.wait_ge(st_ready, HB * (NBLK + b))
                r0 = BLK * (b // 4)
                rows = slice(r0, r0 + BLK)
                outer(NBLK + b, kd_s[rows, b % 4, :], v_ts[rows, :])
                if b == 0:
                    for i in range(KE):
                        pe.matmul(bank[6][:, DEC * i:DEC * i + DEC], v_ts[:, P * i:P * i + P], att_s[:, i // 2, :],
                                  start=i == 0, stop=False, skip_group_check=True)
                pe.wait_ge(s0_loaded[b % 4], 16 * (b // 4 + 1))
                for i in range(KE):
                    h, half = i // 2, i % 2
                    c0 = DEC * i + DEC_L * b
                    m = pe.matmul(bank[6][:, c0:c0 + DEC_L], s0[:, b % 4, h, P * half:P * half + P],
                                  q_dec[:, h, SEQ + DEC_L * b:SEQ + DEC_L * b + DEC_L], start=False, stop=False,
                                  skip_group_check=True)
                m.then_inc(o_done, 1)
                if 1 <= b <= 3:
                    if b == 1:
                        pe.wait_ge(va_normed, KE)
                    else:
                        pe.wait_ge(vat_copied, 2 * (b - 1))
                    to_tokens(va_sb, b - 1, vat_done)
                if b >= 4:
                    if b == 4:
                        pe.wait_ge(vat_copied, 6)
                        pe.wait_ge(ws_masked, 2)
                    else:
                        pe.wait_ge(sp_read, 4 * (b - 4))
                    for c in range(2):
                        i = 2 * (b - 4) + c
                        for t in range(2):
                            pe.matmul(bank[2 + c][:, P * t:P * t + P], va_t[:, t, P * i:P * i + P],
                                      wst[:, i // 2, :], start=True, stop=True)
                        m = pe.matmul(bank[2 + c][:, SEQ:T], va_ts[:, P * i:P * i + P], wsb[:, i // 2, :],
                                      start=True, stop=True)
                    m.then_inc(sp_done, 1)

            for j, s in enumerate(range(S_U, S_GATE)):
                step(s, xhi, xlo)
                if j == 0:
                    pe.wait_ge(sq_ready, 3)
                    pe.wait_ge(st_ready, HB * (NBLK + DEC_B))
                    for h in range(HB):
                        m = sum_partitions(bank[4 + h][:, 0:T], o_sum[:, h, :])
                    m.then_inc(sum_done, 1)

            with repeat(pe, KX // 2, {}) as i:
                for b in range(2):
                    for g in range(2):
                        step(S_GATE + 3 * b + g, xhi, xlo, i, 6)
                    s = S_GATE + 3 * b + 2
                    pe.wait_ge(y_split, 2 * KE)
                    pe.wait_ge(acc_read, 6 * i + (s - 1))
                    for half in range(2):
                        ready(2 * s + half, i, 12)
                        product(bank[2 + half][:, 0:T], 2 * (s % 2) + half, yhi[half], ylo[half], 0, True, True)
            step(S_WO, mhi, mlo, wait_k=m_split)
            step(S_WO + 1, mhi, mlo)
            with repeat(pe, KX // 2 - 1, {}) as i:
                for b in range(2):
                    step(S_WO + 2 + b, mhi, mlo, i)
            pe.wait_ge(p_split, 1)
            pe.wait_ge(acc_read, S_PE)
            for n, s in enumerate((S_PE, S_PE + 1)):
                for half in range(2):
                    if n == 1:
                        if half == 0:
                            pe.wait_ge(sq_ready, 4)
                            pe.wait_ge(pe_read, 4)
                            sum_partitions(bank[0][:, 0:T], sig[:, 0, :]).then_inc(sum_done, 1)
                            pe.wait_ge(pe_read, 8)
                        else:
                            pe.wait_ge(var_ready, 3 + HB)
                    q = 2 * (s % 2) + half
                    ready(2 * s + half)
                    for c in range(4):
                        acc = bank[(4 * half + 4 * n + c) % 8][:, 0:T]
                        for k in range(PLE // P):
                            h, l = whi[:, q, 2 * c + k, :], wlo[:, q, 2 * c + k, :]
                            pe.matmul(acc, h, p_hi[:, k, :], start=k == 0, stop=False)
                            pe.matmul(acc, h, p_lo[:, k, :], start=False, stop=False)
                            m = pe.matmul(acc, l, p_hi[:, k, :], start=False, stop=k == PLE // P - 1)
                    m.then_inc(units_used, 1)
            pe.wait_ge(pe_read, KX)
            step(S_PG, mhi, mlo, free=S_PE, wait_k=h_split)
            step(S_PG + 1, mhi, mlo, free=S_PE)
            with repeat(pe, KX // 2 - 1, {}) as i:
                for b in range(2):
                    step(S_PG + 2 + b, mhi, mlo, i, free=S_PE + 1 + b)


def columns():
    sizes = (EA, EA, EA, HB * DK, HB * DK, EB, EB, RANK, D, D)
    u, va, za, q, k, vb, zb, lr, ma, mb = np.cumsum((0,) + sizes[:-1]).tolist()
    order = [s + P * i for s, n in ((k, HB), (q, HB), (vb, KE), (zb, KE), (va, KE), (za, KE), (u, KE)) for i in range(n)]
    return order, lr, ma, mb


def constants():
    c = np.zeros((P, C_CONSTS), np.float32)
    c[:, C_ID:C_ID + P] = np.eye(P)
    c[:, C_ONE:C_ONE + P] = 1
    s, t = np.mgrid[0:P, 0:P]
    c[:, C_ATT:C_ATT + P] = (s // BLK == t // BLK) & (t >= s)
    s, t = np.mgrid[0:DEC, 0:DEC]
    c[:DEC, C_ATS:C_ATS + DEC] = (s // DEC_L == t // DEC_L) & (t >= s)
    s, n = np.mgrid[0:DEC, 0:4]
    c[:DEC, C_SEQ:C_SEQ + 4] = (s // DEC_L) % 4 == n
    c[:, C_RESET:C_RESET + T] = 1
    c[:, C_RESET:C_RESET + SEQ:BLK] = 0
    c[:, C_RESET + SEQ:C_RESET + T:DEC_L] = 0
    return c


def kernel(**inputs):
    import concourse.bacc as _bacc
    from concourse.bass_utils import run_bass_kernel_spmd as _run

    a = {n: np.asarray(v) for n, v in inputs.items()}
    f32 = np.float32

    def tokens_last(prompt, sample):
        x = np.concatenate([prompt.reshape(SEQ, -1), sample.reshape(DEC, -1)])
        return np.ascontiguousarray(x.reshape(T, -1, P).transpose(2, 1, 0))

    order, lr, ma, mb = columns()
    w_in, w_pa, w_pb, w_o, w_pg, w_pe = (a[n][0] for n in ("w_in", "w_pa", "w_pb", "w_o", "w_pg", "w_pe"))
    units = np.empty((UNITS, P, UK, P), f32)
    at = [0]

    def add(w, c):
        for k in range(0, w.shape[0], UK * P):
            units[at[0]] = w[k:k + UK * P, c:c + P].reshape(UK, P, P).transpose(1, 0, 2)
            at[0] += 1

    for c in order:
        add(w_in, c)
    for j in range(KX):
        add(w_in, ma + P * j)
        add(w_in, mb + P * j)
        add(w_pa, P * j)
        add(w_pb, P * j)
    for j in range(KX):
        add(w_o, P * j)
    for j in range(0, KX, 4):
        units[at[0]] = w_pe[:, P * j:P * (j + 4)].reshape(2, P, 4, P).transpose(1, 2, 0, 3).reshape(P, UK, P)
        at[0] += 1
    for j in range(KX):
        add(w_pg, P * j)
    assert at[0] == UNITS

    params = np.concatenate([a[n][0].reshape(-1, P).T for n in ("g_pre", "g_v", "g_o", "b_a", "g_post")], axis=1)
    w_s = a["w_s"][0]
    w_s_dec = np.zeros((DEC, HA, DEC), f32)
    for b in range(DEC_B):
        r = slice(DEC_L * b, DEC_L * (b + 1))
        w_s_dec[r, :, r] = w_s[:, :DEC_L, :DEC_L].transpose(2, 0, 1)
    arrays = {
        "x_t": tokens_last(a["x_prompt"], a["x_sample"]),
        "p_t": tokens_last(a["p_prompt"][0], a["p_sample"][0]),
        "w_units": units,
        "w_alr": np.ascontiguousarray(w_in[:, lr:lr + RANK].reshape(KX, P, RANK).transpose(1, 0, 2)),
        "params": np.ascontiguousarray(params),
        "consts": constants(),
        "w_s_t": np.ascontiguousarray(w_s.transpose(2, 0, 1)),
        "w_s_dec": w_s_dec,
        "b_s_rows": np.ascontiguousarray(np.broadcast_to(a["b_s"][0][None], (P, HA, CHUNK))),
        "w_a2": np.ascontiguousarray(a["w_a2"][0]),
        "s0": np.ascontiguousarray(a["state_gla"][0]),
    }
    outs = {"y": (P, KX, T), "st_prompt": (HB, DK, DV), "st_dec": (DEC_B, HB, DK, DV), "cv": (KE, P, DEC)}

    nc = _bacc.Bacc("TRN2", target_bir_lowering=False, num_devices=1)
    A = {n: nc.dram_tensor(f"in_{n}", v.shape, F32, kind="ExternalInput").ap() for n, v in arrays.items()}
    O = {n: nc.dram_tensor(f"out_{n}", s, F32, kind="ExternalOutput").ap() for n, s in outs.items()}
    build(nc, A, O)
    got = _run(nc, [{f"in_{n}": v for n, v in arrays.items()}], core_ids=[0]).results[0]
    y = got["out_y"].transpose(2, 1, 0).reshape(T, D)
    return (
        y[:SEQ].reshape(1, SEQ, D),
        y[SEQ:].reshape(DEC_B, DEC_L, D),
        got["out_st_prompt"][None, None],
        got["out_st_dec"][None],
        got["out_cv"].transpose(2, 0, 1).reshape(1, DEC_B, DEC_L, EA),
    )
```

```python
from contextlib import ExitStack, contextmanager

import concourse.bass as bass
import numpy as np
from concourse import mybir

F32, F32R, I32 = mybir.dt.float32, mybir.dt.float32r, mybir.dt.int32
ACT = mybir.ActivationFunctionType
ALU = mybir.AluOpType

P = 128
D = 2048
SEQ, CHUNK = 256, 128
DEC_B, DEC_L = 8, 8
DEC = DEC_B * DEC_L
T = SEQ + DEC
EA = EB = D // 2
HA, HB = 4, 4
DV, DK = EB // HB, EB // HB // 2
RANK, TAU, EPS = 16, 16.0, 1e-6
PLE = 256
KX = D // P
KE = EA // P
UK = 8
BLK = 32
NBLK = SEQ // BLK
MID = BLK // 2 - 1
GRP = 4

S_K = 0
S_Q = S_K + HB
S_V = S_Q + HB
S_ZB = S_V + KE
S_VA = S_ZB + KE
S_ZA = S_VA + KE
S_U = S_ZA + KE
S_GATE = S_U + KE
S_WO = S_GATE + 3 * KX
S_PE = S_WO + KX
S_PG = S_PE + 2
STEPS = S_PG + KX
UNITS = 2 * STEPS

C_GPRE, C_GV, C_GO, C_BA, C_GPOST, C_PARAMS = 0, KX, KX + KE, KX + 2 * KE, KX + 2 * KE + HB, 2 * KX + 2 * KE + HB
C_ID, C_ONE, C_ATT, C_ATS, C_RESET, C_CONSTS = 0, P, 2 * P, 3 * P, 3 * P + DEC, 3 * P + DEC + T


class Tally:

    def __init__(self, sem):
        self.sem, self.base, self.k = sem, 0, 0

    @property
    def value(self):
        return self.base + self.k

    def up(self, ins):
        ins.then_inc(self.sem, 1)
        self.k += 1

    def next(self, eng, n=1):
        self.k += n
        eng.wait_ge(self.sem, self.value)


@contextmanager
def repeat(eng, n, per):
    starts = {t: t.value for t in per}
    with eng.Fori(0, n) as i:
        for t, by in per.items():
            t.base, t.k = starts[t] + by * i, 0
        yield i
        for t, by in per.items():
            assert t.k == by, (t.sem, t.k, by)
    for t, by in per.items():
        t.base, t.k = starts[t] + by * n, 0


def build(nc, A, O):
    ctx = ExitStack()
    with ctx:
        XC = 8
        XB = KX // XC

        def sem(name):
            return ctx.enter_context(nc.semaphore(name))

        KB = 1024
        start = -(-nc.sbuf_base // 64) * 64
        SMALL = 19 * KB + 256
        total = 188 * KB + SMALL
        ctx.enter_context(nc.sbuf_tensor("arena", [P, (total + start - nc.sbuf_base + 3) // 4 + 1], F32))

        def at(name, off, shape, dtype=F32):
            assert off + int(np.prod(shape[1:])) * 4 <= total, name
            return nc.alloc_sbuf_tensor_at(name, shape, dtype, offset=start + off)

        W0, XG0, M0, Y0, X0, C0 = 0, 48 * KB, 88 * KB, 128 * KB, 168 * KB, 188 * KB
        TB = T * 4

        raw = at("w_raw", W0, [P, 4, UK, P])
        whi = at("w_hi", W0 + 16 * KB, [P, 4, UK, P], F32R)
        wlo = at("w_lo", W0 + 32 * KB, [P, 4, UK, P], F32R)
        xhi = at("x_hi", XG0, [P, KX, T], F32R)
        xlo = at("x_lo", XG0 + 20 * KB, [P, KX, T], F32R)
        p_raw = at("p_raw", XG0, [P, PLE // P, T])
        p_hi = at("p_hi", XG0 + 2 * TB, [P, PLE // P, T], F32R)
        p_lo = at("p_lo", XG0 + 4 * TB, [P, PLE // P, T], F32R)
        pe_out = at("pe_out", XG0 + 20 * KB, [P, KX, T])
        slot = HB * TB
        squares = at("squares", M0 + 2 * slot, [P, KX, T])
        k_dec = at("k_dec", M0, [P, HB, T])
        cum = at("decay_cum", M0 + slot, [P, HB, T])
        k_64 = at("k_64", M0 + slot, [P, HB, 2, 64])
        k_128 = at("k_128", M0 + slot + 2 * KB, [P, HB, P])
        q_sb = at("q", M0 + 2 * slot, [P, HB, T])
        k_256 = at("k_256", M0 + 2 * slot, [P, HB, SEQ])
        k_sb = at("k", M0 + 3 * slot, [P, HB, T])
        q_mid = at("q_mid", M0 + 4 * slot, [P, HB, T])
        k_mid = at("k_mid", M0 + 5 * slot, [P, HB, T])
        q_dec = at("q_dec", M0 + 6 * slot, [P, HB, T])
        wa2 = at("w_a2_sb", M0 + 7 * slot, [RANK, HB * DK])
        alr = at("a_lr", M0 + 7 * slot + 2 * KB, [RANK, T])
        q_64 = at("q_64", M0 + 7 * slot, [P, HB, 2, 64])
        q_128 = at("q_128", M0 + 7 * slot + 2 * KB, [P, HB, P])
        v_x = at("v_stacked", M0 + 4 * slot, [P, KE, DEC_B, 4, DEC_L])
        k_x = at("k_stacked", M0 + slot, [P, HB, DEC_B, 4, DEC_L])
        o_sb = at("o", M0 + 2 * slot, [P, KE, T])
        za_gate = at("za_gate", M0, [P, KE, T])
        va_t = at("va_tokens", M0 + 4 * slot, [P, 2, EA])
        va_ts = at("va_tokens_dec", M0 + 7 * slot, [DEC, EA])
        v_sq = at("v_sq", M0 + 5 * slot, [P, T])
        v_sum = at("v_sum", M0 + 5 * slot + TB, [P, T])
        r_o = at("r_o", M0 + 6 * slot, [P, HB, T])
        mhi = at("m_hi", M0, [P, KX, T], F32R)
        mlo = at("m_lo", M0 + 20 * KB, [P, KX, T], F32R)
        vx_t = at("v_stacked_rows", Y0, [P, 2, EB], F32R)
        kx_t = at("k_stacked_rows", Y0 + 8 * KB, [P, 2, HB * DK], F32R)
        v_ts = at("v_tokens_dec", Y0 + 12 * KB, [DEC, EB])
        att_s = at("att_dec", Y0 + 16 * KB, [DEC, HB, DEC])
        st = at("state", Y0 + 17 * KB, [P, HB, DV])
        v_t = at("v_tokens", Y0 + 21 * KB, [P, 2, EB])
        kd_t = at("kd_tokens", Y0 + 29 * KB, [P, 2, HB * DK])
        att0 = at("att0", Y0 + 33 * KB, [P, HB, SEQ])
        att1 = at("att1", Y0 + 37 * KB, [P, HB, P])
        wr_raw = at("w_alr_raw", Y0 + 25 * KB, [P, KX, RANK])
        wr_hi = at("w_alr_hi", Y0 + 26 * KB, [P, KX, RANK], F32R)
        wr_lo = at("w_alr_lo", Y0 + 27 * KB, [P, KX, RANK], F32R)
        s0 = at("state_dec", Y0 + 24 * KB, [P, 4, HB, DV])
        o_sq = at("o_sq", Y0, [P, HB, 2, T])
        o_sum = at("o_sum", Y0 + 10 * KB, [P, HB, T])
        yhi = [at(n, Y0 + o * KB, [P, KE, T], F32R) for n, o in (("ya_hi", 0), ("yb_hi", 20))]
        ylo = [at(n, Y0 + o * KB, [P, KE, T], F32R) for n, o in (("ya_lo", 10), ("yb_lo", 30))]
        h_sb = at("h", Y0, [P, KX, T])
        x_sb = at("x_sb", X0, [P, KX, T])
        v_sb = at("v_b", X0, [P, KE, T])
        va_sb = at("v_a", X0, [P, KE, T])
        sp_sb = at("spatial", X0, [P, KE, T])
        zb_gate = at("zb_gate", X0 + 10 * KB, [P, KE, T])
        mo_sb = at("mo", X0, [P, KX, T])
        off = C0
        small = {}
        for name, shape in (("params", [P, C_PARAMS]), ("consts", [P, C_CONSTS]), ("w_s_t", [P, HA, CHUNK]),
                            ("w_s_dec", [DEC, HA, DEC]), ("b_s_sb", [P, HA, CHUNK]), ("decays", [P, HB, 2 * NBLK + 8]),
                            ("r_tok", [P, T]), ("tmp", [P, 4, T]), ("sig", [P, 2, T]), ("warm", [P, 8])):
            small[name] = at(name, off, shape)
            off += -(-int(np.prod(shape[1:])) * 4 // 32) * 32
        par, con, wst, wsb, bs = (small[n] for n in ("params", "consts", "w_s_t", "w_s_dec", "b_s_sb"))
        decays, r_tok, tmp, sig = (small[n] for n in ("decays", "r_tok", "tmp", "sig"))
        ident, ones = con[:, C_ID:C_ID + P], con[:, C_ONE:C_ONE + P]

        def col(c, i):
            return par[:, c + i:c + i + 1]

        bank = [ctx.enter_context(nc.psum_tensor(f"bank{b}", [P, 512], F32)) for b in range(8)]

        VT_BANKS = ((6, 7), (2, 3), (6, 7))
        OP_BANKS = ((6, 7), (2, 3))
        PE_BANKS = ((4, 5, 6, 7), (2, 3, 0, 1), (4, 5, 6, 7), (2, 3, 0, 1))
        D64, D128, DDEC = NBLK, NBLK + 4, NBLK + 5
        PG_BANKS = (6, 7)
        NORM_BANK = 3
        H_WITH = (0, 2, 6, 10, KX)

        x_loaded = [sem(f"x_loaded{c}") for c in range(XC)]
        par_loaded, consts_loaded, alrw_loaded = sem("par_loaded"), sem("consts_loaded"), sem("alrw_loaded")
        raw_loaded = [sem(f"raw_loaded{q}") for q in range(4)]
        hi_ready = sem("hi_ready")
        lo_ready = sem("lo_ready")
        units_used = sem("units_used")
        acc_read = sem("acc_read")
        alr_hi, alr_lo = sem("alr_hi"), sem("alr_lo")
        x_rounded, x_split = sem("x_rounded"), sem("x_split")
        alr_done, alr_ready = sem("alr_done"), sem("alr_ready")
        squared = sem("squared")
        sq_ready = sem("sq_ready")
        sum_done = sem("sum_done")
        var_ready = sem("var_ready")
        r_ready = sem("r_ready")
        logits_done = sem("logits_done")
        absneg_ready, softplus_ready = sem("absneg_ready"), sem("softplus_ready")
        spans_ready, exps_ready = sem("spans_ready"), sem("exps_ready")
        decays_kept, gla_in = sem("decays_kept"), sem("gla_in")
        att_zeroed, att_done, att_masked = sem("att_zeroed"), sem("att_done"), sem("att_masked")
        att_copied = sem("att_copied")
        kdt_done, kdt_copied = sem("kdt_done"), sem("kdt_copied")
        vt_done, vt_copied = sem("vt_done"), sem("vt_copied")
        x_hi_parts, x_lo_parts = sem("stacked_rounded"), sem("stacked_split")
        xt_done, xt_copied = sem("stacked_transposed"), sem("stacked_copied")
        ps_done, ps_copied = sem("prompt_state_done"), sem("prompt_state_copied")
        op_done, op_copied = sem("o_prompt_done"), sem("o_prompt_copied")
        kv_done, st_ready = sem("kv_done"), sem("st_ready")
        o_done, o_copied = sem("o_done"), sem("o_copied")
        ws_masked = sem("ws_masked")
        va_normed, vat_done, vat_copied = sem("va_normed"), sem("vat_done"), sem("vat_copied")
        sp_done, sp_read = sem("sp_done"), sem("sp_read")
        s0_loaded = [sem(f"s0_loaded{q}") for q in range(4)]
        s0_stored = [sem(f"s0_stored{q}") for q in range(4)]
        st_stored, cv_stored = sem("st_stored"), sem("cv_stored")
        sig_done = sem("sig_done")
        y_full, y_rounded, y_split = sem("y_full"), sem("y_rounded"), sem("y_split")
        m_full, m_rounded, m_split = sem("m_full"), sem("m_rounded"), sem("m_split")
        p_loaded, p_rounded, p_split = sem("p_loaded"), sem("p_rounded"), sem("p_split")
        xr_loaded = [sem(f"xr_loaded{c}") for c in range(4)]
        pe_read = sem("pe_read")
        sum_last, hn_ready, h_full, h_rounded, h_split = sem("sum_last"), sem("hn_ready"), sem("h_full"), sem("h_rounded"), sem("h_split")
        out_ready, out_stored = sem("out_ready"), sem("out_stored")
        dve_own, act_own, pool_own = sem("dve_own"), sem("act_own"), sem("pool_own")

        block = ctx.enter_context(nc.Block())

        @block.sync
        def _(sp):
            def load_x(c):
                sp.dma_start(x_sb[:, XB * c:XB * c + XB, :], A["x_t"][:, XB * c:XB * c + XB, :])\
                  .then_inc(x_loaded[c], 16)

            def load_unit(q):
                sp.dma_start(raw[:, q], A["w_units"][q]).then_inc(raw_loaded[q], 16)

            for half in range(2):
                for c in range(XC // 2):
                    load_x(XC // 2 * half + c)
                load_unit(2 * half)
                load_unit(2 * half + 1)
            with sp.Fori(1, UNITS // 4) as i:
                for q in range(4):
                    sp.wait_ge(lo_ready, 4 * i + (q - 3))
                    sp.dma_start(raw[:, q], A["w_units"][4 * i + q]).then_inc(raw_loaded[q], 16)

        @block.scalar
        def _(act):
            sig_t, m_full_t, out_t = Tally(sig_done), Tally(m_full), Tally(out_ready)
            y_full_t = Tally(y_full)

            def copy_o_prompt(n):
                act.wait_ge(op_done, n + 1)
                for c in range(2):
                    i = 4 * n + 2 * c
                    act.activation(o_sb[:, i:i + 2, 0:SEQ],
                                   bank[OP_BANKS[n][c]][:, :].rearrange("p (i t) -> p i t", i=2), ACT.Copy)\
                       .then_inc(op_copied, 1)

            def split_hi(s, i=None):
                for half in range(2):
                    q = 2 * (s % 2) + half
                    turn = 16 * ((s + 2) // 2 + 1)
                    used = 2 * (s + 2) + half - 3
                    act.wait_ge(raw_loaded[q], turn if i is None else 16 * i + turn)
                    act.wait_ge(units_used, used if i is None else 4 * i + used)
                    act.activation(whi[:, q], raw[:, q], ACT.Copy).then_inc(hi_ready, 1)

            act.dma_start(par[:, :], A["params"]).then_inc(par_loaded, 16)
            act.dma_start(wr_raw[:], A["w_alr"]).then_inc(alrw_loaded, 16)
            act.wait_ge(alrw_loaded, 16)
            act.activation(wr_hi[:], wr_raw[:], ACT.Copy).then_inc(alr_hi, 1)
            act.wait_ge(par_loaded, 16)
            for k in range(KX):
                if k % XB == 0:
                    act.wait_ge(x_loaded[k // XB], 16)
                act.activation(xhi[:, k, :], x_sb[:, k, :], ACT.Copy, scale=col(C_GPRE, k)).then_inc(x_rounded, 1)
                if k % 8 == 7:
                    for q in (k // 8 * 2, k // 8 * 2 + 1):
                        act.wait_ge(raw_loaded[q], 16)
                        act.activation(whi[:, q], raw[:, q], ACT.Copy).then_inc(hi_ready, 1)
                    if k == 7:
                        for dst, name in ((con, "consts"), (wst, "w_s_t"), (wsb, "w_s_dec"), (bs, "b_s_rows")):
                            act.dma_start(dst[:], A[name]).then_inc(consts_loaded, 16)
                        act.dma_start(wa2[:, :], A["w_a2"]).then_inc(consts_loaded, 16)
                    act.activation(squares[:, k - 7:k + 1, :], x_sb[:, k - 7:k + 1, :], ACT.Square)\
                       .then_inc(squared, 1)

            def root(n, out, x):
                act.wait_ge(var_ready, n)
                act.activation(out, x, ACT.Sqrt).then_inc(r_ready, 1)

            for s in range(S_K, S_V):
                split_hi(s)
                if s == S_K:
                    root(1, r_tok[:, :], tmp[:, 0, :])
                if s == S_Q:
                    act.wait_ge(absneg_ready, 1)
                    act.activation(cum[:], cum[:], ACT.Exp).then_inc(act_own, 1)
                    act.wait_ge(act_own, 1)
                    act.activation(cum[:], cum[:], ACT.Ln, bias=1.0).then_inc(softplus_ready, 1)
            act.wait_ge(spans_ready, 4)
            act.activation(q_dec[:], cum[:], ACT.Exp, scale=1 / TAU).then_inc(exps_ready, 1)
            act.activation(k_mid[:], q_mid[:], ACT.Exp, scale=-1 / TAU).then_inc(exps_ready, 1)
            act.wait_ge(exps_ready, 2)
            act.activation(q_mid[:], q_mid[:], ACT.Exp, scale=1 / TAU).then_inc(exps_ready, 1)
            act.activation(k_dec[:], k_dec[:], ACT.Exp, scale=1 / TAU).then_inc(exps_ready, 1)
            with repeat(act, KE // 2, {}) as i:
                for b in range(2):
                    split_hi(S_V + b, i)

            def sigmoid(s):
                act.wait_ge(acc_read, s + 1)
                sig_t.up(act.activation(sig[:, 0, :], tmp[:, 0, :], ACT.Sigmoid))

            def copy_banks(dst, banks, rows, done):
                for c, b in enumerate(banks):
                    act.activation(dst[:, 512 * c:512 * c + 512], bank[b][0:rows, :], ACT.Copy).then_inc(done, 1)

            for t, s in enumerate(range(S_ZB, S_VA)):
                split_hi(s)
                sigmoid(s)
                if t == 0:
                    act.wait_ge(att_done, 1)
                    act.wait_ge(att_masked, 3)
                    for sub in range(2):
                        r0, r1 = 2 * BLK * sub, 2 * BLK * sub + BLK
                        part = bank[6][:, :].rearrange("p (c h t) -> p c h t", c=2, h=HB)
                        for c, dst in enumerate((att0, att1)):
                            act.activation(dst[r0:r1, :, r1:r1 + BLK], part[r0:r1, c, :, BLK * sub:BLK * sub + BLK],
                                           ACT.Copy).then_inc(att_copied, 1)
                    part = bank[7][:, :].rearrange("p (c h t) -> p c h t", c=2, h=HB)
                    for c, dst in enumerate((att0, att1)):
                        act.activation(dst[0:64, :, 64:P], part[0:64, c, :, :], ACT.Copy).then_inc(att_copied, 1)
                    act.activation(att0[:, :, P:SEQ], bank[2][:, :].rearrange("p (h t) -> p h t", h=HB), ACT.Copy)\
                       .then_inc(att_copied, 1)
                if t == 1:
                    v_new = v_sb[:, :, SEQ:T].rearrange("p i (b t) -> p i b t", t=DEC_L)
                    k_new = k_dec[:, :, SEQ:T].rearrange("p i (b t) -> p i b t", t=DEC_L)
                    for n in (0, 2):
                        act.activation(v_x[:, :, :, n, :].bitcast(F32R), v_new, ACT.Copy).then_inc(x_hi_parts, 1)
                    for n in (0, 1):
                        act.activation(k_x[:, :, :, n, :].bitcast(F32R), k_new, ACT.Copy).then_inc(x_hi_parts, 1)
                    act.wait_ge(kdt_done, 1)
                    copy_banks(kd_t[:].rearrange("p c n -> p (c n)"), (4, 5), P, kdt_copied)
                if 2 <= t <= 4:
                    act.wait_ge(vt_done, t - 1)
                    copy_banks(*((v_t[:, t - 2, :], VT_BANKS[t - 2], P) if t < 4 else (v_ts[:, :], VT_BANKS[2], DEC)),
                               vt_copied)
                if t == 5:
                    act.wait_ge(xt_done, 1)
                    copy_banks(vx_t[:].rearrange("p g n -> p (g n)"), (4, 5, 6, 7), P, xt_copied)
                if t == 6:
                    act.wait_ge(xt_done, 2)
                    copy_banks(kx_t[:].rearrange("p g n -> p (g n)"), (2, 3), P, xt_copied)
                    act.wait_ge(ps_done, 1)
                    copy_banks(st[:].rearrange("p h n -> p (h n)"), (4, 5), P, ps_copied)
                    act.wait_ge(ps_copied, 2)
                    act.dma_start(O["st_prompt"].rearrange("h d v -> d h v"), st[:]).then_inc(st_stored, 16)
                if t == 7:
                    copy_o_prompt(0)

            def load_s0(b):
                act.dma_start(s0[:, b % 4], A["s0"][b].rearrange("h d v -> d h v")).then_inc(s0_loaded[b % 4], 16)

            def finish(b):
                act.wait_ge(st_ready, HB * (b + 1))
                act.dma_start(O["st_dec"][b].rearrange("h d v -> d h v"), s0[:, b % 4]).then_inc(s0_stored[b % 4], 16)

            for c, s in enumerate(range(S_VA, S_ZA)):
                split_hi(s)
                if c == 0:
                    copy_o_prompt(1)
                    for b in range(4):
                        load_s0(b)
                if c >= 2:
                    finish(c - 2)
                if 3 <= c < 7:
                    act.wait_ge(s0_stored[c - 3], 16)
                    load_s0(c + 1)

            for b, s in enumerate(range(S_ZA, S_U)):
                split_hi(s)
                if b == 0:
                    root(2, tmp[:, 1, :], tmp[:, 1, :])
                sigmoid(s)
                if b == 0:
                    finish(6)
                    act.wait_ge(o_done, DEC_B)
                    act.activation(o_sb[:, :, SEQ:T], bank[6][:, :].rearrange("p (i t) -> p i t", t=DEC),
                                   ACT.Copy).then_inc(o_copied, 1)
                if b == 1:
                    finish(7)
                    act.wait_ge(va_normed, KE)
                    act.dma_start(O["cv"].rearrange("i p t -> p i t"), va_sb[:, :, SEQ:T]).then_inc(cv_stored, 16)
                if 1 <= b <= 3:
                    act.wait_ge(vat_done, b)
                    copy_banks(*((va_t[:, b - 1, :], (2, 3), P) if b < 3 else (va_ts[:, :], (2, 3), DEC)), vat_copied)
                if b == 5:
                    root(2 + HB, r_o[:], r_o[:])

            act.wait_ge(st_stored, 16)
            for q in range(4):
                act.wait_ge(s0_stored[q], 32)
            for j, s in enumerate(range(S_U, S_GATE)):
                split_hi(s)
                for br in range(2):
                    y_full_t.next(act)
                    act.activation(yhi[br][:, j, :], tmp[:, 2 + br, :], ACT.Copy).then_inc(y_rounded, 1)

            with repeat(act, KX // 2, {sig_t: 4, m_full_t: 2}) as i:
                for b in range(2):
                    for g in range(3):
                        n = 3 * b + g
                        for half in range(2):
                            q = 2 * (n % 2) + half
                            turn = 16 * ((S_GATE + n + 2) // 2 + 1)
                            used = 2 * (S_GATE + n + 2) + half - 3
                            act.wait_ge(raw_loaded[q], 48 * i + turn)
                            act.wait_ge(units_used, 12 * i + used)
                            act.activation(whi[:, q], raw[:, q], ACT.Copy).then_inc(hi_ready, 1)
                        if g < 2:
                            act.wait_ge(acc_read, 6 * i + (S_GATE + n + 1))
                            sig_t.up(act.activation(sig[:, g, :], tmp[:, g, :], ACT.Sigmoid))
                        else:
                            m_full_t.next(act)
                            act.activation(mhi[:, 2 * i + b, :], tmp[:, 2, :], ACT.Copy).then_inc(m_rounded, 1)

            act.wait_ge(units_used, 2 * S_WO)
            act.dma_start(p_raw[:], A["p_t"]).then_inc(p_loaded, 16)
            for c in range(4):
                act.dma_start(h_sb[:, 4 * c:4 * c + 4, :], A["x_t"][:, 4 * c:4 * c + 4, :]).then_inc(xr_loaded[c], 16)
            for b in range(2):
                split_hi(S_WO + b)
            act.wait_ge(p_loaded, 16)
            act.activation(p_hi[:], p_raw[:], ACT.Copy).then_inc(p_rounded, 1)
            with repeat(act, KX // 2 - 1, {}) as i:
                for b in range(2):
                    split_hi(S_WO + 2 + b, i)
            act.activation(small["warm"][0:1, 0:1], par[0:1, 0:1], ACT.Sqrt, scale=0.0).then_inc(act_own, 1)
            root(3 + HB, r_tok[:, :], r_tok[:, :])
            for n in range(4):
                act.wait_ge(units_used, 2 * S_PE + n + 1)
                for c in range(4):
                    act.activation(pe_out[:, 4 * n + c, :], bank[PE_BANKS[n][c]][:, 0:T], ACT.Copy).then_inc(pe_read, 1)
                act.wait_ge(raw_loaded[n], 16 * (S_PG // 2 + 1))
                act.activation(whi[:, n], raw[:, n], ACT.Copy).then_inc(hi_ready, 1)
                for k in range(H_WITH[n], H_WITH[n + 1]):
                    act.wait_ge(h_full, k + 1)
                    act.activation(mhi[:, k, :], h_sb[:, k, :], ACT.Copy).then_inc(h_rounded, 1)

            def last_gate(s, b, i=None, used=None, at_=None):
                used = used or 2 * s + 2
                act.wait_ge(units_used, used if i is None else 4 * i + used)
                sig_t.up(act.activation(sig[:, b, :], bank[at_ or b][:, 0:T], ACT.Sigmoid))

            def store(j):
                out_t.next(act)
                act.dma_start(O["y"][:, j, :], pe_out[:, j, :]).then_inc(out_stored, 16)

            for j in range(2):
                split_hi(S_PG + j)
                last_gate(S_PG + j, j, used=2 * S_PG + 3 + j, at_=PG_BANKS[j])
            with repeat(act, KX // 2 - 2, {sig_t: 2, out_t: 2}) as i:
                for b in range(2):
                    split_hi(S_PG + 2 + b, i)
                    last_gate(S_PG + 2 + b, b, i)
                    store(2 * i + b)
            for j in range(KX - 2, KX):
                last_gate(S_PG + j, j % 2)
                store(j - 2)
            store(KX - 2)
            store(KX - 1)
            act.wait_ge(out_stored, 16 * KX)
            act.wait_ge(cv_stored, 16)

        @block.vector
        def _(dve):
            own = Tally(dve_own)
            sig_t, acc_t = Tally(sig_done), Tally(acc_read)
            y_full_t, y_round_t = Tally(y_full), Tally(y_rounded)
            m_full_t, m_round_t = Tally(m_full), Tally(m_rounded)
            out_t = Tally(out_ready)
            st_t = Tally(st_ready)

            def then(ins):
                own.up(ins)
                dve.wait_ge(dve_own, own.value)

            def low(q, ready, used):
                dve.wait_ge(hi_ready, ready)
                dve.wait_ge(units_used, used)
                dve.tensor_tensor(wlo[:, q], raw[:, q], whi[:, q].bitcast(F32), ALU.subtract).then_inc(lo_ready, 1)

            def split_lo(s, i=None):
                for half in range(2):
                    u = 2 * (s + 2) + half
                    low(2 * (s % 2) + half, *((u + 1, u - 3) if i is None else (4 * i + (u + 1), 4 * i + (u - 3))))

            def sums(s, i=None, by=4):
                dve.wait_ge(units_used, 2 * s + 2 if i is None else by * i + (2 * s + 2))

            def variance(out, src, n):
                then(dve.tensor_scalar(out, src, 1.0 / n, EPS, ALU.mult, ALU.add))
                dve.reciprocal(out, out).then_inc(var_ready, 1)

            dve.wait_ge(par_loaded, 16)
            dve.wait_ge(alr_hi, 1)
            dve.tensor_tensor(wr_lo[:], wr_raw[:], wr_hi[:].bitcast(F32), ALU.subtract).then_inc(alr_lo, 1)
            for k in range(KX):
                dve.wait_ge(x_rounded, k + 1)
                dve.scalar_tensor_tensor(xlo[:, k, :], x_sb[:, k, :], col(C_GPRE, k), xhi[:, k, :].bitcast(F32),
                                         ALU.mult, ALU.subtract).then_inc(x_split, 1)
                if k % 8 == 7:
                    for q in (k // 8 * 2, k // 8 * 2 + 1):
                        dve.wait_ge(hi_ready, q + 1)
                        dve.tensor_tensor(wlo[:, q], raw[:, q], whi[:, q].bitcast(F32), ALU.subtract)\
                           .then_inc(lo_ready, 1)
            dve.wait_ge(consts_loaded, 16 * 5)

            r = r_tok[:, :]
            for s in range(S_K, S_V):
                split_lo(s)
                if s == S_K:
                    dve.wait_ge(sum_done, 1)
                    variance(tmp[:, 0, :], bank[5][:, 0:T], D)
                    dve.wait_ge(r_ready, 1)
                    dve.wait_ge(units_used, 4)
                else:
                    sums(s)
                if s < S_Q:
                    acc_t.up(dve.tensor_tensor(k_sb[:, s - S_K, :], bank[s % 4][:, 0:T], r, ALU.mult))
                else:
                    acc_t.up(dve.scalar_tensor_tensor(q_sb[:, s - S_Q, :], bank[s % 2][:, 0:T], float(DK) ** -0.5, r,
                                                      ALU.mult, ALU.mult))
                if s == S_K:
                    dve.wait_ge(alr_done, 1)
                    dve.tensor_tensor(alr[:, :], bank[4][0:RANK, 0:T], r_tok[0:RANK, :], ALU.mult)\
                       .then_inc(alr_ready, 1)
                if s == S_K + 3:
                    dve.wait_ge(logits_done, 1)
                    for h in range(HB):
                        own.up(dve.tensor_scalar(k_dec[:, h, :], bank[4 + h][:, 0:T], col(C_BA, h), None, ALU.add))
                    dve.wait_ge(dve_own, own.value)
                    dve.scalar_tensor_tensor(cum[:], k_dec[:], -1.0, k_dec[:], ALU.mult, ALU.min)\
                       .then_inc(absneg_ready, 1)
                if s == S_Q + 1:
                    dve.wait_ge(softplus_ready, 1)
                    then(dve.scalar_tensor_tensor(k_dec[:], k_dec[:], 0.0, cum[:], ALU.min, ALU.subtract))
                    for h in range(HB):
                        own.up(dve.tensor_tensor_scan(cum[:, h, :], con[:, C_RESET:C_RESET + T], k_dec[:, h, :], 0.0,
                                                      ALU.mult, ALU.add))
                    dve.wait_ge(dve_own, own.value)
                if s == S_Q + 2:
                    prompt = [x[:, :, 0:SEQ].rearrange("p h (c t) -> p h c t", t=BLK) for x in (cum, q_mid, k_dec)]
                    dec = [x[:, :, SEQ:T].rearrange("p h (c t) -> p h c t", t=DEC_L) for x in (cum, k_dec)]
                    mid = prompt[0][:, :, :, MID:MID + 1].to_broadcast([P, HB, NBLK, BLK])
                    end = prompt[0][:, :, :, BLK - 1:BLK].to_broadcast([P, HB, NBLK, BLK])
                    end_d = dec[0][:, :, :, DEC_L - 1:DEC_L].to_broadcast([P, HB, DEC_B, DEC_L])
                    dve.tensor_tensor(prompt[1], prompt[0], mid, ALU.subtract).then_inc(spans_ready, 1)
                    dve.tensor_copy(q_mid[:, :, SEQ:T], cum[:, :, SEQ:T]).then_inc(spans_ready, 1)
                    dve.tensor_tensor(prompt[2], end, prompt[0], ALU.subtract).then_inc(spans_ready, 1)
                    dve.tensor_tensor(dec[1], end_d, dec[0], ALU.subtract).then_inc(spans_ready, 1)
            dve.wait_ge(exps_ready, 4)
            ends = q_dec[:, :, 0:SEQ].rearrange("p h (c t) -> p h c t", t=BLK)[:, :, :, BLK - 1]
            ends_d = q_dec[:, :, SEQ:T].rearrange("p h (c t) -> p h c t", t=DEC_L)[:, :, :, DEC_L - 1]
            then(dve.tensor_copy(decays[:, :, 0:NBLK], ends))
            then(dve.tensor_tensor(decays[:, :, D64:D64 + 4], decays[:, :, 0:NBLK:2], decays[:, :, 1:NBLK:2], ALU.mult))
            dve.tensor_tensor(decays[:, :, D128:D128 + 1], decays[:, :, D64 + 2:D64 + 3],
                              decays[:, :, D64 + 3:D64 + 4], ALU.mult).then_inc(decays_kept, 1)
            dve.tensor_copy(decays[:, :, DDEC:DDEC + DEC_B], ends_d).then_inc(decays_kept, 1)
            with repeat(dve, KE // 2, {acc_t: 2}) as i:
                for b in range(2):
                    split_lo(S_V + b, i)
                    sums(S_V + b, i)
                    acc_t.up(dve.tensor_tensor(v_sb[:, 2 * i + b, :], bank[b][:, 0:T], r, ALU.mult))

            def silu(s, out):
                sums(s)
                acc_t.up(dve.tensor_tensor(tmp[:, 0, :], bank[s % 2][:, 0:T], r, ALU.mult))
                sig_t.next(dve)
                then(dve.tensor_tensor(out, tmp[:, 0, :], sig[:, 0, :], ALU.mult))

            for t, s in enumerate(range(S_ZB, S_VA)):
                split_lo(s)
                silu(s, zb_gate[:, t, :])
                if t == 0:
                    dve.wait_ge(att_zeroed, 3)
                    dve.wait_ge(att_done, 1)
                    mask = con[:, C_ATT:C_ATT + P].bitcast(I32)
                    for c, dst in enumerate((att0, att1)):
                        for h in range(HB):
                            last = dve.copy_predicated(dst[:, h, 0:P], mask, bank[4 + c][:, P * h:P * h + P])
                        last.then_inc(att_masked, 1)
                    mask = con[0:DEC, C_ATS:C_ATS + DEC].bitcast(I32)
                    for h in range(HB):
                        last = dve.copy_predicated(att_s[:, h, :], mask, bank[3][0:DEC, DEC * h:DEC * h + DEC])
                    last.then_inc(att_masked, 1)
                if t == 1:
                    dve.wait_ge(x_hi_parts, 4)
                    v_new = v_sb[:, :, SEQ:T].rearrange("p i (b t) -> p i b t", t=DEC_L)
                    k_new = k_dec[:, :, SEQ:T].rearrange("p i (b t) -> p i b t", t=DEC_L)
                    for n in (1, 3):
                        dve.tensor_tensor(v_x[:, :, :, n, :].bitcast(F32R), v_new, v_x[:, :, :, 0, :], ALU.subtract)\
                           .then_inc(x_lo_parts, 1)
                    for n in (2, 3):
                        dve.tensor_tensor(k_x[:, :, :, n, :].bitcast(F32R), k_new, k_x[:, :, :, 0, :], ALU.subtract)\
                           .then_inc(x_lo_parts, 1)

            def new_state(b):
                dve.wait_ge(kv_done, b + 1)
                dve.wait_ge(o_done, b + 1)
                for h in range(HB):
                    kv = bank[4 + h // 2][:, DV * (h % 2):DV * (h % 2) + DV]
                    st_t.up(dve.scalar_tensor_tensor(s0[:, b % 4, h, :], s0[:, b % 4, h, :],
                                                     decays[:, h, DDEC + b:DDEC + b + 1], kv, ALU.mult, ALU.add))

            for c, s in enumerate(range(S_VA, S_ZA)):
                split_lo(s)
                sums(s)
                acc_t.up(dve.tensor_tensor(va_sb[:, c, :], bank[s % 2][:, 0:T], r, ALU.mult))
                if c:
                    new_state(c - 1)

            for b, s in enumerate(range(S_ZA, S_U)):
                split_lo(s)
                if b == 0:
                    dve.wait_ge(sum_done, 2)
                    variance(tmp[:, 1, :], bank[7][:, 0:T], EA)
                silu(s, za_gate[:, b, :])
                if b == 0:
                    new_state(DEC_B - 1)
                if b == 4:
                    dve.wait_ge(sum_done, 3)
                    for h in range(HB):
                        variance(r_o[:, h, :], bank[4 + h][:, 0:T], DV)
                if b == 0:
                    dve.wait_ge(r_ready, 2)
                    for i in range(KE):
                        dve.scalar_tensor_tensor(va_sb[:, i, :], va_sb[:, i, :], col(C_GV, i), tmp[:, 1, :],
                                                 ALU.mult, ALU.mult).then_inc(va_normed, 1)
                if b >= 4:
                    dve.wait_ge(sp_done, b - 3)
                    if b == 4:
                        dve.wait_ge(cv_stored, 16)
                    for c in range(2):
                        i = 2 * (b - 4) + c
                        h = i // 2
                        dve.tensor_tensor(sp_sb[:, i, 0:SEQ].rearrange("p (c t) -> p c t", t=CHUNK),
                                          bank[2 + c][:, 0:SEQ].rearrange("p (c t) -> p c t", t=CHUNK),
                                          bs[:, h:h + 1, :].to_broadcast([P, 2, CHUNK]), ALU.add).then_inc(sp_read, 1)
                        dve.tensor_tensor(sp_sb[:, i, SEQ:T].rearrange("p (c t) -> p c t", t=DEC_L),
                                          bank[2 + c][:, SEQ:T].rearrange("p (c t) -> p c t", t=DEC_L),
                                          bs[:, h:h + 1, 0:DEC_L].to_broadcast([P, DEC_B, DEC_L]), ALU.add)\
                           .then_inc(sp_read, 1)
            dve.wait_ge(sp_read, 4 * 4)

            def yb(i):
                then(dve.scalar_tensor_tensor(tmp[:, 1, :], o_sb[:, i, :], col(C_GO, i), r_o[:, i // 2, :],
                                              ALU.mult, ALU.mult))
                y_full_t.up(dve.tensor_tensor(tmp[:, 3, :], tmp[:, 1, :], zb_gate[:, i, :], ALU.mult))

            def y_low(br, i):
                y_round_t.next(dve)
                dve.tensor_tensor(ylo[br][:, i, :], tmp[:, 2 + br, :], yhi[br][:, i, :].bitcast(F32), ALU.subtract)\
                   .then_inc(y_split, 1)

            dve.wait_ge(r_ready, 3)
            for j, s in enumerate(range(S_U, S_GATE)):
                split_lo(s)
                sums(s)
                acc_t.up(dve.tensor_tensor(tmp[:, 0, :], bank[s % 2][:, 0:T], r, ALU.mult))
                own.up(dve.scalar_tensor_tensor(tmp[:, 3, :], o_sb[:, j, :], col(C_GO, j), r_o[:, j // 2, :],
                                                ALU.mult, ALU.mult))
                dve.wait_ge(acc_read, acc_t.value)
                own.up(dve.tensor_tensor(tmp[:, 2, :], tmp[:, 0, :], za_gate[:, j, :], ALU.mult))
                dve.wait_ge(dve_own, own.value)
                y_full_t.up(dve.tensor_tensor(tmp[:, 2, :], tmp[:, 2, :], sp_sb[:, j, :], ALU.mult))
                y_full_t.up(dve.tensor_tensor(tmp[:, 3, :], tmp[:, 3, :], zb_gate[:, j, :], ALU.mult))
                for br in range(2):
                    y_round_t.next(dve)
                    dve.tensor_tensor(ylo[br][:, j, :], tmp[:, 2 + br, :], yhi[br][:, j, :].bitcast(F32),
                                      ALU.subtract).then_inc(y_split, 1)
                dve.wait_ge(y_split, 2 * j + 2)

            with repeat(dve, KX // 2, {acc_t: 6, sig_t: 4, own: 2, m_full_t: 2, m_round_t: 2}) as i:
                for b in range(2):
                    for g in range(3):
                        n = 3 * b + g
                        for half in range(2):
                            u = 2 * (S_GATE + n + 2) + half
                            low(2 * (n % 2) + half, 12 * i + (u + 1), 12 * i + (u - 3))
                        sums(S_GATE + n, i, 12)
                        if g < 2:
                            acc_t.up(dve.tensor_tensor(tmp[:, g, :], bank[n % 2][:, 0:T], r, ALU.mult))
                    sig_t.next(dve, 2)
                    own.up(dve.tensor_tensor(tmp[:, 2, :], bank[2][:, 0:T], sig[:, 0, :], ALU.mult))
                    acc_t.up(dve.tensor_tensor(tmp[:, 3, :], bank[3][:, 0:T], sig[:, 1, :], ALU.mult))
                    dve.wait_ge(acc_read, acc_t.value)
                    m_full_t.up(dve.tensor_tensor(tmp[:, 2, :], tmp[:, 2, :], tmp[:, 3, :], ALU.add))
                    m_round_t.next(dve)
                    dve.tensor_tensor(mlo[:, 2 * i + b, :], tmp[:, 2, :], mhi[:, 2 * i + b, :].bitcast(F32),
                                      ALU.subtract).then_inc(m_split, 1)
                    dve.wait_ge(m_split, 2 * i + (b + 1))

            def wo_sums(s, i=None, j=None):
                u = 2 * (s + 2)
                q = 2 * (s % 2)
                low(q, *((u + 1, u - 3) if i is None else (4 * i + (u + 1), 4 * i + (u - 3))))
                sums(s, i)
                acc_t.up(dve.tensor_copy(mo_sb[:, j, :], bank[s % 2][:, 0:T]))
                if s != S_WO + KX - 1:
                    low(q + 1, *((u + 2, u - 2) if i is None else (4 * i + (u + 2), 4 * i + (u - 2))))

            for b in range(2):
                wo_sums(S_WO + b, None, b)
            dve.wait_ge(p_rounded, 1)
            dve.tensor_tensor(p_lo[:], p_raw[:], p_hi[:].bitcast(F32), ALU.subtract).then_inc(p_split, 1)
            with repeat(dve, KX // 2 - 2, {acc_t: 2}) as i:
                for b in range(2):
                    wo_sums(S_WO + 2 + b, i, 2 * i + (2 + b))
            for b in range(2):
                wo_sums(S_WO + KX - 2 + b, None, KX - 2 + b)
            dve.wait_ge(acc_read, acc_t.value)
            dve.tensor_tensor(tmp[:, 0, :], mo_sb[:, KX - 1, :], mo_sb[:, KX - 1, :], ALU.mult).then_inc(sum_last, 1)
            low(3, 2 * S_PE + 4, 2 * S_PE)
            dve.wait_ge(sum_done, 4)
            variance(r_tok[:, :], bank[NORM_BANK][:, 0:T], D)
            AHEAD = 2

            def h_norm(k):
                if k >= 4:
                    dve.wait_ge(h_full, k - 3)
                dve.scalar_tensor_tensor(tmp[:, k % 4, :], mo_sb[:, k, :], col(C_GPOST, k), r, ALU.mult, ALU.mult)\
                   .then_inc(hn_ready, 1)

            for n in range(4):
                if n == 0:
                    low(n, 2 * S_PG + 1, 2 * S_PE + 1)
                    dve.wait_ge(r_ready, 4)
                    dve.wait_ge(sum_last, 1)
                    for k in range(AHEAD):
                        h_norm(k)
                else:
                    low(n, 2 * S_PG + n + 1, 2 * S_PE + n + 1)
                for k in range(H_WITH[n], H_WITH[n + 1]):
                    if k + AHEAD < KX:
                        h_norm(k + AHEAD)
                    dve.wait_ge(h_rounded, k + 1)
                    dve.tensor_tensor(mlo[:, k, :], h_sb[:, k, :], mhi[:, k, :].bitcast(F32), ALU.subtract)\
                       .then_inc(h_split, 1)

            def output(j, b):
                sig_t.next(dve)
                acc_t.up(dve.tensor_tensor(tmp[:, b, :], sig[:, b, :], pe_out[:, j, :], ALU.mult))
                dve.wait_ge(acc_read, acc_t.value)
                out_t.up(dve.tensor_tensor(pe_out[:, j, :], tmp[:, b, :], h_sb[:, j, :], ALU.add))
                dve.wait_ge(out_ready, out_t.value)

            for j in range(2):
                split_lo(S_PG + j)
                output(j, j)
            with repeat(dve, KX // 2 - 2, {sig_t: 2, acc_t: 2, out_t: 2}) as i:
                for b in range(2):
                    split_lo(S_PG + 2 + b, i)
                    output(2 * i + (b + 2), b)
            for j in range(KX - 2, KX):
                output(j, j % 2)

        @block.gpsimd
        def _(pool):
            own = Tally(pool_own)

            def then(ins):
                own.up(ins)
                pool.wait_ge(pool_own, own.value)

            for x in (att0, att1, att_s):
                pool.memset(x[:], 0.0).then_inc(att_zeroed, 1)
            for c in range(2):
                pool.wait_ge(squared, c + 1)
                for w in (4, 2):
                    a = 8 * c
                    then(pool.tensor_tensor(squares[:, a:a + w, :], squares[:, a:a + w, :],
                                            squares[:, a + w:a + 2 * w, :], ALU.add))
            then(pool.tensor_tensor(squares[:, 0:2, :], squares[:, 0:2, :], squares[:, 8:10, :], ALU.add))
            pool.tensor_tensor(squares[:, 0, :], squares[:, 0, :], squares[:, 1, :], ALU.add).then_inc(sq_ready, 1)
            pool.wait_ge(consts_loaded, 16 * 5)
            for w, n in ((wst, CHUNK), (wsb, DEC)):
                pool.affine_select(out=w[:], in_=w[:], compare_op=ALU.is_ge, fill=0.0, base=0,
                                   pattern=[[0, HA], [1, n]], channel_multiplier=-1).then_inc(ws_masked, 1)
            pool.wait_ge(acc_read, S_V)
            pool.wait_ge(decays_kept, 2)
            for x, y in ((k_dec, k_sb), (q_dec, q_sb), (k_mid, k_sb), (q_mid, q_sb)):
                pool.tensor_tensor(x[:], x[:], y[:], ALU.mult).then_inc(gla_in, 1)
            blk_k = k_dec[:, :, 0:SEQ].rearrange("p h (c t) -> p h c t", t=BLK)
            blk_q = q_dec[:, :, 0:SEQ].rearrange("p h (c t) -> p h c t", t=BLK)

            def decayed(out, x, d0, d1=None, step=1, positions=BLK):
                if d0 is None:
                    return pool.tensor_copy(out, x)
                n = 1 if d1 is None else len(range(d0, d1, step))
                by = decays[:, :, d0:(d0 + 1 if d1 is None else d1):step]
                if n == 1:
                    return pool.tensor_tensor(out, x, by.to_broadcast([P, HB, positions]), ALU.mult)
                by = by.rearrange("p h (c o) -> p h c o", o=1).to_broadcast([P, HB, n, positions])
                return pool.tensor_tensor(out, x, by, ALU.mult)

            pool.wait_ge(gla_in, 4)
            then(decayed(q_64[:, :, :, 0:BLK], blk_q[:, :, 2::4, :], None))
            then(decayed(q_64[:, :, :, BLK:2 * BLK], blk_q[:, :, 3::4, :], 2, NBLK, 4))
            then(decayed(k_64[:, :, :, 0:BLK], blk_k[:, :, 0::4, :], 1, NBLK, 4))
            then(decayed(k_64[:, :, :, BLK:2 * BLK], blk_k[:, :, 1::4, :], None))
            then(decayed(q_128[:, :, 0:BLK], blk_q[:, :, 4, :], None))
            then(decayed(q_128[:, :, BLK:2 * BLK], blk_q[:, :, 5, :], 4))
            then(decayed(q_128[:, :, 2 * BLK:P], q_64[:, :, 1, :], D64 + 2, positions=64))
            then(decayed(k_128[:, :, 0:2 * BLK], k_64[:, :, 0, :], D64 + 1, positions=64))
            then(decayed(k_128[:, :, 2 * BLK:3 * BLK], blk_k[:, :, 2, :], 3))
            then(decayed(k_128[:, :, 3 * BLK:P], blk_k[:, :, 3, :], None))
            then(decayed(k_256[:, :, 0:P], k_128[:], D128, positions=P))
            then(decayed(k_256[:, :, P:P + 64], k_64[:, :, 1, :], D64 + 3, positions=64))
            then(decayed(k_256[:, :, P + 64:P + 96], blk_k[:, :, 6, :], 7))
            pool.tensor_copy(k_256[:, :, P + 96:SEQ], blk_k[:, :, 7, :]).then_inc(gla_in, 1)

            def add_squares(x, first, last):
                if first:
                    then(pool.tensor_tensor(v_sum[:, :], x, x, ALU.mult))
                else:
                    then(pool.tensor_tensor(v_sq[:, :], x, x, ALU.mult))
                    add = pool.tensor_tensor(v_sum[:, :], v_sum[:, :], v_sq[:, :], ALU.add)
                    if last:
                        add.then_inc(sq_ready, 1)
                    else:
                        then(add)

            for c in range(KE):
                pool.wait_ge(acc_read, S_VA + c + 1)
                add_squares(va_sb[:, c, :], c == 0, c == KE - 1)
            pool.wait_ge(o_copied, 1)
            pool.wait_ge(st_stored, 16)
            then(pool.tensor_tensor(o_sq[:], o_sb[:].rearrange("p (h i) t -> p h i t", i=2),
                                    o_sb[:].rearrange("p (h i) t -> p h i t", i=2), ALU.mult))
            pool.tensor_tensor(o_sum[:], o_sq[:, :, 0, :], o_sq[:, :, 1, :], ALU.add).then_inc(sq_ready, 1)
            pool.wait_ge(acc_read, S_WO + 1)
            then(pool.tensor_tensor(sig[:, 0, :], mo_sb[:, 0, :], mo_sb[:, 0, :], ALU.mult))
            with repeat(pool, KX - 3, {own: 2}) as i:
                pool.wait_ge(acc_read, i + (S_WO + 2))
                then(pool.tensor_tensor(sig[:, 1, :], mo_sb[:, i + 1, :], mo_sb[:, i + 1, :], ALU.mult))
                then(pool.tensor_tensor(sig[:, 0, :], sig[:, 0, :], sig[:, 1, :], ALU.add))
            pool.wait_ge(acc_read, S_WO + KX - 1)
            then(pool.tensor_tensor(sig[:, 1, :], mo_sb[:, KX - 2, :], mo_sb[:, KX - 2, :], ALU.mult))
            pool.tensor_tensor(sig[:, 0, :], sig[:, 0, :], sig[:, 1, :], ALU.add).then_inc(sq_ready, 1)
            for k in range(KX):
                if k % 4 == 0:
                    pool.wait_ge(xr_loaded[k // 4], 16)
                pool.wait_ge(hn_ready, k + 1)
                pool.tensor_tensor(h_sb[:, k, :], h_sb[:, k, :], tmp[:, k % 4, :], ALU.add).then_inc(h_full, 1)

        @block.tensor
        def _(pe):
            def product(acc, q, hi, lo, k0, first, last, used=True, wait_k=None):
                for k in range(UK):
                    if wait_k is not None:
                        pe.wait_ge(wait_k, k0 + k + 1)
                    h, l = whi[:, q, k, :], wlo[:, q, k, :]
                    pe.matmul(acc, h, hi[:, k0 + k, :], start=first and k == 0, stop=False)
                    pe.matmul(acc, h, lo[:, k0 + k, :], start=False, stop=False)
                    m = pe.matmul(acc, l, hi[:, k0 + k, :], start=False, stop=last and k == UK - 1)
                m.then_inc(units_used, 1)

            def ready(u, i=None, by=4):
                pe.wait_ge(lo_ready, u + 1 if i is None else by * i + (u + 1))

            def step(s, hi, lo, i=None, by=2, free=None, wait_k=None, acc=None):
                if free is not False:
                    n = s - 1 if free is None else free
                    pe.wait_ge(acc_read, n if i is None else by * i + n)
                acc = acc or bank[s % 2]
                for half in range(2):
                    ready(2 * s + half, i, 2 * by)
                    product(acc[:, 0:T], 2 * (s % 2) + half, hi, lo, UK * half, half == 0, half == 1,
                            wait_k=wait_k)

            def sum_partitions(acc, x):
                return pe.matmul(acc, ones, x, start=True, stop=True)

            def three(acc, h, l, hi, lo, first, last):
                pe.matmul(acc, h, hi, start=first, stop=False)
                pe.matmul(acc, h, lo, start=False, stop=False)
                return pe.matmul(acc, l, hi, start=False, stop=last)

            pe.wait_ge(alr_lo, 1)
            for half in range(2):
                for k in range(UK * half, UK * half + UK):
                    pe.wait_ge(x_split, k + 1)
                    m = three(bank[4][0:RANK, 0:T], wr_hi[:, k, :], wr_lo[:, k, :], xhi[:, k, :], xlo[:, k, :],
                              k == 0, k == KX - 1)
                if half:
                    m.then_inc(alr_done, 1)
                for b in range(2):
                    ready(2 * half + b)
                    product(bank[b][:, 0:T], 2 * half + b, xhi, xlo, UK * half, half == 0, half == 1)
            pe.wait_ge(consts_loaded, 16 * 5)
            for s in range(S_K + 2, S_V):
                if s == S_K + 2:
                    step(s, xhi, xlo, acc=bank[2], free=False)
                    pe.wait_ge(sq_ready, 1)
                    sum_partitions(bank[5][:, 0:T], squares[:, 0, :]).then_inc(sum_done, 1)
                elif s == S_K + 3:
                    step(s, xhi, xlo, acc=bank[3], free=False)
                    pe.wait_ge(alr_ready, 1)
                    for h in range(HB):
                        m = pe.matmul(bank[4 + h][:, 0:T], wa2[:, DK * h:DK * h + DK], alr[:, :], start=True, stop=True)
                    m.then_inc(logits_done, 1)
                else:
                    step(s, xhi, xlo)
            with repeat(pe, KE // 2, {}) as i:
                for b in range(2):
                    step(S_V + b, xhi, xlo, i)

            def to_tokens(x, t, banks, done):
                w = P if t < 2 else DEC
                for i in range(KE):
                    m = pe.transpose(bank[banks[i // 4]][0:w, P * (i % 4):P * (i % 4) + P],
                                     x[:, i, P * t:P * t + w], ident)
                m.then_inc(done, 1)

            def stack_rows(x, n, banks):
                for g in range(2):
                    for i in range(n):
                        c = n * g + i
                        m = pe.transpose(bank[banks[c // 4]][:, P * (c % 4):P * (c % 4) + P],
                                         x[:, i, GRP * g:GRP * g + GRP].rearrange("p b n t -> p (b n t)"), ident)
                m.then_inc(xt_done, 1)

            def o_prompt(n):
                for c in range(4):
                    i = 4 * n + c
                    acc = bank[OP_BANKS[n][c // 2]][:, SEQ * (c % 2):SEQ * (c % 2) + SEQ]
                    v0, v1 = (v_t[:, t, P * i:P * i + P] for t in range(2))
                    pe.matmul(acc[:, 0:P], v0, att0[:, i // 2, 0:P], start=True, stop=True)
                    pe.matmul(acc[:, P:SEQ], v0, att0[:, i // 2, P:SEQ], start=True, stop=False)
                    m = pe.matmul(acc[:, P:SEQ], v1, att1[:, i // 2, :], start=False, stop=True)
                m.then_inc(op_done, 1)

            for t, s in enumerate(range(S_ZB, S_VA)):
                step(s, xhi, xlo)
                if t == 0:
                    pe.wait_ge(gla_in, 5)
                    for c in range(2):
                        for h in range(HB):
                            pe.matmul(bank[4 + c][:, P * h:P * h + P], k_mid[:, h, P * c:P * c + P],
                                      q_mid[:, h, P * c:P * c + P], start=True, stop=True)
                    for h in range(HB):
                        pe.matmul(bank[3][0:DEC, DEC * h:DEC * h + DEC], k_mid[:, h, SEQ:T], q_mid[:, h, SEQ:T],
                                  start=True, stop=True)
                    for c in range(2):
                        for h in range(HB):
                            c0 = 64 * (HB * c + h)
                            odd = q_dec[:, h, P * c:P * c + P].rearrange("p (c t) -> p c t", t=BLK)[:, 1::2, :]
                            pe.matmul(bank[6][:, c0:c0 + 64], k_dec[:, h, P * c:P * c + P], odd, start=True, stop=True)
                            pe.matmul(bank[7][0:64, c0:c0 + 64], k_64[:, h, c, :], q_64[:, h, c, :],
                                      start=True, stop=True)
                    for h in range(HB):
                        m = pe.matmul(bank[2][:, P * h:P * h + P], k_128[:, h, :], q_128[:, h, :],
                                      start=True, stop=True)
                    m.then_inc(att_done, 1)
                if t == 1:
                    pe.wait_ge(att_masked, 3)
                    for c in range(2):
                        for h in range(HB):
                            m = pe.transpose(bank[4 + c][:, P * h:P * h + P], k_256[:, h, P * c:P * c + P], ident)
                    m.then_inc(kdt_done, 1)
                if 2 <= t <= 4:
                    pe.wait_ge(att_copied, 7)
                    if t == 4:
                        pe.wait_ge(vt_copied, 2)
                    to_tokens(v_sb, t - 2, VT_BANKS[t - 2], vt_done)
                if t == 5:
                    pe.wait_ge(x_lo_parts, 4)
                    pe.wait_ge(kdt_copied, 2)
                    pe.wait_ge(vt_copied, 6)
                    stack_rows(v_x, KE, (4, 5, 6, 7))
                    stack_rows(k_x, HB, (2, 3))
                if t == 6:
                    pe.wait_ge(xt_copied, 4)
                    for h in range(HB):
                        for c in range(2):
                            m = pe.matmul(bank[4 + h // 2][:, DV * (h % 2):DV * (h % 2) + DV],
                                          kd_t[:, c, DK * h:DK * h + DK], v_t[:, c, DV * h:DV * h + DV],
                                          start=c == 0, stop=c == 1)
                    m.then_inc(ps_done, 1)
                if t == 7:
                    o_prompt(0)

            def sequence(b):
                rows = slice(BLK * (b % GRP), BLK * (b % GRP) + BLK)
                for h in range(HB):
                    m = pe.matmul(bank[4 + h // 2][:, DV * (h % 2):DV * (h % 2) + DV],
                                  kx_t[rows, b // GRP, DK * h:DK * h + DK], vx_t[rows, b // GRP, DV * h:DV * h + DV],
                                  start=True, stop=True)
                m.then_inc(kv_done, 1)
                if b == 0:
                    for i in range(KE):
                        pe.matmul(bank[6][:, DEC * i:DEC * i + DEC], v_ts[:, P * i:P * i + P], att_s[:, i // 2, :],
                                  start=i == 0, stop=False, skip_group_check=True)
                pe.wait_ge(s0_loaded[b % 4], 16 * (b // 4 + 1))
                for i in range(KE):
                    h, half = i // 2, i % 2
                    c0 = DEC * i + DEC_L * b
                    m = pe.matmul(bank[6][:, c0:c0 + DEC_L], s0[:, b % 4, h, P * half:P * half + P],
                                  q_dec[:, h, SEQ + DEC_L * b:SEQ + DEC_L * b + DEC_L], start=False,
                                  stop=True, skip_group_check=True)
                m.then_inc(o_done, 1)

            for c, s in enumerate(range(S_VA, S_ZA)):
                step(s, xhi, xlo)
                if c == 0:
                    pe.wait_ge(xt_copied, 6)
                    o_prompt(1)
                else:
                    if c == 1:
                        pe.wait_ge(ps_copied, 2)
                        pe.wait_ge(op_copied, 2)
                    else:
                        pe.wait_ge(st_ready, HB * (c - 1))
                    sequence(c - 1)

            for b, s in enumerate(range(S_ZA, S_U)):
                step(s, xhi, xlo)
                if b == 0:
                    pe.wait_ge(sq_ready, 2)
                    sum_partitions(bank[7][:, 0:T], v_sum[:, :]).then_inc(sum_done, 1)
                    pe.wait_ge(st_ready, HB * (DEC_B - 1))
                    sequence(DEC_B - 1)
                if b == 3:
                    pe.wait_ge(sq_ready, 3)
                    pe.wait_ge(st_ready, HB * DEC_B)
                    pe.wait_ge(var_ready, 2)
                    for h in range(HB):
                        m = sum_partitions(bank[4 + h][:, 0:T], o_sum[:, h, :])
                    m.then_inc(sum_done, 1)
                if 1 <= b <= 3:
                    if b == 1:
                        pe.wait_ge(va_normed, KE)
                    else:
                        pe.wait_ge(vat_copied, 2 * (b - 1))
                    to_tokens(va_sb, b - 1, (2, 3), vat_done)
                if b >= 4:
                    if b == 4:
                        pe.wait_ge(vat_copied, 6)
                        pe.wait_ge(ws_masked, 2)
                    else:
                        pe.wait_ge(sp_read, 4 * (b - 4))
                    for c in range(2):
                        i = 2 * (b - 4) + c
                        for t in range(2):
                            pe.matmul(bank[2 + c][:, P * t:P * t + P], va_t[:, t, P * i:P * i + P],
                                      wst[:, i // 2, :], start=True, stop=True)
                        m = pe.matmul(bank[2 + c][:, SEQ:T], va_ts[:, P * i:P * i + P], wsb[:, i // 2, :],
                                      start=True, stop=True)
                    m.then_inc(sp_done, 1)

            for j, s in enumerate(range(S_U, S_GATE)):
                step(s, xhi, xlo)
            with repeat(pe, KX // 2, {}) as i:
                for b in range(2):
                    for g in range(2):
                        step(S_GATE + 3 * b + g, xhi, xlo, i, 6)
                    s = S_GATE + 3 * b + 2
                    pe.wait_ge(y_split, 2 * KE)
                    pe.wait_ge(acc_read, 6 * i + (s - 1))
                    for half in range(2):
                        ready(2 * s + half, i, 12)
                        product(bank[2 + half][:, 0:T], 2 * (s % 2) + half, yhi[half], ylo[half], 0, True, True)
            step(S_WO, mhi, mlo, wait_k=m_split)
            step(S_WO + 1, mhi, mlo)
            with repeat(pe, KX // 2 - 1, {}) as i:
                for b in range(2):
                    step(S_WO + 2 + b, mhi, mlo, i)
            pe.wait_ge(p_split, 1)
            for n in range(4):
                if n == 1:
                    pe.wait_ge(acc_read, S_PE)
                if n >= 2:
                    pe.wait_ge(pe_read, 4 * (n - 1))
                ready(2 * S_PE + n)
                for c in range(4):
                    if n == 0 and c == 2:
                        pe.wait_ge(sq_ready, 4)
                        pe.matmul(bank[NORM_BANK][:, 0:T], ones, sig[:, 0, :], start=True, stop=False)
                        pe.wait_ge(sum_last, 1)
                        pe.matmul(bank[NORM_BANK][:, 0:T], ones, tmp[:, 0, :], start=False, stop=True)\
                          .then_inc(sum_done, 1)
                    if n == 1 and PE_BANKS[n][c] == NORM_BANK:
                        pe.wait_ge(var_ready, 3 + HB)
                    for k in range(PLE // P):
                        m = three(bank[PE_BANKS[n][c]][:, 0:T], whi[:, n, 2 * c + k, :], wlo[:, n, 2 * c + k, :],
                                  p_hi[:, k, :], p_lo[:, k, :], k == 0, k == PLE // P - 1)
                m.then_inc(units_used, 1)
            pe.wait_ge(pe_read, 12)
            for half in range(2):
                ready(2 * S_PG + 2 * half + 1)
                for k in range(UK):
                    n = UK * half + k
                    pe.wait_ge(h_split, n + 1)
                    for b in range(2):
                        m = three(bank[PG_BANKS[b]][:, 0:T], whi[:, 2 * half + b, k, :], wlo[:, 2 * half + b, k, :],
                                  mhi[:, n, :], mlo[:, n, :], n == 0, n == KX - 1)
                        if k == UK - 1:
                            m.then_inc(units_used, 1)
            pe.wait_ge(pe_read, 16)
            with repeat(pe, KX // 2 - 1, {}) as i:
                for b in range(2):
                    step(S_PG + 2 + b, mhi, mlo, i, free=S_PE + 1 + b)


def columns():
    sizes = (EA, EA, EA, HB * DK, HB * DK, EB, EB, RANK, D, D)
    u, va, za, q, k, vb, zb, lr, ma, mb = np.cumsum((0,) + sizes[:-1]).tolist()
    order = [s + P * i for s, n in ((k, HB), (q, HB), (vb, KE), (zb, KE), (va, KE), (za, KE), (u, KE)) for i in range(n)]
    return order, lr, ma, mb


def constants():
    c = np.zeros((P, C_CONSTS), np.float32)
    c[:, C_ID:C_ID + P] = np.eye(P)
    c[:, C_ONE:C_ONE + P] = 1
    s, t = np.mgrid[0:P, 0:P]
    c[:, C_ATT:C_ATT + P] = (s // BLK == t // BLK) & (t >= s)
    s, t = np.mgrid[0:DEC, 0:DEC]
    c[:DEC, C_ATS:C_ATS + DEC] = (s // DEC_L == t // DEC_L) & (t >= s)
    c[:, C_RESET:C_RESET + T] = 1
    c[:, C_RESET:C_RESET + SEQ:BLK] = 0
    c[:, C_RESET + SEQ:C_RESET + T:DEC_L] = 0
    return c


def kernel(**inputs):
    import concourse.bacc as _bacc
    from concourse.bass_utils import run_bass_kernel_spmd as _run

    a = {n: np.asarray(v) for n, v in inputs.items()}
    f32 = np.float32

    def tokens_last(prompt, sample):
        x = np.concatenate([prompt.reshape(SEQ, -1), sample.reshape(DEC, -1)])
        return np.ascontiguousarray(x.reshape(T, -1, P).transpose(2, 1, 0))

    order, lr, ma, mb = columns()
    w_in, w_pa, w_pb, w_o, w_pg, w_pe = (a[n][0] for n in ("w_in", "w_pa", "w_pb", "w_o", "w_pg", "w_pe"))
    units = np.empty((UNITS, P, UK, P), f32)
    at = [0]

    def add(w, c):
        for k in range(0, w.shape[0], UK * P):
            units[at[0]] = w[k:k + UK * P, c:c + P].reshape(UK, P, P).transpose(1, 0, 2)
            at[0] += 1

    for c in order:
        add(w_in, c)
    for j in range(KX):
        add(w_in, ma + P * j)
        add(w_in, mb + P * j)
        add(w_pa, P * j)
        add(w_pb, P * j)
    for j in range(KX):
        add(w_o, P * j)
    for j in range(0, KX, 4):
        units[at[0]] = w_pe[:, P * j:P * (j + 4)].reshape(2, P, 4, P).transpose(1, 2, 0, 3).reshape(P, UK, P)
        at[0] += 1
    for j in range(KX):
        add(w_pg, P * j)
    assert at[0] == UNITS
    for s in (S_K, S_PG):
        units[2 * s + 1:2 * s + 3] = units[[2 * s + 2, 2 * s + 1]]

    params = np.concatenate([a[n][0].reshape(-1, P).T for n in ("g_pre", "g_v", "g_o", "b_a", "g_post")], axis=1)
    w_s = a["w_s"][0]
    w_s_dec = np.zeros((DEC, HA, DEC), f32)
    for b in range(DEC_B):
        r = slice(DEC_L * b, DEC_L * (b + 1))
        w_s_dec[r, :, r] = w_s[:, :DEC_L, :DEC_L].transpose(2, 0, 1)
    arrays = {
        "x_t": tokens_last(a["x_prompt"], a["x_sample"]),
        "p_t": tokens_last(a["p_prompt"][0], a["p_sample"][0]),
        "w_units": units,
        "w_alr": np.ascontiguousarray(w_in[:, lr:lr + RANK].reshape(KX, P, RANK).transpose(1, 0, 2)),
        "params": np.ascontiguousarray(params),
        "consts": constants(),
        "w_s_t": np.ascontiguousarray(w_s.transpose(2, 0, 1)),
        "w_s_dec": w_s_dec,
        "b_s_rows": np.ascontiguousarray(np.broadcast_to(a["b_s"][0][None], (P, HA, CHUNK))),
        "w_a2": np.ascontiguousarray(a["w_a2"][0]),
        "s0": np.ascontiguousarray(a["state_gla"][0]),
    }
    outs = {"y": (P, KX, T), "st_prompt": (HB, DK, DV), "st_dec": (DEC_B, HB, DK, DV), "cv": (KE, P, DEC)}

    nc = _bacc.Bacc("TRN2", target_bir_lowering=False, num_devices=1)
    A = {n: nc.dram_tensor(f"in_{n}", v.shape, F32, kind="ExternalInput").ap() for n, v in arrays.items()}
    O = {n: nc.dram_tensor(f"out_{n}", s, F32, kind="ExternalOutput").ap() for n, s in outs.items()}
    build(nc, A, O)
    got = _run(nc, [{f"in_{n}": v for n, v in arrays.items()}], core_ids=[0]).results[0]
    y = got["out_y"].transpose(2, 1, 0).reshape(T, D)
    return (
        y[:SEQ].reshape(1, SEQ, D),
        y[SEQ:].reshape(DEC_B, DEC_L, D),
        got["out_st_prompt"][None, None],
        got["out_st_dec"][None],
        got["out_cv"].transpose(2, 0, 1).reshape(1, DEC_B, DEC_L, EA),
    )
```

```python
from contextlib import ExitStack, contextmanager

import concourse.bass as bass
import numpy as np
from concourse import mybir

F32, F32R, I32 = mybir.dt.float32, mybir.dt.float32r, mybir.dt.int32
ACT = mybir.ActivationFunctionType
ALU = mybir.AluOpType

P = 128
D = 2048
SEQ, CHUNK = 256, 128
DEC_B, DEC_L = 8, 8
DEC = DEC_B * DEC_L
T = SEQ + DEC
EA = EB = D // 2
HA, HB = 4, 4
DV, DK = EB // HB, EB // HB // 2
RANK, TAU, EPS = 16, 16.0, 1e-6
PLE = 256
KX = D // P
KE = EA // P
UK = 8
BLK = 32
NBLK = SEQ // BLK
MID = BLK // 2 - 1
QR = 2 * DEC_L
GRP = 4

S_K = 0
S_Q = S_K + HB
S_V = S_Q + HB
S_ZB = S_V + KE
S_VA = S_ZB + KE
S_ZA = S_VA + KE
S_U = S_ZA + KE
S_GATE = S_U + KE
S_WO = S_GATE + 3 * KX
S_PE = S_WO + KX
S_PG = S_PE + 2
STEPS = S_PG + KX
UNITS = 2 * STEPS

C_GPRE, C_GV, C_GO, C_BA, C_GPOST, C_PARAMS = 0, KX, KX + KE, KX + 2 * KE, KX + 2 * KE + HB, 2 * KX + 2 * KE + HB
C_ID, C_ONE, C_ATT, C_ATS, C_RESET, C_SEL = 0, P, 2 * P, 3 * P, 3 * P + DEC, 3 * P + DEC + T
C_CONSTS = C_SEL + DEC


class Tally:

    def __init__(self, sem, value=0):
        self.sem, self.base, self.k = sem, value, 0

    @property
    def value(self):
        return self.base + self.k

    def up(self, ins):
        ins.then_inc(self.sem, 1)
        self.k += 1

    def next(self, eng, n=1):
        self.k += n
        eng.wait_ge(self.sem, self.value)


@contextmanager
def repeat(eng, n, per):
    starts = {t: t.value for t in per}
    with eng.Fori(0, n) as i:
        for t, by in per.items():
            t.base, t.k = starts[t] + by * i, 0
        yield i
        for t, by in per.items():
            assert t.k == by, (t.sem, t.k, by)
    for t, by in per.items():
        t.base, t.k = starts[t] + by * n, 0


def build(nc, A, O):
    ctx = ExitStack()
    with ctx:
        XC = 8
        XB = KX // XC

        def sem(name):
            return ctx.enter_context(nc.semaphore(name))

        KB = 1024
        start = -(-nc.sbuf_base // 64) * 64
        SMALL = 19 * KB + 256
        total = 188 * KB + SMALL
        ctx.enter_context(nc.sbuf_tensor("arena", [P, (total + start - nc.sbuf_base + 3) // 4 + 1], F32))

        def at(name, off, shape, dtype=F32):
            assert off + int(np.prod(shape[1:])) * 4 <= total, name
            return nc.alloc_sbuf_tensor_at(name, shape, dtype, offset=start + off)

        W0, XG0, M0, Y0, X0, C0 = 0, 48 * KB, 88 * KB, 128 * KB, 168 * KB, 188 * KB
        TB = T * 4

        raw = at("w_raw", W0, [P, 4, UK, P])
        whi = at("w_hi", W0 + 16 * KB, [P, 4, UK, P], F32R)
        wlo = at("w_lo", W0 + 32 * KB, [P, 4, UK, P], F32R)
        xhi = at("x_hi", XG0, [P, KX, T], F32R)
        xlo = at("x_lo", XG0 + 20 * KB, [P, KX, T], F32R)
        p_raw = at("p_raw", XG0, [P, PLE // P, T])
        p_hi = at("p_hi", XG0 + 2 * TB, [P, PLE // P, T], F32R)
        p_lo = at("p_lo", XG0 + 4 * TB, [P, PLE // P, T], F32R)
        pe_out = at("pe_out", XG0 + 20 * KB, [P, KX, T])
        slot = HB * TB
        squares = at("squares", M0 + 2 * slot, [P, KX, T])
        k_dec = at("k_dec", M0, [P, HB, T])
        cum = at("decay_cum", M0 + slot, [P, HB, T])
        k_64 = at("k_64", M0 + slot, [P, HB, 2, 64])
        k_128 = at("k_128", M0 + slot + 2 * KB, [P, HB, P])
        q_sb = at("q", M0 + 2 * slot, [P, HB, T])
        k_256 = at("k_256", M0 + 2 * slot, [P, HB, SEQ])
        k_sb = at("k", M0 + 3 * slot, [P, HB, T])
        q_mid = at("q_mid", M0 + 4 * slot, [P, HB, T])
        k_mid = at("k_mid", M0 + 5 * slot, [P, HB, T])
        q_dec = at("q_dec", M0 + 6 * slot, [P, HB, T])
        wa2 = at("w_a2_sb", M0 + 7 * slot, [2 * RANK, HB * DK])
        alr = at("a_lr", M0 + 7 * slot + 2 * KB, [2 * RANK, T])
        q_64 = at("q_64", M0 + 7 * slot, [P, HB, 2, 64])
        q_128 = at("q_128", M0 + 7 * slot + 2 * KB, [P, HB, P])
        v_x = at("v_stacked", M0 + 4 * slot, [P, KE, DEC_B, 4, DEC_L])
        k_x = at("k_stacked", M0 + slot, [P, HB, DEC_B, 4, DEC_L])
        o_sb = at("o", M0 + 2 * slot, [P, KE, T])
        s0_hi = at("state_hi", M0 + 4 * slot, [P, HB, DV], F32R)
        s0_lo = at("state_lo", M0 + slot, [P, HB, DV], F32R)
        QW = P - QR
        q_x = at("q_among_zeros", M0 + 7 * slot, [P, HB, QW + P], F32R)
        oq = at("o_old_states", M0 + 4 * slot, [P, EB])
        za_gate = at("za_gate", M0, [P, KE, T])
        va_t = at("va_tokens", M0 + 4 * slot, [P, 2, EA])
        va_ts = at("va_tokens_dec", M0 + 7 * slot, [DEC, EA])
        v_sq = at("v_sq", M0 + 5 * slot, [P, T])
        v_sum = at("v_sum", M0 + 5 * slot + TB, [P, T])
        r_o = at("r_o", M0 + 6 * slot, [P, HB, T])
        mhi = at("m_hi", M0, [P, KX, T], F32R)
        mlo = at("m_lo", M0 + 20 * KB, [P, KX, T], F32R)
        vx_t = at("v_stacked_rows", Y0, [P, 2, EB], F32R)
        kx_t = at("k_stacked_rows", Y0 + 8 * KB, [P, 2, HB * DK], F32R)
        v_ts = at("v_tokens_dec", Y0 + 12 * KB, [DEC, EB])
        att_s = at("att_dec", Y0 + 16 * KB, [DEC, HB, DEC])
        st = at("state", Y0 + 17 * KB, [P, HB, DV])
        v_t = at("v_tokens", Y0 + 21 * KB, [P, 2, EB])
        kd_t = at("kd_tokens", Y0 + 29 * KB, [P, 2, HB * DK])
        att0 = at("att0", Y0 + 33 * KB, [P, HB, SEQ])
        att1 = at("att1", Y0 + 37 * KB, [P, HB, P])
        wr_raw = at("w_alr_raw", Y0 + 25 * KB, [P, KX, RANK])
        wr = at("w_alr_parts", Y0 + 26 * KB, [P, KX, 2 * RANK], F32R)
        s0 = at("state_dec", Y0 + 24 * KB, [P, 4, HB, DV])
        o_sq = at("o_sq", Y0, [P, HB, 2, T])
        o_sum = at("o_sum", Y0 + 10 * KB, [P, HB, T])
        yhi = [at(n, Y0 + o * KB, [P, KE, T], F32R) for n, o in (("ya_hi", 0), ("yb_hi", 20))]
        ylo = [at(n, Y0 + o * KB, [P, KE, T], F32R) for n, o in (("ya_lo", 10), ("yb_lo", 30))]
        h_sb = at("h", Y0, [P, KX, T])
        x_sb = at("x_sb", X0, [P, KX, T])
        v_sb = at("v_b", X0, [P, KE, T])
        va_sb = at("v_a", X0, [P, KE, T])
        sp_sb = at("spatial", X0, [P, KE, T])
        zb_gate = at("zb_gate", X0 + 10 * KB, [P, KE, T])
        mo_sb = at("mo", X0, [P, KX, T])
        off = C0
        small = {}
        for name, shape in (("params", [P, C_PARAMS]), ("consts", [P, C_CONSTS]), ("w_s_t", [P, HA, CHUNK]),
                            ("w_s_dec", [DEC, HA, DEC]), ("b_s_sb", [P, HA, CHUNK]), ("decays", [P, HB, 2 * NBLK + 8]),
                            ("r_tok", [P, T]), ("tmp", [P, 4, T]), ("sig", [P, 2, T]), ("warm", [P, 8])):
            small[name] = at(name, off, shape)
            off += -(-int(np.prod(shape[1:])) * 4 // 32) * 32
        par, con, wst, wsb, bs = (small[n] for n in ("params", "consts", "w_s_t", "w_s_dec", "b_s_sb"))
        decays, r_tok, tmp, sig = (small[n] for n in ("decays", "r_tok", "tmp", "sig"))
        ident, ones = con[:, C_ID:C_ID + P], con[:, C_ONE:C_ONE + P]

        def col(c, i):
            return par[:, c + i:c + i + 1]

        bank = [ctx.enter_context(nc.psum_tensor(f"bank{b}", [P, 512], F32)) for b in range(8)]

        VT_BANKS = ((6, 7), (2, 3), (6, 7))
        OP_BANKS = ((6, 7), (2, 3))
        PE_BANKS = ((4, 5, 6, 7), (0, 1, 2, 3), (4, 5, 6, 7), (0, 1, 2, 3))
        VAT_BANKS = ((2, 3), (6, 7), (2, 3))
        O_NORM = tuple(S_ZA + 5 + 2 * h for h in range(HB))
        D64, D128, DDEC = NBLK, NBLK + 4, NBLK + 5
        PG_BANKS = (6, 7)
        NORM_BANK = 3
        H_WITH = (0, 2, 5, 9, KX)

        x_loaded = [sem(f"x_loaded{c}") for c in range(XC)]
        par_loaded, consts_loaded, alrw_loaded = sem("par_loaded"), sem("consts_loaded"), sem("alrw_loaded")
        raw_loaded = [sem(f"raw_loaded{q}") for q in range(4)]
        hi_ready = sem("hi_ready")
        lo_ready = sem("lo_ready")
        units_used = sem("units_used")
        acc_read = sem("acc_read")
        alr_hi, alr_lo = sem("alr_hi"), sem("alr_lo")
        x_rounded, x_split = sem("x_rounded"), sem("x_split")
        alr_done, alr_ready = sem("alr_done"), sem("alr_ready")
        tables_loaded = sem("tables_loaded")
        squared = sem("squared")
        sq_ready = sem("sq_ready")
        o_squared = sem("o_squared")
        sum_done = sem("sum_done")
        var_ready = sem("var_ready")
        r_ready = sem("r_ready")
        logits_done = sem("logits_done")
        absneg_ready, softplus_ready = sem("absneg_ready"), sem("softplus_ready")
        spans_ready, exps_ready = sem("spans_ready"), sem("exps_ready")
        decays_kept, gla_in = sem("decays_kept"), sem("gla_in")
        att_zeroed, att_done, att_masked = sem("att_zeroed"), sem("att_done"), sem("att_masked")
        att_copied = sem("att_copied")
        kdt_done, kdt_copied = sem("kdt_done"), sem("kdt_copied")
        vt_done, vt_copied = sem("vt_done"), sem("vt_copied")
        x_hi_parts, x_lo_parts = sem("stacked_rounded"), sem("stacked_split")
        xt_done, xt_copied = sem("stacked_transposed"), sem("stacked_copied")
        ps_done, ps_copied = sem("prompt_state_done"), sem("prompt_state_copied")
        op_done, op_copied = sem("o_prompt_done"), sem("o_prompt_copied")
        q_zeroed = sem("q_zeroed")
        old_hi, old_lo = sem("old_state_hi"), sem("old_state_lo")
        oq_done, oq_copied = sem("o_old_states_done"), sem("o_old_states_copied")
        kv_done, st_ready = sem("kv_done"), sem("st_ready")
        o_done, o_copied = sem("o_done"), sem("o_copied")
        ws_masked = sem("ws_masked")
        va_normed, vat_done, vat_copied = sem("va_normed"), sem("vat_done"), sem("vat_copied")
        sp_done, sp_read = sem("sp_done"), sem("sp_read")
        s0_loaded = [sem(f"s0_loaded{q}") for q in range(4)]
        s0_stored = [sem(f"s0_stored{q}") for q in range(4)]
        st_stored, cv_stored = sem("st_stored"), sem("cv_stored")
        sig_done = sem("sig_done")
        gate_ready = sem("gate_ready")
        branch_gated = sem("branch_gated")
        yb_full = sem("yb_full")
        y_full, y_rounded, y_split = sem("y_full"), sem("y_rounded"), sem("y_split")
        m_full, m_rounded, m_split = sem("m_full"), sem("m_rounded"), sem("m_split")
        p_loaded, p_rounded, p_split = sem("p_loaded"), sem("p_rounded"), sem("p_split")
        xr_loaded = [sem(f"xr_loaded{c}") for c in range(4)]
        pe_read = sem("pe_read")
        sum_last, hn_ready = sem("sum_last"), sem("hn_ready")
        h_full, h_rounded, h_split = sem("h_full"), sem("h_rounded"), sem("h_split")
        out_ready, out_stored = sem("out_ready"), sem("out_stored")
        dve_own, act_own, pool_own = sem("dve_own"), sem("act_own"), sem("pool_own")

        block = ctx.enter_context(nc.Block())

        @block.sync
        def _(sp):
            def load_x(c):
                sp.dma_start(x_sb[:, XB * c:XB * c + XB, :], A["x_t"][:, XB * c:XB * c + XB, :])\
                  .then_inc(x_loaded[c], 16)

            def load_unit(q):
                sp.dma_start(raw[:, q], A["w_units"][q]).then_inc(raw_loaded[q], 16)

            for half in range(2):
                for c in range(XC // 2):
                    load_x(XC // 2 * half + c)
                    if half == 0 and c == 0:
                        sp.dma_start(par[:, :], A["params"]).then_inc(par_loaded, 16)
                        sp.dma_start(wr_raw[:], A["w_alr"]).then_inc(alrw_loaded, 16)
                load_unit(2 * half)
                load_unit(2 * half + 1)
            for dst, name in ((con, "consts"), (wst, "w_s_t"), (wsb, "w_s_dec"), (bs, "b_s_rows")):
                sp.dma_start(dst[:], A[name]).then_inc(consts_loaded, 16)
            for n in range(2):
                sp.dma_start(wa2[RANK * n:RANK * n + RANK, :], A["w_a2"]).then_inc(consts_loaded, 16)
            with sp.Fori(1, UNITS // 4) as i:
                for q in range(4):
                    sp.wait_ge(lo_ready, 4 * i + (q - 3))
                    sp.dma_start(raw[:, q], A["w_units"][4 * i + q]).then_inc(raw_loaded[q], 16)

        @block.scalar
        def _(act):
            sig_t, m_full_t, out_t = Tally(sig_done), Tally(m_full), Tally(out_ready)

            def copy_o_prompt(n):
                act.wait_ge(op_done, n + 1)
                for c in range(2):
                    i = 4 * n + 2 * c
                    act.activation(o_sb[:, i:i + 2, 0:SEQ],
                                   bank[OP_BANKS[n][c]][:, :].rearrange("p (i t) -> p i t", i=2), ACT.Copy)\
                       .then_inc(op_copied, 1)

            def split_hi(s, i=None):
                for half in range(2):
                    q = 2 * (s % 2) + half
                    turn = 16 * ((s + 2) // 2 + 1)
                    used = 2 * (s + 2) + half - 3
                    act.wait_ge(raw_loaded[q], turn if i is None else 16 * i + turn)
                    act.wait_ge(units_used, used if i is None else 4 * i + used)
                    act.activation(whi[:, q], raw[:, q], ACT.Copy).then_inc(hi_ready, 1)

            act.wait_ge(att_zeroed, 1)
            act.activation(small["warm"][0:1, 1:2], att1[0:1, 0, 0:1], ACT.Copy).then_inc(tables_loaded, 1)
            act.wait_ge(par_loaded, 16)
            for k in range(KX):
                if k == XB:
                    act.wait_ge(alrw_loaded, 16)
                    act.activation(wr[:, :, 0:RANK], wr_raw[:], ACT.Copy).then_inc(alr_hi, 1)
                if k % XB == 0:
                    act.wait_ge(x_loaded[k // XB], 16)
                act.activation(xhi[:, k, :], x_sb[:, k, :], ACT.Copy, scale=col(C_GPRE, k)).then_inc(x_rounded, 1)
                if k % 8 == 7:
                    for q in (k // 8 * 2, k // 8 * 2 + 1):
                        act.wait_ge(raw_loaded[q], 16)
                        act.activation(whi[:, q], raw[:, q], ACT.Copy).then_inc(hi_ready, 1)

            def root(n, out, x):
                act.wait_ge(var_ready, n)
                act.activation(out, x, ACT.Sqrt).then_inc(r_ready, 1)

            for s in range(S_K, S_V):
                split_hi(s)
                if s == S_K:
                    act.activation(squares[:, 8:16, :], x_sb[:, 8:16, :], ACT.Square).then_inc(squared, 1)
                if s == S_K + 1:
                    root(1, r_tok[:, :], tmp[:, 0, :])
                if s == S_Q:
                    act.wait_ge(absneg_ready, 1)
                    act.activation(cum[:], cum[:], ACT.Exp).then_inc(act_own, 1)
                    act.wait_ge(act_own, 1)
                    act.activation(cum[:], cum[:], ACT.Ln, bias=1.0).then_inc(softplus_ready, 1)
            act.wait_ge(spans_ready, 4)
            act.activation(q_dec[:], cum[:], ACT.Exp, scale=1 / TAU).then_inc(exps_ready, 1)
            act.activation(k_mid[:], q_mid[:], ACT.Exp, scale=-1 / TAU).then_inc(exps_ready, 1)
            act.wait_ge(exps_ready, 2)
            act.activation(q_mid[:], q_mid[:], ACT.Exp, scale=1 / TAU).then_inc(exps_ready, 1)
            act.activation(k_dec[:], k_dec[:], ACT.Exp, scale=1 / TAU).then_inc(exps_ready, 1)
            with repeat(act, KE // 2, {}) as i:
                for b in range(2):
                    split_hi(S_V + b, i)

            def sigmoid(s):
                act.wait_ge(acc_read, s + 1)
                sig_t.up(act.activation(sig[:, s % 2, :], tmp[:, s % 2, :], ACT.Sigmoid))

            def copy_banks(dst, banks, rows, done):
                for c, b in enumerate(banks):
                    act.activation(dst[:, 512 * c:512 * c + 512], bank[b][0:rows, :], ACT.Copy).then_inc(done, 1)

            for t, s in enumerate(range(S_ZB, S_VA)):
                split_hi(s)
                sigmoid(s)
                if t == 0:
                    act.wait_ge(att_done, 1)
                    act.wait_ge(att_masked, 3)
                    for sub in range(2):
                        r0, r1 = 2 * BLK * sub, 2 * BLK * sub + BLK
                        part = bank[6][:, :].rearrange("p (c h t) -> p c h t", c=2, h=HB)
                        for c, dst in enumerate((att0, att1)):
                            act.activation(dst[r0:r1, :, r1:r1 + BLK], part[r0:r1, c, :, BLK * sub:BLK * sub + BLK],
                                           ACT.Copy).then_inc(att_copied, 1)
                    part = bank[7][:, :].rearrange("p (c h t) -> p c h t", c=2, h=HB)
                    for c, dst in enumerate((att0, att1)):
                        act.activation(dst[0:64, :, 64:P], part[0:64, c, :, :], ACT.Copy).then_inc(att_copied, 1)
                    act.activation(att0[:, :, P:SEQ], bank[2][:, :].rearrange("p (h t) -> p h t", h=HB), ACT.Copy)\
                       .then_inc(att_copied, 1)
                if t == 1:
                    v_new = v_sb[:, :, SEQ:T].rearrange("p i (b t) -> p i b t", t=DEC_L)
                    k_new = k_dec[:, :, SEQ:T].rearrange("p i (b t) -> p i b t", t=DEC_L)
                    for n in (0, 2):
                        act.activation(v_x[:, :, :, n, :].bitcast(F32R), v_new, ACT.Copy).then_inc(x_hi_parts, 1)
                    for n in (0, 1):
                        act.activation(k_x[:, :, :, n, :].bitcast(F32R), k_new, ACT.Copy).then_inc(x_hi_parts, 1)
                    act.wait_ge(kdt_done, 1)
                    copy_banks(kd_t[:].rearrange("p c n -> p (c n)"), (4, 5), P, kdt_copied)
                if 2 <= t <= 4:
                    act.wait_ge(vt_done, t - 1)
                    copy_banks(*((v_t[:, t - 2, :], VT_BANKS[t - 2], P) if t < 4 else (v_ts[:, :], VT_BANKS[2], DEC)),
                               vt_copied)
                if t == 5:
                    act.wait_ge(xt_done, 1)
                    copy_banks(vx_t[:].rearrange("p g n -> p (g n)"), (4, 5, 6, 7), P, xt_copied)
                if t == 6:
                    act.wait_ge(xt_done, 2)
                    copy_banks(kx_t[:].rearrange("p g n -> p (g n)"), (2, 3), P, xt_copied)
                    act.wait_ge(ps_done, 1)
                    copy_banks(st[:].rearrange("p h n -> p (h n)"), (4, 5), P, ps_copied)
                    act.wait_ge(ps_copied, 2)
                    act.dma_start(O["st_prompt"].rearrange("h d v -> d h v"), st[:]).then_inc(st_stored, 16)
                if t == 7:
                    copy_o_prompt(0)

            def root_o(h):
                root(3 + h, r_o[:, h, :], r_o[:, h, :])

            def load_s0(b):
                act.dma_start(s0[:, b % 4], A["s0"][b].rearrange("h d v -> d h v")).then_inc(s0_loaded[b % 4], 16)

            def finish(b):
                act.wait_ge(st_ready, HB * (b + 1))
                act.dma_start(O["st_dec"][b].rearrange("h d v -> d h v"), s0[:, b % 4]).then_inc(s0_stored[b % 4], 16)

            def old_state_hi(b):
                act.wait_ge(s0_loaded[b % 4], 16 * (b // 4 + 1))
                act.wait_ge(q_zeroed, 1)
                if b:
                    act.wait_ge(oq_done, b)
                act.activation(s0_hi[:], s0[:, b % 4], ACT.Copy).then_inc(old_hi, 1)
                q_b = q_dec[:, :, SEQ + DEC_L * b:SEQ + DEC_L * b + DEC_L]
                act.activation(q_x[:, :, QW:QW + DEC_L], q_b, ACT.Copy).then_inc(old_hi, 1)

            for c, s in enumerate(range(S_VA, S_ZA)):
                if c:
                    old_state_hi(c - 1)
                split_hi(s)
                if c == 0:
                    copy_o_prompt(1)
                    for b in range(4):
                        load_s0(b)
                if c >= 2:
                    finish(c - 2)
                if 3 <= c < 7:
                    act.wait_ge(s0_stored[c - 3], 16)
                    load_s0(c + 1)

            for b, s in enumerate(range(S_ZA, S_U)):
                if b == 0:
                    old_state_hi(DEC_B - 1)
                split_hi(s)
                if b == 0:
                    root(2, tmp[:, 2, :], tmp[:, 2, :])
                sigmoid(s)
                if b == 0:
                    finish(6)
                    act.wait_ge(oq_done, DEC_B)
                    copy_banks(oq, (2, 3), P, oq_copied)
                if b == 1:
                    act.wait_ge(o_done, 1)
                    act.activation(o_sb[:, :, SEQ:T], bank[6][:, :].rearrange("p (i t) -> p i t", t=DEC),
                                   ACT.Copy).then_inc(o_copied, 1)
                if b == 1:
                    finish(7)
                    act.wait_ge(va_normed, KE)
                    act.dma_start(O["cv"].rearrange("i p t -> p i t"), va_sb[:, :, SEQ:T]).then_inc(cv_stored, 16)
                if b == 2:
                    for t in range(2):
                        act.wait_ge(vat_done, t + 1)
                        copy_banks(va_t[:, t, :], VAT_BANKS[t], P, vat_copied)
                if b == 3:
                    act.wait_ge(vat_done, 3)
                    copy_banks(va_ts[:, :], VAT_BANKS[2], DEC, vat_copied)
                if s in O_NORM:
                    root_o(O_NORM.index(s))

            act.wait_ge(st_stored, 16)
            for q in range(4):
                act.wait_ge(s0_stored[q], 32)
            for j, s in enumerate(range(S_U, S_GATE)):
                split_hi(s)
                act.wait_ge(y_full, j + 1)
                act.activation(yhi[0][:, j, :], tmp[:, 2 + j % 2, :], ACT.Copy).then_inc(y_rounded, 1)
                act.wait_ge(yb_full, j + 1)
                act.activation(yhi[1][:, j, :], o_sb[:, j, :], ACT.Copy, scale=col(C_GO, j)).then_inc(y_rounded, 1)
                if s in O_NORM:
                    root_o(O_NORM.index(s))

            with repeat(act, KX // 2, {sig_t: 4, m_full_t: 2}) as i:
                for b in range(2):
                    for g in range(3):
                        n = 3 * b + g
                        for half in range(2):
                            q = 2 * (n % 2) + half
                            turn = 16 * ((S_GATE + n + 2) // 2 + 1)
                            used = 2 * (S_GATE + n + 2) + half - 3
                            act.wait_ge(raw_loaded[q], 48 * i + turn)
                            act.wait_ge(units_used, 12 * i + used)
                            act.activation(whi[:, q], raw[:, q], ACT.Copy).then_inc(hi_ready, 1)
                        if g < 2:
                            act.wait_ge(acc_read, 6 * i + (S_GATE + n + 1))
                            sig_t.up(act.activation(sig[:, g, :], tmp[:, g, :], ACT.Sigmoid))
                        else:
                            m_full_t.next(act)
                            act.activation(mhi[:, 2 * i + b, :], tmp[:, 2, :], ACT.Copy).then_inc(m_rounded, 1)

            act.wait_ge(units_used, 2 * S_WO)
            act.dma_start(p_raw[:], A["p_t"]).then_inc(p_loaded, 16)
            for c in range(4):
                act.dma_start(h_sb[:, 4 * c:4 * c + 4, :], A["x_t"][:, 4 * c:4 * c + 4, :]).then_inc(xr_loaded[c], 16)
            for b in range(2):
                split_hi(S_WO + b)
            act.wait_ge(p_loaded, 16)
            act.activation(p_hi[:], p_raw[:], ACT.Copy).then_inc(p_rounded, 1)
            with repeat(act, KX // 2 - 1, {}) as i:
                for b in range(2):
                    split_hi(S_WO + 2 + b, i)
            act.activation(small["warm"][0:1, 0:1], par[0:1, 0:1], ACT.Sqrt, scale=0.0)\
               .then_inc(tables_loaded, 1)
            root(3 + HB, r_tok[:, :], r_tok[:, :])
            for n in range(4):
                act.wait_ge(units_used, 2 * S_PE + n + 1)
                for c in range(4):
                    act.activation(pe_out[:, 4 * n + c, :], bank[PE_BANKS[n][c]][:, 0:T], ACT.Copy).then_inc(pe_read, 1)
                act.wait_ge(raw_loaded[n], 16 * (S_PG // 2 + 1))
                act.activation(whi[:, n], raw[:, n], ACT.Copy).then_inc(hi_ready, 1)
                for k in range(H_WITH[n], H_WITH[n + 1]):
                    act.wait_ge(h_full, k + 1)
                    act.activation(mhi[:, k, :], h_sb[:, k, :], ACT.Copy).then_inc(h_rounded, 1)

            def last_gate(s, b, i=None, used=None, at_=None):
                used = used or 2 * s + 2
                if s >= S_PG + 2:
                    n = S_PE + s - S_PG - 1
                    act.wait_ge(acc_read, n if i is None else 2 * i + n)
                act.wait_ge(units_used, used if i is None else 4 * i + used)
                sig_t.up(act.activation(sig[:, b, :], bank[at_ or b][:, 0:T], ACT.Sigmoid))

            def store(j):
                out_t.next(act)
                act.dma_start(O["y"][:, j, :], pe_out[:, j, :]).then_inc(out_stored, 16)

            for j in range(2):
                split_hi(S_PG + j)
                last_gate(S_PG + j, j, used=2 * S_PG + 3 + j, at_=PG_BANKS[j])
            with repeat(act, KX // 2 - 2, {sig_t: 2, out_t: 2}) as i:
                for b in range(2):
                    split_hi(S_PG + 2 + b, i)
                    last_gate(S_PG + 2 + b, b, i)
                    store(2 * i + b)
            for j in range(KX - 2, KX):
                last_gate(S_PG + j, j % 2)
                store(j - 2)
            store(KX - 2)
            store(KX - 1)
            act.wait_ge(out_stored, 16 * KX)
            act.wait_ge(cv_stored, 16)

        @block.vector
        def _(dve):
            own = Tally(dve_own)
            acc_t = Tally(acc_read)
            sig_t = Tally(sig_done, 2 * KE)
            m_full_t, m_round_t = Tally(m_full), Tally(m_rounded)
            out_t = Tally(out_ready)
            st_t = Tally(st_ready)

            def then(ins):
                own.up(ins)
                dve.wait_ge(dve_own, own.value)

            def low(q, ready, used):
                dve.wait_ge(hi_ready, ready)
                dve.wait_ge(units_used, used)
                dve.tensor_tensor(wlo[:, q], raw[:, q], whi[:, q].bitcast(F32), ALU.subtract).then_inc(lo_ready, 1)

            def split_lo(s, i=None):
                for half in range(2):
                    u = 2 * (s + 2) + half
                    low(2 * (s % 2) + half, *((u + 1, u - 3) if i is None else (4 * i + (u + 1), 4 * i + (u - 3))))

            def sums(s, i=None, by=4):
                dve.wait_ge(units_used, 2 * s + 2 if i is None else by * i + (2 * s + 2))

            def variance(out, src, n):
                then(dve.tensor_scalar(out, src, 1.0 / n, EPS, ALU.mult, ALU.add))
                dve.reciprocal(out, out).then_inc(var_ready, 1)

            dve.wait_ge(par_loaded, 16)
            for k in range(KX):
                if k == XB:
                    dve.wait_ge(alr_hi, 1)
                    dve.tensor_tensor(wr[:, :, RANK:2 * RANK], wr_raw[:], wr[:, :, 0:RANK].bitcast(F32),
                                      ALU.subtract).then_inc(alr_lo, 1)
                dve.wait_ge(x_rounded, k + 1)
                dve.scalar_tensor_tensor(xlo[:, k, :], x_sb[:, k, :], col(C_GPRE, k), xhi[:, k, :].bitcast(F32),
                                         ALU.mult, ALU.subtract).then_inc(x_split, 1)
                if k % 8 == 7:
                    for q in (k // 8 * 2, k // 8 * 2 + 1):
                        dve.wait_ge(hi_ready, q + 1)
                        dve.tensor_tensor(wlo[:, q], raw[:, q], whi[:, q].bitcast(F32), ALU.subtract)\
                           .then_inc(lo_ready, 1)
            dve.wait_ge(consts_loaded, 16 * 6)

            r = r_tok[:, :]
            for s in range(S_K, S_V):
                split_lo(s)
                if s == S_K:
                    continue
                if s == S_K + 1:
                    dve.wait_ge(sum_done, 1)
                    variance(tmp[:, 0, :], bank[5][:, 0:T], D)
                    dve.wait_ge(r_ready, 1)
                    dve.wait_ge(alr_done, 1)
                    dve.tensor_tensor(alr[:, :], bank[4][0:2 * RANK, 0:T], r_tok[0:2 * RANK, :], ALU.mult)\
                       .then_inc(alr_ready, 1)
                    sums(s)
                    for k in range(2):
                        acc_t.up(dve.tensor_tensor(k_sb[:, k, :], bank[k][:, 0:T], r, ALU.mult))
                elif s < S_Q:
                    sums(s)
                    acc_t.up(dve.tensor_tensor(k_sb[:, s - S_K, :], bank[s][:, 0:T], r, ALU.mult))
                else:
                    sums(s)
                    acc_t.up(dve.scalar_tensor_tensor(q_sb[:, s - S_Q, :], bank[s % 2][:, 0:T], float(DK) ** -0.5, r,
                                                      ALU.mult, ALU.mult))
                if s == S_K + 3:
                    dve.wait_ge(logits_done, 1)
                    for h in range(HB):
                        own.up(dve.tensor_scalar(k_dec[:, h, :], bank[4 + h][:, 0:T], col(C_BA, h), None, ALU.add))
                    dve.wait_ge(dve_own, own.value)
                    dve.scalar_tensor_tensor(cum[:], k_dec[:], -1.0, k_dec[:], ALU.mult, ALU.min)\
                       .then_inc(absneg_ready, 1)
                if s == S_Q + 1:
                    dve.wait_ge(softplus_ready, 1)
                    then(dve.scalar_tensor_tensor(k_dec[:], k_dec[:], 0.0, cum[:], ALU.min, ALU.subtract))
                    for h in range(HB):
                        own.up(dve.tensor_tensor_scan(cum[:, h, :], con[:, C_RESET:C_RESET + T], k_dec[:, h, :], 0.0,
                                                      ALU.mult, ALU.add))
                    dve.wait_ge(dve_own, own.value)
                if s == S_Q + 2:
                    prompt = [x[:, :, 0:SEQ].rearrange("p h (c t) -> p h c t", t=BLK) for x in (cum, q_mid, k_dec)]
                    dec = [x[:, :, SEQ:T].rearrange("p h (c t) -> p h c t", t=DEC_L) for x in (cum, k_dec)]
                    mid = prompt[0][:, :, :, MID:MID + 1].to_broadcast([P, HB, NBLK, BLK])
                    end = prompt[0][:, :, :, BLK - 1:BLK].to_broadcast([P, HB, NBLK, BLK])
                    end_d = dec[0][:, :, :, DEC_L - 1:DEC_L].to_broadcast([P, HB, DEC_B, DEC_L])
                    dve.tensor_tensor(prompt[1], prompt[0], mid, ALU.subtract).then_inc(spans_ready, 1)
                    dve.tensor_copy(q_mid[:, :, SEQ:T], cum[:, :, SEQ:T]).then_inc(spans_ready, 1)
                    dve.tensor_tensor(prompt[2], end, prompt[0], ALU.subtract).then_inc(spans_ready, 1)
                    dve.tensor_tensor(dec[1], end_d, dec[0], ALU.subtract).then_inc(spans_ready, 1)
            dve.wait_ge(exps_ready, 4)
            ends = q_dec[:, :, 0:SEQ].rearrange("p h (c t) -> p h c t", t=BLK)[:, :, :, BLK - 1]
            ends_d = q_dec[:, :, SEQ:T].rearrange("p h (c t) -> p h c t", t=DEC_L)[:, :, :, DEC_L - 1]
            then(dve.tensor_copy(decays[:, :, 0:NBLK], ends))
            then(dve.tensor_tensor(decays[:, :, D64:D64 + 4], decays[:, :, 0:NBLK:2], decays[:, :, 1:NBLK:2], ALU.mult))
            dve.tensor_tensor(decays[:, :, D128:D128 + 1], decays[:, :, D64 + 2:D64 + 3],
                              decays[:, :, D64 + 3:D64 + 4], ALU.mult).then_inc(decays_kept, 1)
            dve.tensor_copy(decays[:, :, DDEC:DDEC + DEC_B], ends_d).then_inc(decays_kept, 1)
            with repeat(dve, KE // 2, {acc_t: 2}) as i:
                for b in range(2):
                    split_lo(S_V + b, i)
                    sums(S_V + b, i)
                    acc_t.up(dve.tensor_tensor(v_sb[:, 2 * i + b, :], bank[b][:, 0:T], r, ALU.mult))

            def gate_input(s, n):
                sums(s)
                if n >= 2:
                    dve.wait_ge(gate_ready, n - 1)
                acc_t.up(dve.tensor_tensor(tmp[:, s % 2, :], bank[s % 2][:, 0:T], r, ALU.mult))

            for t, s in enumerate(range(S_ZB, S_VA)):
                split_lo(s)
                gate_input(s, t)
                if t == 0:
                    dve.wait_ge(att_zeroed, 3)
                    dve.wait_ge(att_done, 1)
                    mask = con[:, C_ATT:C_ATT + P].bitcast(I32)
                    for c, dst in enumerate((att0, att1)):
                        for h in range(HB):
                            last = dve.copy_predicated(dst[:, h, 0:P], mask, bank[4 + c][:, P * h:P * h + P])
                        last.then_inc(att_masked, 1)
                    mask = con[0:DEC, C_ATS:C_ATS + DEC].bitcast(I32)
                    for h in range(HB):
                        last = dve.copy_predicated(att_s[:, h, :], mask, bank[3][0:DEC, DEC * h:DEC * h + DEC])
                    last.then_inc(att_masked, 1)
                if t == 1:
                    dve.wait_ge(x_hi_parts, 4)
                    v_new = v_sb[:, :, SEQ:T].rearrange("p i (b t) -> p i b t", t=DEC_L)
                    k_new = k_dec[:, :, SEQ:T].rearrange("p i (b t) -> p i b t", t=DEC_L)
                    for n in (1, 3):
                        dve.tensor_tensor(v_x[:, :, :, n, :].bitcast(F32R), v_new, v_x[:, :, :, 0, :], ALU.subtract)\
                           .then_inc(x_lo_parts, 1)
                    for n in (2, 3):
                        dve.tensor_tensor(k_x[:, :, :, n, :].bitcast(F32R), k_new, k_x[:, :, :, 0, :], ALU.subtract)\
                           .then_inc(x_lo_parts, 1)

            def variance_o(h):
                dve.wait_ge(sum_done, 3)
                variance(r_o[:, h, :], bank[4 + h][:, 0:T], DV)

            def new_state(b):
                dve.wait_ge(kv_done, b + 1)
                dve.wait_ge(old_lo, 2 * b + 2)
                for h in range(HB):
                    kv = bank[4 + h // 2][:, DV * (h % 2):DV * (h % 2) + DV]
                    st_t.up(dve.scalar_tensor_tensor(s0[:, b % 4, h, :], s0[:, b % 4, h, :],
                                                     decays[:, h, DDEC + b:DDEC + b + 1], kv, ALU.mult, ALU.add))

            def old_state_lo(b):
                dve.wait_ge(old_hi, 2 * b + 2)
                dve.tensor_tensor(s0_lo[:], s0[:, b % 4], s0_hi[:].bitcast(F32), ALU.subtract).then_inc(old_lo, 1)
                dve.tensor_tensor(q_x[:, :, QW + DEC_L:P], q_dec[:, :, SEQ + DEC_L * b:SEQ + DEC_L * b + DEC_L],
                                  q_x[:, :, QW:QW + DEC_L].bitcast(F32), ALU.subtract).then_inc(old_lo, 1)

            for c, s in enumerate(range(S_VA, S_ZA)):
                if c:
                    old_state_lo(c - 1)
                split_lo(s)
                sums(s)
                acc_t.up(dve.tensor_tensor(va_sb[:, c, :], bank[s % 2][:, 0:T], r, ALU.mult))
                if c:
                    new_state(c - 1)

            for b, s in enumerate(range(S_ZA, S_U)):
                if b == 0:
                    old_state_lo(DEC_B - 1)
                split_lo(s)
                if b == 0:
                    dve.wait_ge(sum_done, 2)
                    variance(tmp[:, 2, :], bank[7][:, 0:T], EA)
                gate_input(s, KE + b)
                if b == 0:
                    new_state(DEC_B - 1)
                if s in O_NORM:
                    variance_o(O_NORM.index(s))
                if b == 0:
                    dve.wait_ge(r_ready, 2)
                    for i in range(KE):
                        dve.scalar_tensor_tensor(va_sb[:, i, :], va_sb[:, i, :], col(C_GV, i), tmp[:, 2, :],
                                                 ALU.mult, ALU.mult).then_inc(va_normed, 1)
                if b >= 4:
                    dve.wait_ge(sp_done, b - 3)
                    if b == 4:
                        dve.wait_ge(cv_stored, 16)
                    for c in range(2):
                        i = 2 * (b - 4) + c
                        h = i // 2
                        dve.tensor_tensor(sp_sb[:, i, 0:SEQ].rearrange("p (c t) -> p c t", t=CHUNK),
                                          bank[2 + c][:, 0:SEQ].rearrange("p (c t) -> p c t", t=CHUNK),
                                          bs[:, h:h + 1, :].to_broadcast([P, 2, CHUNK]), ALU.add).then_inc(sp_read, 1)
                        dve.tensor_tensor(sp_sb[:, i, SEQ:T].rearrange("p (c t) -> p c t", t=DEC_L),
                                          bank[2 + c][:, SEQ:T].rearrange("p (c t) -> p c t", t=DEC_L),
                                          bs[:, h:h + 1, 0:DEC_L].to_broadcast([P, DEC_B, DEC_L]), ALU.add)\
                           .then_inc(sp_read, 1)

            def y_low(j):
                dve.wait_ge(y_rounded, 2 * j + 1)
                dve.tensor_tensor(ylo[0][:, j, :], tmp[:, 2 + j % 2, :], yhi[0][:, j, :].bitcast(F32), ALU.subtract)\
                   .then_inc(y_split, 1)
                dve.wait_ge(y_rounded, 2 * j + 2)
                dve.scalar_tensor_tensor(ylo[1][:, j, :], o_sb[:, j, :], col(C_GO, j), yhi[1][:, j, :].bitcast(F32),
                                         ALU.mult, ALU.subtract).then_inc(y_split, 1)

            dve.wait_ge(gate_ready, 2 * KE)
            for j, s in enumerate(range(S_U, S_GATE)):
                split_lo(s)
                if s in O_NORM:
                    variance_o(O_NORM.index(s))
                sums(s)
                if j >= 2:
                    dve.wait_ge(y_full, j - 1)
                acc_t.up(dve.tensor_tensor(tmp[:, j % 2, :], bank[s % 2][:, 0:T], r, ALU.mult))
                dve.wait_ge(branch_gated, j + 1)
                if j >= 2:
                    dve.wait_ge(y_split, 2 * j - 2)
                dve.wait_ge(acc_read, acc_t.value)
                dve.tensor_tensor(tmp[:, 2 + j % 2, :], tmp[:, j % 2, :], za_gate[:, j, :], ALU.mult)\
                   .then_inc(y_full, 1)
                if j:
                    y_low(j - 1)
            y_low(KE - 1)
            dve.wait_ge(y_full, KE)
            dve.wait_ge(y_split, 2 * KE)

            with repeat(dve, KX // 2, {acc_t: 6, sig_t: 4, own: 2, m_full_t: 2, m_round_t: 2}) as i:
                for b in range(2):
                    for g in range(3):
                        n = 3 * b + g
                        for half in range(2):
                            u = 2 * (S_GATE + n + 2) + half
                            low(2 * (n % 2) + half, 12 * i + (u + 1), 12 * i + (u - 3))
                        sums(S_GATE + n, i, 12)
                        if g < 2:
                            acc_t.up(dve.tensor_tensor(tmp[:, g, :], bank[n % 2][:, 0:T], r, ALU.mult))
                    sig_t.next(dve, 2)
                    own.up(dve.tensor_tensor(tmp[:, 2, :], bank[2][:, 0:T], sig[:, 0, :], ALU.mult))
                    acc_t.up(dve.tensor_tensor(tmp[:, 3, :], bank[3][:, 0:T], sig[:, 1, :], ALU.mult))
                    dve.wait_ge(acc_read, acc_t.value)
                    m_full_t.up(dve.tensor_tensor(tmp[:, 2, :], tmp[:, 2, :], tmp[:, 3, :], ALU.add))
                    m_round_t.next(dve)
                    dve.tensor_tensor(mlo[:, 2 * i + b, :], tmp[:, 2, :], mhi[:, 2 * i + b, :].bitcast(F32),
                                      ALU.subtract).then_inc(m_split, 1)
                    dve.wait_ge(m_split, 2 * i + (b + 1))

            def wo_sums(s, i=None, j=None):
                u = 2 * (s + 2)
                q = 2 * (s % 2)
                low(q, *((u + 1, u - 3) if i is None else (4 * i + (u + 1), 4 * i + (u - 3))))
                sums(s, i)
                acc_t.up(dve.tensor_copy(mo_sb[:, j, :], bank[s % 2][:, 0:T]))
                if s != S_WO + KX - 1:
                    low(q + 1, *((u + 2, u - 2) if i is None else (4 * i + (u + 2), 4 * i + (u - 2))))

            for b in range(2):
                wo_sums(S_WO + b, None, b)
            dve.wait_ge(p_rounded, 1)
            dve.tensor_tensor(p_lo[:], p_raw[:], p_hi[:].bitcast(F32), ALU.subtract).then_inc(p_split, 1)
            with repeat(dve, KX // 2 - 2, {acc_t: 2}) as i:
                for b in range(2):
                    wo_sums(S_WO + 2 + b, i, 2 * i + (2 + b))
            for b in range(2):
                wo_sums(S_WO + KX - 2 + b, None, KX - 2 + b)
            dve.wait_ge(acc_read, acc_t.value)
            dve.tensor_tensor(tmp[:, 0, :], mo_sb[:, KX - 1, :], mo_sb[:, KX - 1, :], ALU.mult).then_inc(sum_last, 1)
            low(3, 2 * S_PE + 4, 2 * S_PE)
            dve.wait_ge(sum_done, 4)
            variance(r_tok[:, :], bank[NORM_BANK][:, 0:T], D)
            AHEAD = 5

            def h_norm(k):
                dve.scalar_tensor_tensor(mo_sb[:, k, :], mo_sb[:, k, :], col(C_GPOST, k), r, ALU.mult, ALU.mult)\
                   .then_inc(hn_ready, 1)

            for n in range(4):
                if n == 0:
                    dve.wait_ge(r_ready, 3 + HB)
                    dve.wait_ge(sum_last, 1)
                    for k in range(AHEAD):
                        h_norm(k)
                low(n, 2 * S_PG + n + 1, 2 * S_PE + n + 1)
                for k in range(H_WITH[n], H_WITH[n + 1]):
                    if k + AHEAD < KX:
                        h_norm(k + AHEAD)
                    dve.wait_ge(h_rounded, k + 1)
                    dve.tensor_tensor(mlo[:, k, :], h_sb[:, k, :], mhi[:, k, :].bitcast(F32), ALU.subtract)\
                       .then_inc(h_split, 1)

            def output(j, b):
                sig_t.next(dve)
                acc_t.up(dve.tensor_tensor(tmp[:, b, :], sig[:, b, :], pe_out[:, j, :], ALU.mult))
                dve.wait_ge(acc_read, acc_t.value)
                out_t.up(dve.tensor_tensor(pe_out[:, j, :], tmp[:, b, :], h_sb[:, j, :], ALU.add))
                dve.wait_ge(out_ready, out_t.value)

            for j in range(2):
                split_lo(S_PG + j)
                output(j, j)
            with repeat(dve, KX // 2 - 2, {sig_t: 2, acc_t: 2, out_t: 2}) as i:
                for b in range(2):
                    split_lo(S_PG + 2 + b, i)
                    output(2 * i + (b + 2), b)
            for j in range(KX - 2, KX):
                output(j, j % 2)

        @block.gpsimd
        def _(pool):
            own = Tally(pool_own)

            def then(ins):
                own.up(ins)
                pool.wait_ge(pool_own, own.value)

            for x in (att1, att0, att_s):
                pool.memset(x[:], 0.0).then_inc(att_zeroed, 1)
            for c in range(2):
                if c == 0:
                    for n in range(XC // 2):
                        pool.wait_ge(x_loaded[n], 16)
                    then(pool.tensor_tensor(squares[:, 0:8, :], x_sb[:, 0:8, :], x_sb[:, 0:8, :], ALU.mult))
                else:
                    pool.wait_ge(squared, 1)
                for w in (4, 2):
                    a = 8 * c
                    then(pool.tensor_tensor(squares[:, a:a + w, :], squares[:, a:a + w, :],
                                            squares[:, a + w:a + 2 * w, :], ALU.add))
            pool.tensor_tensor(squares[:, 0:2, :], squares[:, 0:2, :], squares[:, 8:10, :], ALU.add)\
                .then_inc(sq_ready, 1)
            pool.wait_ge(consts_loaded, 16 * 6)
            for w, n in ((wst, CHUNK), (wsb, DEC)):
                pool.affine_select(out=w[:], in_=w[:], compare_op=ALU.is_ge, fill=0.0, base=0,
                                   pattern=[[0, HA], [1, n]], channel_multiplier=-1).then_inc(ws_masked, 1)
            pool.wait_ge(acc_read, S_V)
            pool.wait_ge(decays_kept, 2)
            for x, y in ((k_dec, k_sb), (q_dec, q_sb), (k_mid, k_sb), (q_mid, q_sb)):
                pool.tensor_tensor(x[:], x[:], y[:], ALU.mult).then_inc(gla_in, 1)
            blk_k = k_dec[:, :, 0:SEQ].rearrange("p h (c t) -> p h c t", t=BLK)
            blk_q = q_dec[:, :, 0:SEQ].rearrange("p h (c t) -> p h c t", t=BLK)

            def decayed(out, x, d0, d1=None, step=1, positions=BLK):
                if d0 is None:
                    return pool.tensor_copy(out, x)
                n = 1 if d1 is None else len(range(d0, d1, step))
                by = decays[:, :, d0:(d0 + 1 if d1 is None else d1):step]
                if n == 1:
                    return pool.tensor_tensor(out, x, by.to_broadcast([P, HB, positions]), ALU.mult)
                by = by.rearrange("p h (c o) -> p h c o", o=1).to_broadcast([P, HB, n, positions])
                return pool.tensor_tensor(out, x, by, ALU.mult)

            pool.wait_ge(gla_in, 4)
            then(decayed(q_64[:, :, :, 0:BLK], blk_q[:, :, 2::4, :], None))
            then(decayed(q_64[:, :, :, BLK:2 * BLK], blk_q[:, :, 3::4, :], 2, NBLK, 4))
            then(decayed(k_64[:, :, :, 0:BLK], blk_k[:, :, 0::4, :], 1, NBLK, 4))
            then(decayed(k_64[:, :, :, BLK:2 * BLK], blk_k[:, :, 1::4, :], None))
            then(decayed(q_128[:, :, 0:BLK], blk_q[:, :, 4, :], None))
            then(decayed(q_128[:, :, BLK:2 * BLK], blk_q[:, :, 5, :], 4))
            then(decayed(q_128[:, :, 2 * BLK:P], q_64[:, :, 1, :], D64 + 2, positions=64))
            then(decayed(k_128[:, :, 0:2 * BLK], k_64[:, :, 0, :], D64 + 1, positions=64))
            then(decayed(k_128[:, :, 2 * BLK:3 * BLK], blk_k[:, :, 2, :], 3))
            then(decayed(k_128[:, :, 3 * BLK:P], blk_k[:, :, 3, :], None))
            then(decayed(k_256[:, :, 0:P], k_128[:], D128, positions=P))
            then(decayed(k_256[:, :, P:P + 64], k_64[:, :, 1, :], D64 + 3, positions=64))
            then(decayed(k_256[:, :, P + 64:P + 96], blk_k[:, :, 6, :], 7))
            pool.tensor_copy(k_256[:, :, P + 96:SEQ], blk_k[:, :, 7, :]).then_inc(gla_in, 1)

            def add_squares(x, first, last):
                if first:
                    then(pool.tensor_tensor(v_sum[:, :], x, x, ALU.mult))
                else:
                    then(pool.tensor_tensor(v_sq[:, :], x, x, ALU.mult))
                    add = pool.tensor_tensor(v_sum[:, :], v_sum[:, :], v_sq[:, :], ALU.add)
                    if last:
                        add.then_inc(sq_ready, 1)
                    else:
                        then(add)

            def gate(n, out):
                pool.wait_ge(sig_done, n + 1)
                pool.tensor_tensor(out, tmp[:, n % 2, :], sig[:, n % 2, :], ALU.mult).then_inc(gate_ready, 1)

            for t in range(KE):
                gate(t, zb_gate[:, t, :])
                if t == 0:
                    pool.wait_ge(att_done, 1)
                    pool.memset(q_x[:].bitcast(F32), 0.0).then_inc(q_zeroed, 1)
            for c in range(KE):
                pool.wait_ge(acc_read, S_VA + c + 1)
                add_squares(va_sb[:, c, :], c == 0, c == KE - 1)
            for b in range(KE):
                gate(KE + b, za_gate[:, b, :])
                if b == 1:
                    pool.wait_ge(o_copied, 1)
                    pool.wait_ge(st_stored, 16)
                if 1 <= b <= 2:
                    for h in (2 * b - 2, 2 * b - 1):
                        o_h = o_sb[:, 2 * h:2 * h + 2, :]
                        then(pool.tensor_tensor(o_sq[:, h], o_h, o_h, ALU.mult))
                        add = pool.tensor_tensor(o_sum[:, h, :], o_sq[:, h, 0, :], o_sq[:, h, 1, :], ALU.add)
                        add.then_inc(o_squared, 1)
                if b >= 4:
                    pool.wait_ge(sp_read, 4 * (b - 3))
                    pool.wait_ge(gate_ready, KE + b + 1)
                    for i in (2 * b - 8, 2 * b - 7):
                        pool.tensor_tensor(za_gate[:, i, :], za_gate[:, i, :], sp_sb[:, i, :], ALU.mult)\
                            .then_inc(branch_gated, 1)
            for j in range(KE):
                pool.wait_ge(r_ready, 3 + j // 2)
                then(pool.tensor_tensor(o_sb[:, j, :], o_sb[:, j, :], r_o[:, j // 2, :], ALU.mult))
                pool.tensor_tensor(o_sb[:, j, :], o_sb[:, j, :], zb_gate[:, j, :], ALU.mult).then_inc(yb_full, 1)
            pool.wait_ge(acc_read, S_WO + 1)
            then(pool.tensor_tensor(sig[:, 0, :], mo_sb[:, 0, :], mo_sb[:, 0, :], ALU.mult))
            with repeat(pool, KX - 3, {own: 2}) as i:
                pool.wait_ge(acc_read, i + (S_WO + 2))
                then(pool.tensor_tensor(sig[:, 1, :], mo_sb[:, i + 1, :], mo_sb[:, i + 1, :], ALU.mult))
                then(pool.tensor_tensor(sig[:, 0, :], sig[:, 0, :], sig[:, 1, :], ALU.add))
            pool.wait_ge(acc_read, S_WO + KX - 1)
            then(pool.tensor_tensor(sig[:, 1, :], mo_sb[:, KX - 2, :], mo_sb[:, KX - 2, :], ALU.mult))
            pool.tensor_tensor(sig[:, 0, :], sig[:, 0, :], sig[:, 1, :], ALU.add).then_inc(sq_ready, 1)
            for k in range(KX):
                if k % 4 == 0:
                    pool.wait_ge(xr_loaded[k // 4], 16)
                pool.wait_ge(hn_ready, k + 1)
                pool.tensor_tensor(h_sb[:, k, :], h_sb[:, k, :], mo_sb[:, k, :], ALU.add).then_inc(h_full, 1)

        @block.tensor
        def _(pe):
            def product(acc, q, hi, lo, k0, first, last, used=True, wait_k=None):
                for k in range(UK):
                    if wait_k is not None:
                        pe.wait_ge(wait_k, k0 + k + 1)
                    h, l = whi[:, q, k, :], wlo[:, q, k, :]
                    pe.matmul(acc, h, hi[:, k0 + k, :], start=first and k == 0, stop=False)
                    pe.matmul(acc, h, lo[:, k0 + k, :], start=False, stop=False)
                    m = pe.matmul(acc, l, hi[:, k0 + k, :], start=False, stop=last and k == UK - 1)
                m.then_inc(units_used, 1)

            def ready(u, i=None, by=4):
                pe.wait_ge(lo_ready, u + 1 if i is None else by * i + (u + 1))

            def step(s, hi, lo, i=None, by=2, free=None, wait_k=None, acc=None):
                if free is not False:
                    n = s - 1 if free is None else free
                    pe.wait_ge(acc_read, n if i is None else by * i + n)
                acc = acc or bank[s % 2]
                for half in range(2):
                    ready(2 * s + half, i, 2 * by)
                    product(acc[:, 0:T], 2 * (s % 2) + half, hi, lo, UK * half, half == 0, half == 1,
                            wait_k=wait_k)

            def sum_partitions(acc, x):
                return pe.matmul(acc, ones, x, start=True, stop=True)

            def three(acc, h, l, hi, lo, first, last):
                pe.matmul(acc, h, hi, start=first, stop=False)
                pe.matmul(acc, h, lo, start=False, stop=False)
                return pe.matmul(acc, l, hi, start=False, stop=last)

            pe.wait_ge(alr_lo, 1)
            for half in range(2):
                for k in range(UK * half, UK * half + UK):
                    pe.wait_ge(x_split, k + 1)
                    pe.matmul(bank[4][0:2 * RANK, 0:T], wr[:, k, :], xhi[:, k, :], start=k == 0, stop=False)
                    m = pe.matmul(bank[4][0:2 * RANK, 0:T], wr[:, k, :], xlo[:, k, :], start=False, stop=k == KX - 1)
                if half:
                    m.then_inc(alr_done, 1)
                for b in range(2):
                    ready(2 * half + b)
                    product(bank[b][:, 0:T], 2 * half + b, xhi, xlo, UK * half, half == 0, half == 1)
            pe.wait_ge(consts_loaded, 16 * 6)
            for s in range(S_K + 2, S_V):
                if s == S_K + 2:
                    step(s, xhi, xlo, acc=bank[2], free=False)
                    pe.wait_ge(sq_ready, 1)
                    pe.matmul(bank[5][:, 0:T], ones, squares[:, 0, :], start=True, stop=False)
                    pe.matmul(bank[5][:, 0:T], ones, squares[:, 1, :], start=False, stop=True).then_inc(sum_done, 1)
                elif s == S_K + 3:
                    step(s, xhi, xlo, acc=bank[3], free=False)
                    pe.wait_ge(alr_ready, 1)
                    for h in range(HB):
                        m = pe.matmul(bank[4 + h][:, 0:T], wa2[:, DK * h:DK * h + DK], alr[:, :], start=True, stop=True)
                    m.then_inc(logits_done, 1)
                else:
                    step(s, xhi, xlo)
            with repeat(pe, KE // 2, {}) as i:
                for b in range(2):
                    step(S_V + b, xhi, xlo, i)

            def to_tokens(x, t, banks, done):
                w = P if t < 2 else DEC
                for i in range(KE):
                    m = pe.transpose(bank[banks[i // 4]][0:w, P * (i % 4):P * (i % 4) + P],
                                     x[:, i, P * t:P * t + w], ident)
                m.then_inc(done, 1)

            def stack_rows(x, n, banks):
                for g in range(2):
                    for i in range(n):
                        c = n * g + i
                        m = pe.transpose(bank[banks[c // 4]][:, P * (c % 4):P * (c % 4) + P],
                                         x[:, i, GRP * g:GRP * g + GRP].rearrange("p b n t -> p (b n t)"), ident)
                m.then_inc(xt_done, 1)

            def o_prompt(n):
                for c in range(4):
                    i = 4 * n + c
                    acc = bank[OP_BANKS[n][c // 2]][:, SEQ * (c % 2):SEQ * (c % 2) + SEQ]
                    v0, v1 = (v_t[:, t, P * i:P * i + P] for t in range(2))
                    pe.matmul(acc[:, 0:P], v0, att0[:, i // 2, 0:P], start=True, stop=True)
                    pe.matmul(acc[:, P:SEQ], v0, att0[:, i // 2, P:SEQ], start=True, stop=False)
                    m = pe.matmul(acc[:, P:SEQ], v1, att1[:, i // 2, :], start=False, stop=True)
                m.then_inc(op_done, 1)

            for t, s in enumerate(range(S_ZB, S_VA)):
                step(s, xhi, xlo)
                if t == 0:
                    pe.wait_ge(gla_in, 5)
                    for c in range(2):
                        for h in range(HB):
                            pe.matmul(bank[4 + c][:, P * h:P * h + P], k_mid[:, h, P * c:P * c + P],
                                      q_mid[:, h, P * c:P * c + P], start=True, stop=True)
                    for h in range(HB):
                        pe.matmul(bank[3][0:DEC, DEC * h:DEC * h + DEC], k_mid[:, h, SEQ:T], q_mid[:, h, SEQ:T],
                                  start=True, stop=True)
                    for c in range(2):
                        for h in range(HB):
                            c0 = 64 * (HB * c + h)
                            odd = q_dec[:, h, P * c:P * c + P].rearrange("p (c t) -> p c t", t=BLK)[:, 1::2, :]
                            pe.matmul(bank[6][:, c0:c0 + 64], k_dec[:, h, P * c:P * c + P], odd, start=True, stop=True)
                            pe.matmul(bank[7][0:64, c0:c0 + 64], k_64[:, h, c, :], q_64[:, h, c, :],
                                      start=True, stop=True)
                    for h in range(HB):
                        m = pe.matmul(bank[2][:, P * h:P * h + P], k_128[:, h, :], q_128[:, h, :],
                                      start=True, stop=True)
                    m.then_inc(att_done, 1)
                if t == 1:
                    pe.wait_ge(att_masked, 3)
                    for c in range(2):
                        for h in range(HB):
                            m = pe.transpose(bank[4 + c][:, P * h:P * h + P], k_256[:, h, P * c:P * c + P], ident)
                    m.then_inc(kdt_done, 1)
                if 2 <= t <= 4:
                    pe.wait_ge(att_copied, 7)
                    if t == 4:
                        pe.wait_ge(vt_copied, 2)
                    to_tokens(v_sb, t - 2, VT_BANKS[t - 2], vt_done)
                if t == 5:
                    pe.wait_ge(x_lo_parts, 4)
                    pe.wait_ge(kdt_copied, 2)
                    pe.wait_ge(vt_copied, 6)
                    stack_rows(v_x, KE, (4, 5, 6, 7))
                    stack_rows(k_x, HB, (2, 3))
                if t == 6:
                    pe.wait_ge(xt_copied, 4)
                    for h in range(HB):
                        for c in range(2):
                            m = pe.matmul(bank[4 + h // 2][:, DV * (h % 2):DV * (h % 2) + DV],
                                          kd_t[:, c, DK * h:DK * h + DK], v_t[:, c, DV * h:DV * h + DV],
                                          start=c == 0, stop=c == 1)
                    m.then_inc(ps_done, 1)
                if t == 7:
                    o_prompt(0)

            def sequence(b):
                rows = slice(BLK * (b % GRP), BLK * (b % GRP) + BLK)
                for h in range(HB):
                    m = pe.matmul(bank[4 + h // 2][:, DV * (h % 2):DV * (h % 2) + DV],
                                  kx_t[rows, b // GRP, DK * h:DK * h + DK], vx_t[rows, b // GRP, DV * h:DV * h + DV],
                                  start=True, stop=True)
                m.then_inc(kv_done, 1)
                pe.wait_ge(old_lo, 2 * b + 2)
                for h in range(HB):
                    q_b = q_x[:, h, QW - QR * b:QW - QR * b + P]
                    acc = bank[2 + h // 2][:, DV * (h % 2):DV * (h % 2) + DV]
                    pe.matmul(acc, q_b, s0_hi[:, h, :], start=b == 0 and h % 2 == 0, stop=False, skip_group_check=True)
                    m = pe.matmul(acc, q_b, s0_lo[:, h, :], start=False, stop=b == DEC_B - 1, skip_group_check=True)
                m.then_inc(oq_done, 1)

            for c, s in enumerate(range(S_VA, S_ZA)):
                step(s, xhi, xlo)
                if c == 0:
                    pe.wait_ge(xt_copied, 6)
                    pe.wait_ge(op_copied, 2)
                    o_prompt(1)
                    for i in range(KE):
                        pe.matmul(bank[6][:, DEC * i:DEC * i + DEC], v_ts[:, P * i:P * i + P], att_s[:, i // 2, :],
                                  start=i == 0, stop=False, skip_group_check=True)
                else:
                    if c == 1:
                        pe.wait_ge(ps_copied, 2)
                        pe.wait_ge(op_copied, 4)
                    else:
                        pe.wait_ge(st_ready, HB * (c - 1))
                    sequence(c - 1)

            for b, s in enumerate(range(S_ZA, S_U)):
                step(s, xhi, xlo)
                if b == 0:
                    pe.wait_ge(sq_ready, 2)
                    sum_partitions(bank[7][:, 0:T], v_sum[:, :]).then_inc(sum_done, 1)
                    pe.wait_ge(st_ready, HB * (DEC_B - 1))
                    sequence(DEC_B - 1)
                if b == 1:
                    pe.wait_ge(oq_copied, 2)
                    for i in range(KE):
                        m = pe.matmul(bank[6][:, DEC * i:DEC * i + DEC], oq[:, P * i:P * i + P],
                                      con[:, C_SEL:C_SEL + DEC], start=False, stop=True, skip_group_check=True)
                    m.then_inc(o_done, 1)
                if b == 4:
                    pe.wait_ge(o_squared, HB)
                    pe.wait_ge(vat_copied, 4)
                    for h in range(HB):
                        m = sum_partitions(bank[4 + h][:, 0:T], o_sum[:, h, :])
                    m.then_inc(sum_done, 1)
                if b == 2:
                    pe.wait_ge(va_normed, KE)
                    for t in range(2):
                        if t:
                            pe.wait_ge(o_copied, 1)
                        to_tokens(va_sb, t, VAT_BANKS[t], vat_done)
                if b == 3:
                    pe.wait_ge(vat_copied, 2)
                    to_tokens(va_sb, 2, VAT_BANKS[2], vat_done)
                if b >= 4:
                    if b == 4:
                        pe.wait_ge(vat_copied, 6)
                        pe.wait_ge(ws_masked, 2)
                    else:
                        pe.wait_ge(sp_read, 4 * (b - 4))
                    for c in range(2):
                        i = 2 * (b - 4) + c
                        for t in range(2):
                            pe.matmul(bank[2 + c][:, P * t:P * t + P], va_t[:, t, P * i:P * i + P],
                                      wst[:, i // 2, :], start=True, stop=True)
                        m = pe.matmul(bank[2 + c][:, SEQ:T], va_ts[:, P * i:P * i + P], wsb[:, i // 2, :],
                                      start=True, stop=True)
                    m.then_inc(sp_done, 1)

            for j, s in enumerate(range(S_U, S_GATE)):
                step(s, xhi, xlo)
            with repeat(pe, KX // 2, {}) as i:
                for b in range(2):
                    for g in range(2):
                        step(S_GATE + 3 * b + g, xhi, xlo, i, 6)
                    s = S_GATE + 3 * b + 2
                    pe.wait_ge(y_split, 2 * KE)
                    pe.wait_ge(acc_read, 6 * i + (s - 1))
                    for half in range(2):
                        ready(2 * s + half, i, 12)
                        product(bank[2 + half][:, 0:T], 2 * (s % 2) + half, yhi[half], ylo[half], 0, True, True)
            step(S_WO, mhi, mlo, wait_k=m_split)
            step(S_WO + 1, mhi, mlo)
            with repeat(pe, KX // 2 - 1, {}) as i:
                for b in range(2):
                    step(S_WO + 2 + b, mhi, mlo, i)
            pe.wait_ge(p_split, 1)
            for n in range(4):
                if n == 1:
                    pe.wait_ge(acc_read, S_PE)
                if n >= 2:
                    pe.wait_ge(pe_read, 4 * (n - 1))
                ready(2 * S_PE + n)
                for c in range(4):
                    if n == 0 and c == 2:
                        pe.wait_ge(sq_ready, 3)
                        pe.matmul(bank[NORM_BANK][:, 0:T], ones, sig[:, 0, :], start=True, stop=False)
                        pe.wait_ge(sum_last, 1)
                        pe.matmul(bank[NORM_BANK][:, 0:T], ones, tmp[:, 0, :], start=False, stop=True)\
                          .then_inc(sum_done, 1)
                    if n == 1 and PE_BANKS[n][c] == NORM_BANK:
                        pe.wait_ge(var_ready, 3 + HB)
                    for k in range(PLE // P):
                        m = three(bank[PE_BANKS[n][c]][:, 0:T], whi[:, n, 2 * c + k, :], wlo[:, n, 2 * c + k, :],
                                  p_hi[:, k, :], p_lo[:, k, :], k == 0, k == PLE // P - 1)
                m.then_inc(units_used, 1)
            pe.wait_ge(pe_read, 12)
            for half in range(2):
                ready(2 * S_PG + 2 * half + 1)
                for k in range(UK):
                    n = UK * half + k
                    pe.wait_ge(h_split, n + 1)
                    for b in range(2):
                        m = three(bank[PG_BANKS[b]][:, 0:T], whi[:, 2 * half + b, k, :], wlo[:, 2 * half + b, k, :],
                                  mhi[:, n, :], mlo[:, n, :], n == 0, n == KX - 1)
                        if k == UK - 1:
                            m.then_inc(units_used, 1)
            pe.wait_ge(pe_read, 16)
            for b in range(2):
                step(S_PG + 2 + b, mhi, mlo, free=False)
            with repeat(pe, KX // 2 - 2, {}) as i:
                for b in range(2):
                    step(S_PG + 4 + b, mhi, mlo, i, free=S_PE + 3 + b)


def columns():
    sizes = (EA, EA, EA, HB * DK, HB * DK, EB, EB, RANK, D, D)
    u, va, za, q, k, vb, zb, lr, ma, mb = np.cumsum((0,) + sizes[:-1]).tolist()
    blocks = ((k, HB), (q, HB), (vb, KE), (zb, KE), (va, KE), (za, KE), (u, KE))
    order = [s + P * i for s, n in blocks for i in range(n)]
    return order, lr, ma, mb


def constants():
    c = np.zeros((P, C_CONSTS), np.float32)
    c[:, C_ID:C_ID + P] = np.eye(P)
    c[:, C_ONE:C_ONE + P] = 1
    s, t = np.mgrid[0:P, 0:P]
    c[:, C_ATT:C_ATT + P] = (s // BLK == t // BLK) & (t >= s)
    s, t = np.mgrid[0:DEC, 0:DEC]
    c[:DEC, C_ATS:C_ATS + DEC] = (s // DEC_L == t // DEC_L) & (t >= s)
    rows = np.arange(P)
    c[rows, C_SEL + rows // QR * DEC_L + rows % DEC_L] = 1
    c[:, C_RESET:C_RESET + T] = 1
    c[:, C_RESET:C_RESET + SEQ:BLK] = 0
    c[:, C_RESET + SEQ:C_RESET + T:DEC_L] = 0
    return c


def kernel(**inputs):
    import concourse.bacc as _bacc
    from concourse.bass_utils import run_bass_kernel_spmd as _run

    a = {n: np.asarray(v) for n, v in inputs.items()}
    f32 = np.float32

    def tokens_last(prompt, sample):
        x = np.concatenate([prompt.reshape(SEQ, -1), sample.reshape(DEC, -1)])
        return np.ascontiguousarray(x.reshape(T, -1, P).transpose(2, 1, 0))

    order, lr, ma, mb = columns()
    w_in, w_pa, w_pb, w_o, w_pg, w_pe = (a[n][0] for n in ("w_in", "w_pa", "w_pb", "w_o", "w_pg", "w_pe"))
    units = np.empty((UNITS, P, UK, P), f32)
    at = [0]

    def add(w, c):
        for k in range(0, w.shape[0], UK * P):
            units[at[0]] = w[k:k + UK * P, c:c + P].reshape(UK, P, P).transpose(1, 0, 2)
            at[0] += 1

    for c in order:
        add(w_in, c)
    for j in range(KX):
        add(w_in, ma + P * j)
        add(w_in, mb + P * j)
        add(w_pa, P * j)
        add(w_pb, P * j)
    for j in range(KX):
        add(w_o, P * j)
    for j in range(0, KX, 4):
        units[at[0]] = w_pe[:, P * j:P * (j + 4)].reshape(2, P, 4, P).transpose(1, 2, 0, 3).reshape(P, UK, P)
        at[0] += 1
    for j in range(KX):
        add(w_pg, P * j)
    assert at[0] == UNITS
    for s in (S_K, S_PG):
        units[2 * s + 1:2 * s + 3] = units[[2 * s + 2, 2 * s + 1]]

    params = np.concatenate([a[n][0].reshape(-1, P).T for n in ("g_pre", "g_v", "g_o", "b_a", "g_post")], axis=1)
    w_s = a["w_s"][0]
    w_s_dec = np.zeros((DEC, HA, DEC), f32)
    for b in range(DEC_B):
        r = slice(DEC_L * b, DEC_L * (b + 1))
        w_s_dec[r, :, r] = w_s[:, :DEC_L, :DEC_L].transpose(2, 0, 1)
    arrays = {
        "x_t": tokens_last(a["x_prompt"], a["x_sample"]),
        "p_t": tokens_last(a["p_prompt"][0], a["p_sample"][0]),
        "w_units": units,
        "w_alr": np.ascontiguousarray(w_in[:, lr:lr + RANK].reshape(KX, P, RANK).transpose(1, 0, 2)),
        "params": np.ascontiguousarray(params),
        "consts": constants(),
        "w_s_t": np.ascontiguousarray(w_s.transpose(2, 0, 1)),
        "w_s_dec": w_s_dec,
        "b_s_rows": np.ascontiguousarray(np.broadcast_to(a["b_s"][0][None], (P, HA, CHUNK))),
        "w_a2": np.ascontiguousarray(a["w_a2"][0]),
        "s0": np.ascontiguousarray(a["state_gla"][0]),
    }
    outs = {"y": (P, KX, T), "st_prompt": (HB, DK, DV), "st_dec": (DEC_B, HB, DK, DV), "cv": (KE, P, DEC)}

    nc = _bacc.Bacc("TRN2", target_bir_lowering=False, num_devices=1)
    A = {n: nc.dram_tensor(f"in_{n}", v.shape, F32, kind="ExternalInput").ap() for n, v in arrays.items()}
    O = {n: nc.dram_tensor(f"out_{n}", s, F32, kind="ExternalOutput").ap() for n, s in outs.items()}
    build(nc, A, O)
    got = _run(nc, [{f"in_{n}": v for n, v in arrays.items()}], core_ids=[0]).results[0]
    y = got["out_y"].transpose(2, 1, 0).reshape(T, D)
    return (
        y[:SEQ].reshape(1, SEQ, D),
        y[SEQ:].reshape(DEC_B, DEC_L, D),
        got["out_st_prompt"][None, None],
        got["out_st_dec"][None],
        got["out_cv"].transpose(2, 0, 1).reshape(1, DEC_B, DEC_L, EA),
    )
```
